# Optimizing a Trainium2 kernel written in Bass

```python
import math
import jax, jax.numpy as jnp
from jax import lax
import numpy as np

D_MODEL = 1024
BATCH = 1
SEQ = 512
DEPTH = 1

N_Q_HEADS = 8
N_KV_HEADS = 2
HEAD_DIM = 64
Q_GROUP = N_Q_HEADS // N_KV_HEADS
ATTN_WIDTH = N_Q_HEADS * HEAD_DIM
KV_WIDTH = N_KV_HEADS * HEAD_DIM
WINDOW = 128
BLOCK = 128
N_BUCKETS = 32
MAX_DISTANCE = 128
NEG_INF = -1e30
SSM_WIDTH = D_MODEL // 2
SSM_GROUP = 16
SSM_GROUPS = SSM_WIDTH // SSM_GROUP
SSM_STATE = 64
DT_MIN = 1e-3
DT_MAX = 1e-1
N_BRANCHES = 2
D_FF = 4 * D_MODEL
IN_WIDTH = ATTN_WIDTH + 2 * KV_WIDTH + SSM_WIDTH + N_BRANCHES * D_MODEL
SPLITS = (ATTN_WIDTH, ATTN_WIDTH + KV_WIDTH, ATTN_WIDTH + 2 * KV_WIDTH,
          ATTN_WIDTH + 2 * KV_WIDTH + SSM_WIDTH, ATTN_WIDTH + 2 * KV_WIDTH + SSM_WIDTH + D_MODEL)
RMS_EPS = 1e-6


def rmsnorm(x, g):
    xf = x.astype(jnp.float32)
    y = xf * lax.rsqrt(jnp.mean(xf * xf, axis=-1, keepdims=True) + RMS_EPS)
    return (y * g.astype(jnp.float32)).astype(x.dtype)

def t5_causal_bucket(dist):
    max_exact = N_BUCKETS // 2
    d = jnp.maximum(dist, 0)
    df = jnp.maximum(d, 1).astype(jnp.float32)
    large = max_exact + (jnp.log(df / max_exact) / math.log(MAX_DISTANCE / max_exact)
                         * (N_BUCKETS - max_exact)).astype(jnp.int32)
    large = jnp.minimum(large, N_BUCKETS - 1)
    return jnp.where(d < max_exact, d, large)

def sliding_window_attention(q, k, v, sinks, rel_bias):
    B, L = q.shape[0], q.shape[1]
    nb = L // BLOCK
    qb = q.reshape(B, nb, BLOCK, N_KV_HEADS, Q_GROUP, HEAD_DIM)

    def band(t):
        tb = t.reshape(B, nb, BLOCK, N_KV_HEADS, HEAD_DIM)
        prev = jnp.pad(tb, ((0, 0), (1, 0), (0, 0), (0, 0), (0, 0)))[:, :-1]
        return jnp.concatenate([prev, tb], axis=2)

    kb, vb = band(k), band(v)
    logits = jnp.einsum('bnqkgd,bnskd->bnkgqs', qb, kb,
                        preferred_element_type=jnp.float32) * (HEAD_DIM ** -0.5)
    qi = jnp.arange(BLOCK)[:, None]
    kj = jnp.arange(2 * BLOCK)[None, :]
    dist = qi + BLOCK - kj
    band_ok = (dist >= 0) & (dist < WINDOW)
    key_pos = jnp.arange(nb)[:, None] * BLOCK - BLOCK + jnp.arange(2 * BLOCK)[None, :]
    mask = band_ok[None] & (key_pos >= 0)[:, None, :]
    bias = rel_bias.astype(jnp.float32)[t5_causal_bucket(dist)]
    bias = jnp.transpose(bias, (2, 0, 1)).reshape(N_KV_HEADS, Q_GROUP, BLOCK, 2 * BLOCK)
    logits = jnp.where(mask[None, :, None, None], logits + bias[None, None], NEG_INF)
    s = sinks.astype(jnp.float32).reshape(1, 1, N_KV_HEADS, Q_GROUP, 1, 1)
    m = jnp.maximum(jnp.max(logits, axis=-1, keepdims=True), s)
    p = jnp.exp(logits - m)
    denom = jnp.sum(p, axis=-1, keepdims=True) + jnp.exp(s - m)
    probs = (p / denom).astype(v.dtype)
    out = jnp.einsum('bnkgqs,bnskd->bnqkgd', probs, vb)
    return out.reshape(B, L, ATTN_WIDTH)

def s5_ssm(u, lam_re, lam_im, log_dt, b_re, b_im, c_re, c_im, d_skip):
    B, L = u.shape[0], u.shape[1]
    uf = u.astype(jnp.float32).reshape(B, L, SSM_GROUPS, SSM_GROUP)
    dt = jnp.exp(log_dt.astype(jnp.float32))[:, None]
    lr = lam_re.astype(jnp.float32)
    li = lam_im.astype(jnp.float32)
    mag = jnp.exp(lr * dt)
    ab_re = mag * jnp.cos(li * dt)
    ab_im = mag * jnp.sin(li * dt)
    nr = ab_re - 1.0
    den = lr * lr + li * li
    f_re = (nr * lr + ab_im * li) / den
    f_im = (ab_im * lr - nr * li) / den
    br = b_re.astype(jnp.float32)
    bi = b_im.astype(jnp.float32)
    bb_re = f_re[..., None] * br - f_im[..., None] * bi
    bb_im = f_re[..., None] * bi + f_im[..., None] * br
    bu_re = jnp.einsum('blgc,gpc->blgp', uf, bb_re)
    bu_im = jnp.einsum('blgc,gpc->blgp', uf, bb_im)
    a_re = jnp.broadcast_to(ab_re, bu_re.shape)
    a_im = jnp.broadcast_to(ab_im, bu_im.shape)

    def combine(e1, e2):
        a1r, a1i, b1r, b1i = e1
        a2r, a2i, b2r, b2i = e2
        return (a2r * a1r - a2i * a1i,
                a2r * a1i + a2i * a1r,
                a2r * b1r - a2i * b1i + b2r,
                a2r * b1i + a2i * b1r + b2i)

    _, _, h_re, h_im = lax.associative_scan(combine, (a_re, a_im, bu_re, bu_im), axis=1)
    y = (jnp.einsum('blgp,gcp->blgc', h_re, c_re.astype(jnp.float32))
         - jnp.einsum('blgp,gcp->blgc', h_im, c_im.astype(jnp.float32)))
    y = y + d_skip.astype(jnp.float32).reshape(SSM_GROUPS, SSM_GROUP) * uf
    return y.reshape(B, L, SSM_WIDTH).astype(u.dtype)

def first_inputs(seed: int = 0) -> dict:
    key = jax.random.key(seed)
    ks = jax.random.split(key, 24)
    f32 = jnp.float32
    nrm = lambda k, shape, scale: jax.random.normal(k, shape, f32) * scale
    n_idx = jnp.arange(SSM_STATE, dtype=f32)
    return {
        "x": jax.random.normal(ks[0], (BATCH, SEQ, D_MODEL), f32),
        "norm_mix_pre": 1.0 + nrm(ks[1], (DEPTH, D_MODEL), 0.05),
        "norm_mix_post": 1.0 + nrm(ks[2], (DEPTH, D_MODEL), 0.05),
        "norm_mlp_pre": 1.0 + nrm(ks[3], (DEPTH, D_MODEL), 0.05),
        "norm_mlp_post": 1.0 + nrm(ks[4], (DEPTH, D_MODEL), 0.05),
        "w_in": nrm(ks[5], (DEPTH, D_MODEL, IN_WIDTH), D_MODEL ** -0.5),
        "rel_bias": nrm(ks[6], (N_BUCKETS, N_Q_HEADS), 0.5),
        "sinks": nrm(ks[7], (DEPTH, N_Q_HEADS), 0.5),
        "lam_re": -0.5 + nrm(ks[8], (DEPTH, SSM_GROUPS, SSM_STATE), 0.02),
        "lam_im": math.pi * n_idx + nrm(ks[9], (DEPTH, SSM_GROUPS, SSM_STATE), 0.02),
        "log_dt": jax.random.uniform(ks[10], (DEPTH, SSM_GROUPS), f32,
                                     math.log(DT_MIN), math.log(DT_MAX)),
        "b_re": nrm(ks[11], (DEPTH, SSM_GROUPS, SSM_STATE, SSM_GROUP), SSM_GROUP ** -0.5),
        "b_im": nrm(ks[12], (DEPTH, SSM_GROUPS, SSM_STATE, SSM_GROUP), SSM_GROUP ** -0.5),
        "c_re": nrm(ks[13], (DEPTH, SSM_GROUPS, SSM_GROUP, SSM_STATE), SSM_STATE ** -0.5),
        "c_im": nrm(ks[14], (DEPTH, SSM_GROUPS, SSM_GROUP, SSM_STATE), SSM_STATE ** -0.5),
        "d_skip": nrm(ks[15], (DEPTH, SSM_WIDTH), 1.0),
        "w_glu": nrm(ks[16], (DEPTH, SSM_WIDTH, SSM_WIDTH), SSM_WIDTH ** -0.5),
        "w_attn_branch": nrm(ks[17], (DEPTH, ATTN_WIDTH, D_MODEL), ATTN_WIDTH ** -0.5),
        "w_ssm_branch": nrm(ks[18], (DEPTH, SSM_WIDTH, D_MODEL), SSM_WIDTH ** -0.5),
        "w_out": nrm(ks[19], (DEPTH, D_MODEL, D_MODEL), D_MODEL ** -0.5),
        "w_ff_in": nrm(ks[20], (DEPTH, D_MODEL, D_FF), D_MODEL ** -0.5),
        "w_ff_out": nrm(ks[21], (DEPTH, D_FF, D_MODEL), D_FF ** -0.5),
    }

def first_block(x, norm_mix_pre, norm_mix_post, norm_mlp_pre, norm_mlp_post, w_in, rel_bias,
              sinks, lam_re, lam_im, log_dt, b_re, b_im, c_re, c_im, d_skip, w_glu,
              w_attn_branch, w_ssm_branch, w_out, w_ff_in, w_ff_out):
    B, L = x.shape[0], x.shape[1]
    for l in range(DEPTH):
        h = rmsnorm(x, norm_mix_pre[l])
        proj = h @ w_in[l]
        q, k, v, u, g_attn, g_ssm = jnp.split(proj, SPLITS, axis=-1)
        q = q.reshape(B, L, N_Q_HEADS, HEAD_DIM)
        k = k.reshape(B, L, N_KV_HEADS, HEAD_DIM)
        v = v.reshape(B, L, N_KV_HEADS, HEAD_DIM)
        y_attn = sliding_window_attention(q, k, v, sinks[l], rel_bias) @ w_attn_branch[l]
        z = jax.nn.gelu(s5_ssm(u, lam_re[l], lam_im[l], log_dt[l], b_re[l], b_im[l],
                               c_re[l], c_im[l], d_skip[l]))
        z = z * jax.nn.sigmoid(z @ w_glu[l])
        y_ssm = z @ w_ssm_branch[l]
        merged = jax.nn.sigmoid(g_attn) * y_attn + jax.nn.sigmoid(g_ssm) * y_ssm
        x = x + rmsnorm(merged @ w_out[l], norm_mix_post[l])
        h = rmsnorm(x, norm_mlp_pre[l])
        f = jnp.square(jax.nn.relu(h @ w_ff_in[l])) @ w_ff_out[l]
        x = x + rmsnorm(f, norm_mlp_post[l])
    return x


LRU_WIDTH = D_MODEL
LRU_HEADS = 16
LRU_BLOCK = LRU_WIDTH // LRU_HEADS
CONV_WIDTH = 4
CONV_LEFT = 2
RGLRU_C = 8.0
N_DIR = 2
N_HEADS = 16
N_KV_HEADS_2 = 4
GROUP = N_HEADS // N_KV_HEADS_2
D_FF_2 = ((8 * D_MODEL // 3 + 255) // 256) * 256
N_BRANCH = 2
Q_W = N_HEADS * HEAD_DIM
KV_W = N_KV_HEADS_2 * HEAD_DIM
IN_W = 2 * LRU_WIDTH + Q_W + 2 * KV_W + N_BRANCH * D_MODEL
EPS = 1e-6
NEG_INF_2 = -1e30


def rmsnorm_2(x, g):
    xf = x.astype(jnp.float32)
    y = xf * lax.rsqrt(jnp.mean(xf * xf, axis=-1, keepdims=True) + EPS)
    return (y * g.astype(jnp.float32)).astype(x.dtype)

def centred_depthwise_conv(u, w, b):
    s = u.shape[1]
    up = jnp.pad(u, ((0, 0), (CONV_LEFT, CONV_WIDTH - 1 - CONV_LEFT), (0, 0)))
    out = up[:, 0:s] * w[0]
    for k in range(1, CONV_WIDTH):
        out = out + up[:, k:k + s] * w[k]
    return out + b

def _linear_combine(left, right):
    a1, b1 = left
    a2, b2 = right
    return a1 * a2, a2 * b1 + b2

def rg_lru(u, lam, wa, ba, wx, bx, reverse):
    bsz, s, c = u.shape
    ub = u.reshape(bsz, s, LRU_HEADS, LRU_BLOCK)
    r = jax.nn.sigmoid(jnp.einsum("bshi,hij->bshj", ub, wa.astype(jnp.float32)).reshape(bsz, s, c) + ba.astype(jnp.float32))
    i = jax.nn.sigmoid(jnp.einsum("bshi,hij->bshj", ub, wx.astype(jnp.float32)).reshape(bsz, s, c) + bx.astype(jnp.float32))
    log_a = -RGLRU_C * r * jax.nn.softplus(-lam.astype(jnp.float32))
    a = jnp.exp(log_a)
    beta = jnp.sqrt(jnp.maximum(-jnp.expm1(2.0 * log_a), 0.0))
    _, h = lax.associative_scan(_linear_combine, (a, beta * (i * u)), axis=1, reverse=reverse)
    return h

def banded_alibi_sink_attention(q, k, v, sink):
    bsz, s = q.shape[0], q.shape[1]
    nb = s // BLOCK
    qb = (q.astype(jnp.float32) * (HEAD_DIM ** -0.5)).reshape(bsz, nb, BLOCK, N_KV_HEADS_2, GROUP, HEAD_DIM)

    def key_blocks(t):
        tp = jnp.pad(t.astype(jnp.float32), ((0, 0), (BLOCK, BLOCK), (0, 0), (0, 0)))
        tp = tp.reshape(bsz, nb + 2, BLOCK, N_KV_HEADS_2, HEAD_DIM)
        return jnp.concatenate([tp[:, j:j + nb] for j in range(3)], axis=2)

    kb = key_blocks(k)
    vb = key_blocks(v)
    scores = jnp.einsum("bnqkgd,bnskd->bnkgqs", qb, kb)

    q_loc = jnp.arange(BLOCK)
    k_loc = jnp.arange(3 * BLOCK)
    dist = q_loc[:, None] + BLOCK - k_loc[None, :]
    kpos = jnp.arange(nb)[:, None] * BLOCK - BLOCK + k_loc[None, :]
    valid = (jnp.abs(dist) <= WINDOW)[None] & ((kpos >= 0) & (kpos < s))[:, None, :]

    slopes = jnp.exp2(-8.0 * (jnp.arange(N_HEADS, dtype=jnp.float32) + 1.0) / N_HEADS)
    alibi = -slopes.reshape(N_KV_HEADS_2, GROUP, 1, 1) * jnp.abs(dist).astype(jnp.float32)
    scores = jnp.where(valid[None, :, None, None], scores + alibi, NEG_INF_2)

    sink_l = sink.astype(jnp.float32).reshape(1, 1, N_KV_HEADS_2, GROUP, 1, 1)
    m = jnp.maximum(jnp.max(scores, axis=-1, keepdims=True), sink_l)
    p = jnp.exp(scores - m)
    denom = jnp.sum(p, axis=-1, keepdims=True) + jnp.exp(sink_l - m)
    o = jnp.einsum("bnkgqs,bnskd->bnqkgd", p / denom, vb)
    return o.reshape(bsz, s, Q_W)

def second_inputs(seed: int = 0) -> dict:
    key = jax.random.key(seed)
    ks = jax.random.split(key, 20)
    f32 = jnp.float32
    x = jax.random.normal(ks[0], (BATCH, SEQ, D_MODEL), f32)
    norm_mix_g = 1.0 + 0.05 * jax.random.normal(ks[1], (DEPTH, D_MODEL), f32)
    w_in = jax.random.normal(ks[2], (DEPTH, D_MODEL, IN_W), f32) * D_MODEL ** -0.5
    b_gate = 0.01 * jax.random.normal(ks[3], (DEPTH, N_BRANCH * D_MODEL), f32)
    conv_w = jax.random.normal(ks[4], (DEPTH, CONV_WIDTH, LRU_WIDTH), f32) * CONV_WIDTH ** -0.5
    conv_b = 0.01 * jax.random.normal(ks[5], (DEPTH, LRU_WIDTH), f32)
    u = jax.random.uniform(ks[6], (DEPTH, N_DIR, LRU_WIDTH), f32, minval=0.9, maxval=0.999)
    p = u ** (1.0 / RGLRU_C)
    lru_lambda = jnp.log(p) - jnp.log1p(-p)
    lru_wa = jax.random.normal(ks[7], (DEPTH, N_DIR, LRU_HEADS, LRU_BLOCK, LRU_BLOCK), f32) * LRU_BLOCK ** -0.5
    lru_ba = 0.01 * jax.random.normal(ks[8], (DEPTH, N_DIR, LRU_WIDTH), f32)
    lru_wx = jax.random.normal(ks[9], (DEPTH, N_DIR, LRU_HEADS, LRU_BLOCK, LRU_BLOCK), f32) * LRU_BLOCK ** -0.5
    lru_bx = 0.01 * jax.random.normal(ks[10], (DEPTH, N_DIR, LRU_WIDTH), f32)
    attn_sink = 0.5 * jax.random.normal(ks[11], (DEPTH, N_HEADS), f32)
    w_out = jax.random.normal(ks[12], (DEPTH, D_MODEL, D_MODEL), f32) * D_MODEL ** -0.5
    norm_ffn_g = 1.0 + 0.05 * jax.random.normal(ks[13], (DEPTH, D_MODEL), f32)
    w_ffn_in = jax.random.normal(ks[14], (DEPTH, D_MODEL, 2 * D_FF_2), f32) * D_MODEL ** -0.5
    w_ffn_out = jax.random.normal(ks[15], (DEPTH, D_FF_2, D_MODEL), f32) * D_FF_2 ** -0.5
    norm_final_g = 1.0 + 0.05 * jax.random.normal(ks[16], (D_MODEL,), f32)
    return {"x": x, "norm_mix_g": norm_mix_g, "w_in": w_in, "b_gate": b_gate,
            "conv_w": conv_w, "conv_b": conv_b, "lru_lambda": lru_lambda,
            "lru_wa": lru_wa, "lru_ba": lru_ba, "lru_wx": lru_wx, "lru_bx": lru_bx,
            "attn_sink": attn_sink, "w_out": w_out, "norm_ffn_g": norm_ffn_g,
            "w_ffn_in": w_ffn_in, "w_ffn_out": w_ffn_out, "norm_final_g": norm_final_g}

def second_block(x, norm_mix_g, w_in, b_gate, conv_w, conv_b, lru_lambda, lru_wa, lru_ba,
              lru_wx, lru_bx, attn_sink, w_out, norm_ffn_g, w_ffn_in, w_ffn_out, norm_final_g):
    bsz, s, _ = x.shape
    splits = [LRU_WIDTH, 2 * LRU_WIDTH, 2 * LRU_WIDTH + Q_W, 2 * LRU_WIDTH + Q_W + KV_W,
              2 * LRU_WIDTH + Q_W + 2 * KV_W]
    for l in range(DEPTH):
        xn = rmsnorm_2(x, norm_mix_g[l])
        proj = xn @ w_in[l]
        u, g_lru, q, k, v, z = jnp.split(proj, splits, axis=-1)

        uc = centred_depthwise_conv(u, conv_w[l], conv_b[l]).astype(jnp.float32)
        h_fwd = rg_lru(uc, lru_lambda[l, 0], lru_wa[l, 0], lru_ba[l, 0], lru_wx[l, 0], lru_bx[l, 0], False)
        h_bwd = rg_lru(uc, lru_lambda[l, 1], lru_wa[l, 1], lru_ba[l, 1], lru_wx[l, 1], lru_bx[l, 1], True)
        y_a = ((h_fwd + h_bwd) * jax.nn.gelu(g_lru.astype(jnp.float32))).astype(x.dtype)

        y_b = banded_alibi_sink_attention(
            q.reshape(bsz, s, N_HEADS, HEAD_DIM),
            k.reshape(bsz, s, N_KV_HEADS_2, HEAD_DIM),
            v.reshape(bsz, s, N_KV_HEADS_2, HEAD_DIM),
            attn_sink[l]).astype(x.dtype)

        gates = jax.nn.sigmoid(z + b_gate[l]).reshape(bsz, s, N_BRANCH, D_MODEL)
        merged = gates[:, :, 0] * y_a + gates[:, :, 1] * y_b
        x = x + merged @ w_out[l]

        xn2 = rmsnorm_2(x, norm_ffn_g[l])
        gu = xn2 @ w_ffn_in[l]
        ff_gate, ff_up = jnp.split(gu, [D_FF_2], axis=-1)
        x = x + (jax.nn.silu(ff_gate) * ff_up) @ w_ffn_out[l]
    return rmsnorm_2(x, norm_final_g)


def setup_inputs(seed=0):
    out = dict(first_inputs(seed))
    for name, value in second_inputs(seed + 1).items():
        if name != "x":
            out[name + "_2"] = value
    return out


def reference(
    x, norm_mix_pre, norm_mix_post, norm_mlp_pre, norm_mlp_post, w_in, rel_bias, sinks, lam_re,
    lam_im, log_dt, b_re, b_im, c_re, c_im, d_skip, w_glu, w_attn_branch, w_ssm_branch, w_out,
    w_ff_in, w_ff_out, norm_mix_g_2, w_in_2, b_gate_2, conv_w_2, conv_b_2, lru_lambda_2,
    lru_wa_2, lru_ba_2, lru_wx_2, lru_bx_2, attn_sink_2, w_out_2, norm_ffn_g_2, w_ffn_in_2,
    w_ffn_out_2, norm_final_g_2,
):
    x = first_block(
        x, norm_mix_pre, norm_mix_post, norm_mlp_pre, norm_mlp_post, w_in, rel_bias, sinks,
        lam_re, lam_im, log_dt, b_re, b_im, c_re, c_im, d_skip, w_glu, w_attn_branch,
        w_ssm_branch, w_out, w_ff_in, w_ff_out,
    )
    return second_block(
        x, norm_mix_g_2, w_in_2, b_gate_2, conv_w_2, conv_b_2, lru_lambda_2, lru_wa_2, lru_ba_2,
        lru_wx_2, lru_bx_2, attn_sink_2, w_out_2, norm_ffn_g_2, w_ffn_in_2, w_ffn_out_2,
        norm_final_g_2,
    )


_drawn_inputs = setup_inputs


def setup_inputs(seed=0):
    import zlib

    import numpy as np

    out = dict(_drawn_inputs(seed))
    spreads = {}
    factors = {'sinks': 8.0,
     'lam_re': 8.0,
     'b_gate_2': 8.0,
     'conv_b_2': 3.65,
     'lru_ba_2': 8.0,
     'lru_bx_2': 8.0,
     'attn_sink_2': 8.0,
     'norm_ffn_g_2': 2.791}
    for name, (base, spread) in spreads.items():
        noise = np.random.default_rng([zlib.crc32(name.encode()), seed]).standard_normal(out[name].shape)
        drawn = base * np.exp(spread * noise) if base else spread * noise
        out[name] = __import__('jax').numpy.asarray(drawn.astype(out[name].dtype))
    for name, factor in factors.items():
        out[name] = (out[name] * factor).astype(out[name].dtype)
    return out
```

```python
from contextlib import ExitStack

import numpy as np

import concourse.bass as bass
from concourse import mybir

F32 = mybir.dt.float32
F32R = mybir.dt.float32r
ALU = mybir.AluOpType
ACT = mybir.ActivationFunctionType
AX = mybir.AxisListType

P = 128
D = 1024
T = 512
DC = D // P
HD = 64
EPS = 1e-6

NBUCKET, MAXDIST = 32, 128
SSM_CH = 512
CT = SSM_CH // P
PAIRS = 16
STEP = 4
NB = T // STEP
E0 = 16
E1 = NB // E0
FF1_PARTS = 4
FF1_PART = 8
FF2_CHUNKS = [8, 8, 6]

TILES = 8
RAW = 2
RING = 4
AHEAD = 2

HEADS1 = [par * 4 + h for h in range(4) for par in range(2)]
HEADS2 = [(2 * pp + par) * 4 + h for pp in range(2) for h in range(4) for par in range(2)]

_counts = [("u", 4), ("k", 1), ("v", 1), ("gate_a", 8), ("q", 4), ("branch_a", 4), ("gate_s", 8),
           ("glu", 2), ("branch_s", 4), ("out", 8), ("ff", 16 * FF1_PARTS),
           ("q2", 8), ("k2", 2), ("v2", 2), ("u2", 8), ("lru", 4), ("g2", 8), ("za", 8), ("zb", 8),
           ("out2", 8), ("ff2", sum(2 * c + 8 for c in FF2_CHUNKS))]
SLAB, _n = {}, 0
for _name, _c in _counts:
    SLAB[_name] = _n
    _n += _c
NSLAB = _n
COUNT = dict(_counts)
assert NSLAB % RING == 0

_outs = [("u", 4), ("k", 1), ("v", 1), ("gate_a", 8), ("q", 4), ("branch_a", 8), ("gate_s", 8), ("glu", 4),
         ("branch_s", 8), ("out", 8), ("ff", 16 * FF1_PARTS), ("q2", 8), ("k2", 2), ("v2", 2), ("u2", 8),
         ("g2", 8), ("za", 8), ("zb", 8), ("out2", 8), ("ff2", sum(2 * c + 8 for c in FF2_CHUNKS))]
OUT, _n = {}, 0
for _name, _c in _outs:
    OUT[_name] = _n
    _n += _c

_cols = [("g_mix_pre", 8), ("g_mix_post", 8), ("g_mlp_pre", 8), ("g_mlp_post", 8), ("sinks", 8), ("d_skip", 4),
         ("g_mix2", 8), ("b_gate", 16), ("conv_w", 32), ("conv_b", 8), ("lam", 16), ("ba", 16), ("bx", 16),
         ("sinks2", 16), ("g_ffn2", 8), ("g_fin2", 8), ("iota", 16), ("eps", 1), ("pad", 3),
         ("ident", P), ("ones", P)]
COL, _n = {}, 0
for _name, _c in _cols:
    COL[_name] = _n
    _n += _c
NCOL = _n
SW = PAIRS + CT * P

MAGIC = 1.5 * 2.0 ** 23
TWO_PI = 2.0 * np.pi
C1 = 6.28125
C2 = float(np.float32(np.round((TWO_PI - C1) * 2.0 ** 20) / 2.0 ** 20))
C3 = float(np.float32(TWO_PI - C1 - C2))
TURN = 6.283185


def build(nc, slabs, params, s5p, s5bt, s5b, s5c, bias1, nd2, x_in, out):
    ctx = ExitStack()
    with ctx:
        def sb(name, shape, dt=F32):
            return ctx.enter_context(nc.sbuf_tensor(name, shape, dt))

        def sem(name):
            return ctx.enter_context(nc.semaphore(name))

        raw = sb("raw", [P, RAW, TILES * P])
        w_hi = sb("w_hi", [P, RING, TILES * P], F32R)
        w_lo = sb("w_lo", [P, RING, TILES * P], F32R)
        a_hi = sb("a_hi", [P, DC, T], F32R)
        a_lo = sb("a_lo", [P, DC, T], F32R)
        h_hi = sb("h_hi", [P, DC, T], F32R)
        h_lo = sb("h_lo", [P, DC, T], F32R)
        par = sb("par", [P, NCOL])
        R = sb("R", [P, T])
        AR = 25600
        arena = sb("arena", [P, AR])

        def region(at, *shape):
            n = int(np.prod(shape))
            assert at + n <= AR, (at, shape)
            v = arena[:, at:at + n]
            if len(shape) == 2:
                v = v.rearrange("p (a b) -> p a b", a=shape[0])
            if len(shape) == 3:
                v = v.rearrange("p (a b c) -> p a b c", a=shape[0], b=shape[1])
            if len(shape) == 4:
                v = v.rearrange("p (a b c d) -> p a b c d", a=shape[0], b=shape[1], c=shape[2])
            return v

        def col(name, i=0, n=1):
            return par[:, COL[name] + i:COL[name] + i + n]

        ident = col("ident", 0, P)
        ones = col("ones", 0, P)

        X = region(0, DC, T)
        tab_c, tab_s = region(0, 4, NB), region(512, 4, NB)
        t1, t2 = region(1024, 4, NB), region(1536, 4, NB)
        g_re, g_im = region(2048, 4, NB), region(2560, 4, NB)
        st_re, st_im = region(3072, 4, NB), region(3584, 4, NB)
        win = region(4096, CT, STEP, 2, P)
        ca_re, ca_im = region(8192, STEP + 1, PAIRS, 32), region(10752, STEP + 1, PAIRS, 32)
        b_re, b_im = region(13312, PAIRS, 32), region(13824, PAIRS, 32)
        kloc = region(14336, CT, STEP, P)
        e0c, e0s = region(16384, PAIRS, E0), region(16640, PAIRS, E0)
        e1c, e1s = region(16896, PAIRS, E1), region(17024, PAIRS, E1)
        U = region(17152, CT, T)
        KV = region(19200, 2, T)
        gate1 = region(20224, DC, T)
        rho = region(24320, PAIRS)
        rot = region(24368, 4, PAIRS)
        zp = region(25088, T)
        d_are, d_aim, d_fre, d_fim = (region(20224 + SW * i, SW) for i in range(4))
        bt_re, bt_im = region(20224 + 4 * SW, CT, P), region(20736 + 4 * SW, CT, P)
        w_t1, w_t2 = region(21248 + 4 * SW, CT, P), region(25088, CT, P)
        s_w = [region(14336 + SW * i, SW) for i in range(3)] + [region(8704 + SW * i, SW) for i in range(3)] + \
              [region(11264 + SW * i, SW) for i in range(3)]
        Q = region(4096, 4, T)
        bias8 = region(6144, 8, 2 * P)
        logit1 = [region(8192, 4, 2 * P), region(9216, 4, 2 * P)]
        PT1 = region(10240, 2, T)
        VT1 = region(11264, 1, 4, P)
        mini = [region(24448 + 32 * i, 8, 4) for i in range(2)]
        gate2 = region(4096, DC, T)
        ssum = region(17152, T)
        sq = [region(17664, T), region(18176, T)]
        tmp = [region(24512, T), region(25024, T)]
        fbuf = [region(12288, T), region(12800, T)]
        Y = region(8192, DC, T)
        Fo = region(4096, DC, T)
        UC = region(4096, DC, T)
        Q2 = region(8192, DC, T)
        KV2 = region(12288, 4, T)
        VT2 = region(14336, 2, 4, P)
        G2 = region(15360, DC, T)
        HS = region(19456, DC, T)
        logit2 = [region(15360, 4, 3 * P), region(16896, 4, 3 * P)]
        PT2 = region(18432, 3, T)
        nd8 = region(19968, 3 * P)
        lru = [region(12288 + T * i, T) for i in range(6)]
        lru45 = region(12288 + 4 * T, 2 * T)
        spc = region(23552, 12, 16)
        OUTB = region(4096, DC, T)

        gp = ctx.enter_context(nc.psum_tensor("gp", [P, 2, T], F32))
        mp = ctx.enter_context(nc.psum_tensor("mp", [P, 6, T], F32))

        s_par = sem("params_loaded")
        s_bc = sem("b_and_c_loaded")
        s_x = [sem(f"x_half{c}_loaded") for c in range(2)]
        s_raw = [sem(f"slab_loaded{i}") for i in range(RAW)]
        s_bias = sem("bias_loaded")
        s_x2 = sem("x_loaded_again")
        s_nd = sem("distances_loaded")
        w_hi_ready = sem("w_hi_ready")
        w_lo_ready = sem("w_lo_ready")
        half_done = sem("half_slab_done")
        out_read = sem("output_read")
        vec_step = sem("vec_step")
        act_step = sem("act_step")
        pool_step = sem("pool_step")
        a_hi_ready, a_lo_ready = sem("a_hi_ready"), sem("a_lo_ready")
        h_val, h_hi_ready, h_lo_ready = sem("h_value"), sem("h_hi_ready"), sem("h_lo_ready")
        x_new = sem("x_updated")
        m_val = sem("merged_value")
        sq_done, sq_added = sem("square_done"), sem("square_added")
        rms_sum, rms_root = sem("rms_sum"), sem("rms_root")
        disc_act, disc_vec = sem("discretise_act"), sem("discretise_vec")
        win_ready = sem("win_ready")
        ca_ready = sem("c_powers_ready")
        kloc_done, kloc_ready = sem("kloc_product"), sem("kloc_ready")
        v_done, v_read = sem("state_inputs"), sem("state_inputs_read")
        st_ready, y_done = sem("states_ready"), sem("ssm_output")
        y_val, z_val = sem("ssm_value"), sem("z_value")
        gate_val = sem("gate_value")
        vt_done, vt_ready = sem("v_transposed"), sem("v_ready")
        sc_done, lg_ready = sem("scores_done"), sem("logits_ready")
        nb_ready, ex_done = sem("maximum_ready"), sem("exponentials_done")
        pr_ready, pt_done, pt_ready = sem("probs_ready"), sem("probs_transposed"), sem("probs_t_ready")
        at_done = sem("attention_done")
        glu_sig = sem("glu_sigmoid")
        at_read = sem("attention_read")
        lg_done, lru_sig, lru_act, lru_mid, lru_free = (
            sem("lru_products"), sem("lru_sigmoids"), sem("lru_exp_tanh"), sem("lru_guarded"), sem("lru_free"))
        lru_root = sem("lru_root")
        spc_val, spc_exp, decay_ready = sem("lambda_magnitude"), sem("lambda_exp"), sem("decay_ready")
        s_out = sem("stored")

        block = ctx.enter_context(nc.Block())

        NORM = {"n1": 0, "post1": 1, "n2": 2, "post2": 3, "n3": 4, "n4": 5, "n5": 6}
        A_AT = {"n1": 0, "merged": 8, "n2": 16, "n3": 24, "n4": 32}
        H_AT = {"z": 0, "y1": 4, "z2": 12, "ff": 16, "uc": 48, "m2": 56, "ff2": 64}
        V_AT = {"ff": 0, "uc": 32, "m2": 40, "ff2": 48}
        X_AT = {"post1": 0, "post2": 8, "ff2": 16}
        G_AT = {"gate_a": 0, "gate_s": 8, "g2": 16, "za": 24, "zb": 32, "ff2": 40}
        PART1 = 2 * FF1_PART + DC - FF1_PART
        PART2 = 2 * FF2_CHUNKS[0] + DC

        class Attention:

            def __init__(self, first, chunk0, pairs, back, forth, q, kt, k0, v0, vt, logit, pt, sinks, name):
                self.units = [(b, pp, p) for b in range(T // P) for pp in range(pairs) for p in range(2)]
                self.u0, self.q, self.kt, self.k0, self.v0, self.vt = first, q, kt, k0, v0, vt
                self.logit, self.pt, self.sinks, self.name, self.pairs = logit, pt, sinks, name, pairs
                self.chunks, self.done = [], []
                g = chunk0
                for b, _, _ in self.units:
                    js = [(j, b - back + j) for j in range(back + forth + 1) if 0 <= b - back + j < T // P]
                    self.chunks.append([(g + n, j, kb) for n, (j, kb) in enumerate(js)])
                    g += len(js)
                    self.done.append(g)
                self.width = (back + forth + 1) * P

            def span(self, u):
                return self.chunks[u][0][1] * P, (self.chunks[u][-1][1] + 1) * P

            def scores(self):
                return mp[:, 0:3, :].rearrange("p a b -> p (a b)")[:, 0:4 * self.width].rearrange(
                    "p (h k) -> p h k", h=4)

            def out_ap(self, view, u):
                b, pp, p = self.units[u]
                return view[HD * p:HD * p + HD, 4 * pp:4 * pp + 4, b * P:b * P + P]

        att1 = Attention(0, 0, 1, 1, 0, Q, KV, 0, 1, VT1, logit1, PT1, "sinks", "y1")
        att2 = Attention(len(att1.units), att1.done[-1], 2, 1, 1, Q2, KV2, 0, 2, VT2, logit2, PT2, "sinks2", "")

        class Tally:

            def __init__(self, eng, s):
                self.eng, self.s, self.n, self.i, self.per = eng, s, 0, 0, 0

            def up(self, ins):
                ins.then_inc(self.s, 1)
                self.n += 1

            def settle(self):
                self.eng.wait_ge(self.s, self.n + self.i * self.per)

            def run(self, ins):
                self.up(ins)
                self.settle()

        def loop(eng, count, body, tally=None, per=0, unroll=4):
            if count % unroll or count < 2 * unroll:
                for k in range(count):
                    body(0, k)
                return
            start = tally.n if tally else 0
            with eng.Fori(0, count // unroll) as i:
                if tally:
                    tally.i, tally.per = i, per * unroll
                for k in range(unroll):
                    body(i, k)
            if tally:
                assert tally.n - start == per * unroll, (tally.n - start, per)
                tally.n, tally.i, tally.per = start + per * count, 0, 0

        def at(view, e):
            if isinstance(e, int):
                return view[:, e, :]
            return view[:, bass.ds(e, 1), :].rearrange("p a b -> p (a b)")

        def pcol(name, e):
            if isinstance(e, int):
                return col(name, e)
            return par[:, bass.ds(COL[name] + e, 1)]

        @block.sync
        def _(sp):
            sp.dma_start(par[:, :], params).then_inc(s_par, 16)
            for dst, k in ((s_w[0], 0), (s_w[1], 1), (s_w[2], 2)):
                sp.dma_start(dst, s5p[:, k, :]).then_inc(s_par, 16)

            def load(n, k):
                sp.dma_start(raw[:, k % RAW, :], n).then_inc(s_raw[k % RAW], 16)

            sp.dma_start(X[:, 0:4, :], x_in[:, 0:4, :]).then_inc(s_x[0], 16)
            load(slabs[0], 0)
            sp.dma_start(X[:, 4:8, :], x_in[:, 4:8, :]).then_inc(s_x[1], 16)
            load(slabs[1], 1)
            with sp.Fori(0, (NSLAB - RAW) // RAW) as i:
                for k in range(RAW):
                    sp.wait_ge(w_lo_ready, i * RAW + (k + 1))
                    src = slabs[bass.ds(i * RAW + (k + RAW), 1), :, :].rearrange("a p n -> (a p) n")
                    load(src, k)
            for c in range(DC):
                sp.wait_ge(x_new, X_AT["ff2"] + c + 1)
                sp.dma_start(out[:, c, :], OUTB[:, c, :]).then_inc(s_out, 16)
            sp.wait_ge(s_out, 16 * DC)

        @block.gpsimd
        def _(pool):
            G = Tally(pool, pool_step)
            for dst, src in ((b_re, s5b[:, 0]), (b_im, s5b[:, 1]), (ca_re[:, 0], s5c[:, 0]), (ca_im[:, 0], s5c[:, 1]),
                             (bt_re, s5bt[:, 0]), (bt_im, s5bt[:, 1])):
                pool.dma_start(dst, src).then_inc(s_bc, 16)
            pool.wait_ge(s_bc, 96)
            pool.wait_ge(disc_vec, 2)

            def wide(v):
                return v[:, PAIRS:SW].rearrange("p (a b) -> p a b", a=CT)

            def product(o_re, o_im, a_re, a_im, c_re, c_im, last=None):
                G.up(pool.tensor_tensor(w_t1, a_re, c_re, ALU.mult))
                G.run(pool.tensor_tensor(w_t2, a_im, c_im, ALU.mult))
                G.run(pool.tensor_tensor(o_re, w_t1, w_t2, ALU.subtract))
                G.up(pool.tensor_tensor(w_t1, a_re, c_im, ALU.mult))
                G.run(pool.tensor_tensor(w_t2, a_im, c_re, ALU.mult))
                ins = pool.tensor_tensor(o_im, w_t1, w_t2, ALU.add)
                if last:
                    ins.then_inc(last, 1)
                else:
                    G.run(ins)

            def w(s, part):
                return win[:, :, s, part, :]

            product(w(STEP - 1, 0), w(STEP - 1, 1), wide(d_fre), wide(d_fim), bt_re, bt_im)
            for s in range(STEP - 2, -1, -1):
                product(w(s, 0), w(s, 1), wide(d_are), wide(d_aim), w(s + 1, 0), w(s + 1, 1),
                        win_ready if s == 0 else None)
            pool.wait_ge(v_done, CT)
            pool.dma_start(bias8, bias1).then_inc(s_bias, 16)
            pool.wait_ge(y_done, CT)
            pool.dma_start(X, x_in).then_inc(s_x2, 16)
            pool.wait_ge(x_new, DC)
            pool.dma_start(nd8, nd2).then_inc(s_nd, 16)

        @block.scalar
        def _(act):
            S = Tally(act, act_step)

            def split(base, i, k, per=4):
                n = base + k
                if isinstance(i, int) and n >= NSLAB:
                    return
                act.wait_ge(s_raw[n % RAW], 16 * (n // RAW + 1) + 16 // RAW * per * i)
                if n >= RING:
                    act.wait_ge(half_done, 2 * (n - RING + 1) + 2 * per * i)
                nc.scalar.activation(w_hi[:, n % RING, :], raw[:, n % RAW, :], ACT.Copy).then_inc(w_hi_ready, 1)

            def square(kind, c, i, src, static):
                n = 8 * NORM[kind] + c
                if n >= 2:
                    act.wait_ge(sq_added, n - 1 + 4 * i)
                dst = sq[static % 2]
                nc.scalar.activation(dst, src, ACT.Square).then_inc(sq_done, 1)

            def root(kind):
                act.wait_ge(rms_sum, NORM[kind] + 1)
                nc.scalar.activation(R[:, :], mp[:, 5, :], ACT.Sqrt, bias=col("eps"), scale=1.0 / D).then_inc(rms_root, 1)

            def normalised(kind, gain, wait):
                for c in range(DC):
                    wait(c)
                    nc.scalar.activation(a_hi[:, c, :], X[:, c, :], ACT.Copy, scale=col(gain, c)).then_inc(a_hi_ready, 1)
                    square(kind, c, 0, X[:, c, :], c)

            act.wait_ge(s_par, 64)
            nc.scalar.activation(s_w[2], s_w[2], ACT.Exp).then_inc(disc_act, 1)
            split(0, 0, 0)
            act.wait_ge(disc_vec, 1)
            nc.scalar.activation(s_w[6], s_w[3], ACT.Exp).then_inc(disc_act, 1)
            nc.scalar.activation(s_w[7], s_w[4], ACT.Sin).then_inc(disc_act, 1)
            nc.scalar.activation(s_w[8], s_w[4], ACT.Sin, scale=0.5).then_inc(disc_act, 1)
            normalised("n1", "g_mix_pre", lambda c: act.wait_ge(s_x[c // 4], 16))
            split(1, 0, 0)
            root("n1")

            def z_chunk(ct):
                act.wait_ge(y_val, ct + 1)
                nc.scalar.activation(U[:, ct, :], zp, ACT.Gelu_apprx_tanh).then_inc(z_val, 1)
                act.wait_ge(z_val, ct + 1)
                nc.scalar.activation(h_hi[:, 4 + ct, :], U[:, ct, :], ACT.Copy).then_inc(h_hi_ready, 1)

            for n in range(SLAB["u"], SLAB["branch_a"]):
                split(n + AHEAD, 0, 0)
                if SLAB["gate_a"] <= n < SLAB["gate_a"] + 8:
                    m = n - SLAB["gate_a"]
                    act.wait_ge(out_read, OUT["gate_a"] + m + 1)
                    nc.scalar.activation(gate1[:, m, :], gate1[:, m, :], ACT.Sigmoid).then_inc(gate_val, 1)
                if n == 0:
                    act.wait_ge(disc_vec, 3)
                    nc.scalar.activation(e0c, e0s, ACT.Sin, scale=TURN / 2).then_inc(disc_act, 1)
                    nc.scalar.activation(e1c, e1s, ACT.Sin, scale=TURN / 2).then_inc(disc_act, 1)
                    S.up(nc.scalar.activation(e0s, e0s, ACT.Sin, scale=TURN))
                    nc.scalar.activation(e1s, e1s, ACT.Sin, scale=TURN).then_inc(disc_act, 1)
                for ct in range(CT - 1):
                    if n == 3 * ct + 11:
                        z_chunk(ct)
            z_chunk(CT - 1)

            def attention(A):
                for pp in range(A.pairs):
                    act.wait_ge(vt_done, pp + 1 + (A.u0 > 0))
                    nc.scalar.activation(A.vt[:, pp, :, :].rearrange("p a b -> p (a b)"), mp[:, 3 + pp, :],
                                         ACT.Copy).then_inc(vt_ready, 1)

                def exponentials(u):
                    row = mini[u % 2]
                    lo, hi = A.span(u)
                    act.wait_ge(nb_ready, A.u0 + u + 1)
                    nc.scalar.activation(row[:, 3, :], row[:, 2, :], ACT.Exp)
                    for h in range(4):
                        L = A.logit[u % 2][:, h, lo:hi]
                        ins = nc.scalar.activation(L, L, ACT.Exp, bias=row[:, 1, h:h + 1], scale=0.125,
                                                   accum_out=row[:, 4, h:h + 1])
                    ins.then_inc(ex_done, 1)

                n = len(A.units)
                exponentials(0)
                for u in range(n):
                    if u + 1 < n:
                        exponentials(u + 1)
                    for g, j, _ in A.chunks[u]:
                        if u:
                            act.wait_ge(at_done, A.u0 + u)
                        act.wait_ge(pt_done, g + 1)
                        nc.scalar.activation(A.pt[:, j, :], mp[:, 3 + g % 2, :], ACT.Copy).then_inc(pt_ready, 1)
                    if A.name and u:
                        attention_hi(A, u - 1)
                if A.name:
                    attention_hi(A, n - 1)

            def attention_hi(A, u):
                p = A.units[u][2]
                act.wait_ge(at_done, A.u0 + u + 1)
                nc.scalar.activation(A.out_ap(h_hi, u), mp[HD * p:HD * p + HD, 5, :].rearrange("p (h q) -> p h q", h=4),
                                     ACT.Copy).then_inc(h_hi_ready, 1)

            attention(att1)

            loop(act, COUNT["branch_a"], lambda i, k: split(SLAB["branch_a"] + AHEAD, i, k))

            def gated(name, func, dst, bias=None):
                def body(i, k):
                    split(SLAB[name] + AHEAD, i, k)
                    act.wait_ge(out_read, OUT[name] + k + 1 + 4 * i)
                    d = dst(i, k)
                    kw = {} if bias is None else {"bias": pcol("b_gate", bias + k + 4 * i)}
                    nc.scalar.activation(d, d, func, **kw).then_inc(gate_val, 1)
                loop(act, 8, body)

            gated("gate_s", ACT.Sigmoid, lambda i, k: at(gate2, k + 4 * i))
            for j in range(COUNT["glu"]):
                split(SLAB["glu"] + AHEAD, 0, j)
                for m in (2 * j, 2 * j + 1):
                    act.wait_ge(half_done, 2 * SLAB["glu"] + m + 1)
                    if m >= 2:
                        act.wait_ge(out_read, OUT["glu"] + m - 1)
                    nc.scalar.activation(tmp[m % 2], gp[:, (OUT["glu"] + m) % 2, :], ACT.Sigmoid).then_inc(glu_sig, 1)
                    act.wait_ge(out_read, OUT["glu"] + m + 1)
                    nc.scalar.activation(h_hi[:, m, :], U[:, m, :], ACT.Copy).then_inc(h_hi_ready, 1)
            for j in range(COUNT["branch_s"]):
                split(SLAB["branch_s"] + AHEAD, 0, j)
                for m in (2 * j, 2 * j + 1):
                    act.wait_ge(m_val, m + 1)
                    nc.scalar.activation(a_hi[:, m, :], gate1[:, m, :], ACT.Copy).then_inc(a_hi_ready, 1)

            def out_body(i, k):
                split(SLAB["out"] + AHEAD, i, k)
                act.wait_ge(half_done, 2 * (SLAB["out"] + k + 1) + 8 * i)
                square("post1", k, i, gp[:, (OUT["out"] + k) % 2, :], k)
            loop(act, 8, out_body)
            root("post1")
            normalised("n2", "g_mlp_pre", lambda c: act.wait_ge(x_new, X_AT["post1"] + c + 1))
            root("n2")

            with act.Fori(0, FF1_PARTS) as p:
                for k in range(FF1_PART):
                    split(SLAB["ff"] + AHEAD, p, k, PART1)
                    act.wait_ge(h_val, V_AT["ff"] + k + 1 + FF1_PART * p)
                    nc.scalar.activation(h_hi[:, k, :], fbuf[k % 2], ACT.Copy).then_inc(h_hi_ready, 1)
                for m in range(DC):
                    split(SLAB["ff"] + AHEAD, p, FF1_PART + m, PART1)
            for c in range(DC):
                act.wait_ge(out_read, OUT["ff"] + PART1 * FF1_PARTS)
                square("post2", c, 0, Fo[:, c, :], c)
            root("post2")
            act.wait_ge(spc_val, 1)
            nc.scalar.activation(spc[:, 2, :], spc[:, 1, :], ACT.Exp).then_inc(spc_exp, 1)
            normalised("n3", "g_mix2", lambda c: act.wait_ge(x_new, X_AT["post2"] + c + 1))
            root("n3")

            for name in ("q2", "k2", "v2"):
                loop(act, COUNT[name], lambda i, k: split(SLAB[name] + AHEAD, i, k))

            def u2_body(i, k):
                split(SLAB["u2"] + AHEAD, i, k)
                act.wait_ge(h_val, V_AT["uc"] + k + 1 + 4 * i)
                nc.scalar.activation(at(h_hi, k + 4 * i), at(UC, k + 4 * i), ACT.Copy).then_inc(h_hi_ready, 1)
            loop(act, 8, u2_body)
            attention(att2)

            act.wait_ge(decay_ready, 1)
            for t in range(DC):
                j = t // 2
                if t % 2 == 0:
                    split(SLAB["lru"] + AHEAD, 0, j)
                if t:
                    act.wait_ge(lru_free, t)
                for q, (row, name, d) in enumerate(((0, "ba", 0), (1, "bx", 0), (2, "ba", 1), (3, "bx", 1))):
                    o = 4 * t + q
                    if o % 8 < 7:
                        act.wait_ge(lg_done, 7 * j + o % 8 + 1)
                    else:
                        act.wait_ge(half_done, 2 * (SLAB["lru"] + j + 1))
                    nc.scalar.activation(lru[row], mp[:, o % 6, :], ACT.Sigmoid,
                                         bias=col(name, 8 * d + t)).then_inc(lru_sig, 1)
                act.wait_ge(lru_sig, 4 * t + 4)
                for d in range(2):
                    S.up(nc.scalar.activation(lru[4 + d], lru[2 * d], ACT.Tanh, scale=spc[:, 9, 8 * d + t:8 * d + t + 1]))
                for d in range(2):
                    ins = nc.scalar.activation(lru[2 * d], lru[2 * d], ACT.Exp, scale=spc[:, 8, 8 * d + t:8 * d + t + 1])
                ins.then_inc(lru_act, 1)
                act.wait_ge(lru_mid, t + 1)
                nc.scalar.activation(lru45, lru45, ACT.Sqrt).then_inc(lru_root, 1)

            gated("g2", ACT.Gelu_apprx_tanh, lambda i, k: at(G2, k + 4 * i))
            gated("za", ACT.Sigmoid, lambda i, k: tmp[k % 2], bias=0)

            def zb_body(i, k):
                split(SLAB["zb"] + AHEAD, i, k)
                act.wait_ge(out_read, OUT["zb"] + k + 1 + 4 * i)
                nc.scalar.activation(tmp[k % 2], tmp[k % 2], ACT.Sigmoid,
                                     bias=pcol("b_gate", 8 + k + 4 * i)).then_inc(gate_val, 1)
                act.wait_ge(h_val, V_AT["m2"] + k + 1 + 4 * i)
                nc.scalar.activation(at(h_hi, k + 4 * i), at(Q2, k + 4 * i), ACT.Copy).then_inc(h_hi_ready, 1)
            loop(act, 8, zb_body)

            def out2_body(i, k):
                split(SLAB["out2"] + AHEAD, i, k)
                act.wait_ge(out_read, OUT["out2"] + k + 1 + 4 * i)
                xc = at(X, k + 4 * i)
                nc.scalar.activation(at(a_hi, k + 4 * i), xc, ACT.Copy, scale=pcol("g_ffn2", k + 4 * i)).then_inc(a_hi_ready, 1)
                square("n4", k, i, xc, k)
            loop(act, 8, out2_body, unroll=8)
            root("n4")

            def ff2_part(p, chunks, slab0):
                for c in range(chunks):
                    split(slab0 + AHEAD, p, 2 * c, PART2)
                    act.wait_ge(out_read, OUT["ff2"] + slab0 - SLAB["ff2"] + 2 * c + 1 + PART2 * p)
                    nc.scalar.activation(tmp[0], tmp[0], ACT.Silu).then_inc(gate_val, 1)
                    split(slab0 + AHEAD, p, 2 * c + 1, PART2)
                    v0 = 8 * ((slab0 - SLAB["ff2"]) // PART2)
                    act.wait_ge(h_val, V_AT["ff2"] + v0 + c + 1 + 8 * p)
                    nc.scalar.activation(h_hi[:, c, :], fbuf[c % 2], ACT.Copy).then_inc(h_hi_ready, 1)
                for m in range(DC):
                    split(slab0 + AHEAD, p, 2 * chunks + m, PART2)
                    if chunks != FF2_CHUNKS[0]:
                        act.wait_ge(out_read, OUT["ff2"] + slab0 - SLAB["ff2"] + 2 * chunks + m + 1)
                        square("n5", m, 0, X[:, m, :], m)

            with act.Fori(0, 2) as p:
                ff2_part(p, FF2_CHUNKS[0], SLAB["ff2"])
            ff2_part(0, FF2_CHUNKS[2], SLAB["ff2"] + 2 * PART2)
            root("n5")

        @block.vector
        def _(dve):
            V = Tally(dve, vec_step)
            TT, TS, STT = dve.tensor_tensor, dve.tensor_scalar, dve.scalar_tensor_tensor

            def split(base, i, k, per=4):
                n = base + k
                if isinstance(i, int) and n >= NSLAB:
                    return
                dve.wait_ge(w_hi_ready, n + 1 + per * i)
                TT(w_lo[:, n % RING, :], raw[:, n % RAW, :], w_hi[:, n % RING, :].bitcast(F32),
                   ALU.subtract).then_inc(w_lo_ready, 1)

            def take(name, i, k, half=None, per=4):
                at_half = 2 * (SLAB[name] + k + 1) if half is None else 2 * SLAB[name] + half
                dve.wait_ge(half_done, at_half + 2 * per * i)
                return gp[:, (OUT[name] + k) % 2, :]

            def clear_sum():
                V.run(dve.memset(ssum, 0.0))

            def add_square(kind, c, i=0):
                n = 8 * NORM[kind] + c + 1
                dve.wait_ge(sq_done, n + 4 * i)
                dve.wait_ge(sq_added, n - 1 + 4 * i)
                TT(ssum, ssum, sq[c % 2], ALU.add).then_inc(sq_added, 1)

            def invert_root(kind):
                dve.wait_ge(rms_root, NORM[kind] + 1)
                V.run(dve.reciprocal(R[:, :], R[:, :]))

            def a_low(name, c, i, src, gain=None):
                dve.wait_ge(a_hi_ready, A_AT[name] + c + 1 + 4 * i)
                hi = at(a_hi, c + 4 * i).bitcast(F32)
                lo = at(a_lo, c + 4 * i)
                if gain is None:
                    TT(lo, src, hi, ALU.subtract).then_inc(a_lo_ready, 1)
                else:
                    STT(out=lo, in0=src, scalar=gain, in1=hi, op0=ALU.mult, op1=ALU.subtract).then_inc(a_lo_ready, 1)

            def h_low(count, chunk, src):
                dve.wait_ge(h_hi_ready, count + 1)
                TT(at(h_lo, chunk), src, at(h_hi, chunk).bitcast(F32), ALU.subtract).then_inc(h_lo_ready, 1)

            def normalised(kind, gain):
                clear_sum()
                for c in range(DC):
                    a_low(kind, c, 0, X[:, c, :], col(gain, c))
                    add_square(kind, c)

            lr, li, dt, ld, ang, tmp5, mag, sn, cs = s_w
            dve.wait_ge(s_par, 64)
            dve.wait_ge(disc_act, 1)
            V.up(TT(ld, lr, dt, ALU.mult))
            V.run(TT(ang, li, dt, ALU.mult))
            V.run(TS(tmp5, ang, 1.0 / TWO_PI, MAGIC, ALU.mult, ALU.add))
            V.run(TS(tmp5, tmp5, -MAGIC, None, ALU.add))
            V.run(STT(out=ang, in0=tmp5, scalar=-C1, in1=ang, op0=ALU.mult, op1=ALU.add))
            V.run(STT(out=ang, in0=tmp5, scalar=-C2, in1=ang, op0=ALU.mult, op1=ALU.add))
            STT(out=ang, in0=tmp5, scalar=-C3, in1=ang, op0=ALU.mult, op1=ALU.add).then_inc(disc_vec, 1)
            split(0, 0, 0)
            dve.wait_ge(disc_act, 4)
            V.up(TT(rho, mag[:, 0:PAIRS], mag[:, 0:PAIRS], ALU.mult))
            V.run(TT(cs, cs, cs, ALU.mult))
            V.up(TT(rho, rho, rho, ALU.mult))
            V.run(TS(cs, cs, -2.0, 1.0, ALU.mult, ALU.add))
            V.up(TT(d_are, mag, cs, ALU.mult))
            V.run(TT(d_aim, mag, sn, ALU.mult))
            V.up(TT(mag, lr, lr, ALU.mult))
            V.run(TT(cs, li, li, ALU.mult))
            V.up(TS(dt, d_are, -1.0, None, ALU.add))
            V.run(TT(mag, mag, cs, ALU.add))
            V.run(dve.reciprocal(mag, mag))
            V.up(TT(tmp5, dt, lr, ALU.mult))
            V.run(TT(cs, d_aim, li, ALU.mult))
            V.up(TT(sn, d_aim, lr, ALU.mult))
            V.run(TT(tmp5, tmp5, cs, ALU.add))
            V.up(TT(d_fre, tmp5, mag, ALU.mult))
            V.run(TT(cs, dt, li, ALU.mult))
            V.run(TT(sn, sn, cs, ALU.subtract))
            TT(d_fim, sn, mag, ALU.mult).then_inc(disc_vec, 1)

            normalised("n1", "g_mix_pre")
            split(1, 0, 0)
            invert_root("n1")

            s4 = [region(14336 + 512 * i, PAIRS, 32) for i in range(4)]

            def wave():
                dve.wait_ge(disc_vec, 2)
                V.run(TS(rot[:, 1, :], ang[:, 0:PAIRS], STEP / TWO_PI, None, ALU.mult))
                V.run(TS(rot[:, 2, :], rot[:, 1, :], MAGIC, -MAGIC, ALU.add, ALU.add))
                V.run(TT(rot[:, 1, :], rot[:, 1, :], rot[:, 2, :], ALU.subtract))
                V.run(TS(rot[:, 3, :], rot[:, 1, :], float(E0), None, ALU.mult))
                V.run(TS(rot[:, 2, :], rot[:, 3, :], MAGIC, -MAGIC, ALU.add, ALU.add))
                V.run(TT(rot[:, 3, :], rot[:, 3, :], rot[:, 2, :], ALU.subtract))
                for row, half, turns, n in ((e0s, e0c, 1, E0), (e1s, e1c, 3, E1)):
                    V.run(TT(row, rot[:, turns, :].unsqueeze(2).to_broadcast([P, PAIRS, n]),
                             col("iota", 0, n).unsqueeze(1).to_broadcast([P, PAIRS, n]), ALU.mult))
                    V.run(TS(half, row, MAGIC, -MAGIC, ALU.add, ALU.add))
                    ins = TT(row, row, half, ALU.subtract)
                    if n == E0:
                        V.run(ins)
                    else:
                        ins.then_inc(disc_vec, 1)

            def scale_b():
                dve.wait_ge(disc_act, 7)
                for half in (e0c, e1c):
                    V.run(TT(half, half, half, ALU.mult))
                    V.run(TS(half, half, -2.0, 1.0, ALU.mult, ALU.add))
                dve.wait_ge(s_bc, 96)
                fr = d_fre[:, 0:PAIRS].unsqueeze(2).to_broadcast([P, PAIRS, 32])
                fi = d_fim[:, 0:PAIRS].unsqueeze(2).to_broadcast([P, PAIRS, 32])
                V.up(TT(s4[0], fr, b_re, ALU.mult))
                V.up(TT(s4[1], fi, b_im, ALU.mult))
                V.up(TT(s4[2], fr, b_im, ALU.mult))
                V.run(TT(s4[3], fi, b_re, ALU.mult))
                V.up(TT(b_re, s4[0], s4[1], ALU.subtract))
                V.run(TT(b_im, s4[2], s4[3], ALU.add))
                V.run(TS(ca_im[:, 0], ca_im[:, 0], -1.0, None, ALU.mult))

            def c_power(k):
                ar = d_are[:, 0:PAIRS].unsqueeze(2).to_broadcast([P, PAIRS, 32])
                ai = d_aim[:, 0:PAIRS].unsqueeze(2).to_broadcast([P, PAIRS, 32])
                V.up(TT(s4[0], ca_re[:, k - 1], ar, ALU.mult))
                V.up(TT(s4[1], ca_im[:, k - 1], ai, ALU.mult))
                V.up(TT(s4[2], ca_im[:, k - 1], ar, ALU.mult))
                V.run(TT(s4[3], ca_re[:, k - 1], ai, ALU.mult))
                V.up(TT(ca_re[:, k], s4[0], s4[1], ALU.add))
                V.run(TT(ca_im[:, k], s4[2], s4[3], ALU.subtract))
                if k == STEP:
                    dve.memset(kloc, 0.0).then_inc(ca_ready, 1)

            def local_weights():
                dve.wait_ge(kloc_done, 1)
                dve.wait_ge(ca_ready, 1)
                for pr in range(4):
                    rows = slice(32 * pr, 32 * pr + 32)
                    ins = dve.tensor_copy(kloc[rows, :, :, rows],
                                          mp[rows, 4, :].rearrange("p (a b c) -> p a b c", a=CT, b=STEP))
                    if pr < 3:
                        V.up(ins)
                ins.then_inc(kloc_ready, 1)

            def table(ct):
                prs = slice(4 * ct, 4 * ct + 4)

                def fine(v):
                    return v[:, prs, :].unsqueeze(2).to_broadcast([P, 4, E1, E0])

                def coarse(v):
                    return v[:, prs, :].unsqueeze(3).to_broadcast([P, 4, E1, E0])

                def full(v):
                    return v.rearrange("p a (x y) -> p a x y", x=E1)
                if ct:
                    dve.wait_ge(st_ready, ct)
                V.up(TT(full(t1), coarse(e1c), fine(e0c), ALU.mult))
                V.run(TT(full(t2), coarse(e1s), fine(e0s), ALU.mult))
                V.run(TT(tab_c, t1, t2, ALU.subtract))
                V.up(TT(full(t1), coarse(e1s), fine(e0c), ALU.mult))
                V.run(TT(full(t2), coarse(e1c), fine(e0s), ALU.mult))
                V.run(TT(tab_s, t1, t2, ALU.add))

            def scan_states(ct):
                dve.wait_ge(v_done, ct + 1)
                v_re, v_im = mp[:, 0:4, 0:NB], mp[:, 0:4, NB:2 * NB]
                V.up(TT(t1, tab_c, v_re, ALU.mult))
                V.run(TT(t2, tab_s, v_im, ALU.mult))
                V.run(TT(g_re, t1, t2, ALU.add))
                V.up(TT(t1, tab_c, v_im, ALU.mult))
                TT(t2, tab_s, v_re, ALU.mult).then_inc(v_read, 1)
                dve.wait_ge(v_read, ct + 1)
                V.run(TT(g_im, t1, t2, ALU.subtract))
                for pr in range(4):
                    decay = rho[:, 4 * ct + pr:4 * ct + pr + 1].to_broadcast([P, NB])
                    V.up(dve.tensor_tensor_scan(g_re[:, pr, :], decay, g_re[:, pr, :], 0.0, ALU.mult, ALU.add))
                    V.up(dve.tensor_tensor_scan(g_im[:, pr, :], decay, g_im[:, pr, :], 0.0, ALU.mult, ALU.add))
                V.settle()

            def turn_states(ct):
                V.up(TT(t1, tab_c, g_re, ALU.mult))
                V.run(TT(t2, tab_s, g_im, ALU.mult))
                if ct:
                    dve.wait_ge(y_done, ct)
                V.run(TT(st_re, t1, t2, ALU.subtract))
                V.up(TT(t1, tab_c, g_im, ALU.mult))
                V.run(TT(t2, tab_s, g_re, ALU.mult))
                TT(st_im, t1, t2, ALU.add).then_inc(st_ready, 1)

            def ssm_out(ct):
                dve.wait_ge(y_done, ct + 1)
                STT(out=zp.rearrange("p (b s) -> p s b", s=STEP), in0=U[:, ct, :].rearrange("p (s b) -> p s b", s=STEP),
                    scalar=col("d_skip", ct), in1=mp[:, 5, :].rearrange("p (s b) -> p s b", s=STEP),
                    op0=ALU.mult, op1=ALU.add).then_inc(y_val, 1)

            def z_low(ct):
                h_low(H_AT["z"] + ct, 4 + ct, U[:, ct, :])

            after = {n: [] for n in range(SLAB["branch_a"])}
            after[0].append(wave)
            after[1].append(scale_b)
            for k in range(1, STEP + 1):
                after[1 + k].append(lambda k=k: c_power(k))
            after[7].append(local_weights)
            for ct in range(CT):
                after[3 * ct + 6].append(lambda ct=ct: table(ct))
                after[3 * ct + 7].append(lambda ct=ct: scan_states(ct))
                after[3 * ct + 8].append(lambda ct=ct: turn_states(ct))
                if ct < CT - 1:
                    after[3 * ct + 11].insert(0, lambda ct=ct: ssm_out(ct))
                    after[min(3 * ct + 12, 17)].insert(len(after[17]) if ct == 2 else 0, lambda ct=ct: z_low(ct))
            for name in ("u", "k", "v", "gate_a", "q"):
                for m in range(COUNT[name]):
                    split(SLAB[name] + AHEAD, 0, m)
                    src, r = take(name, 0, m), R[:, :]
                    if name == "u":
                        dst = U[:, m, :].rearrange("p (s b) -> p s b", s=STEP)
                        src, r = (v.rearrange("p (b s) -> p s b", s=STEP) for v in (src, r))
                    else:
                        dst = {"k": KV[:, 0, :], "v": KV[:, 1, :], "gate_a": gate1[:, m, :], "q": Q[:, min(m, 3), :]}[name]
                    if name == "gate_a" and m == 0:
                        dve.wait_ge(win_ready, 1)
                    if name == "q" and m == 0:
                        dve.wait_ge(v_done, CT // 2)
                    TT(dst, src, r, ALU.mult).then_inc(out_read, 1)
                    for piece in after[SLAB[name] + m]:
                        piece()
            ssm_out(CT - 1)
            z_low(CT - 1)

            def attention(A):
                def logits(u):
                    row, L = mini[u % 2], A.logit[u % 2]
                    b, pp, p = A.units[u]
                    lo, hi = A.span(u)
                    kv = 2 * pp + p
                    dve.wait_ge(sc_done, A.u0 + u + 1)
                    if u >= 2:
                        dve.wait_ge(pt_done, A.done[u - 2])
                    sc = A.scores()
                    if A.name:
                        TT(L[:, :, lo:hi], sc[:, :, lo:hi], bias8[:, 4 * kv:4 * kv + 4, lo:hi], ALU.add).then_inc(lg_ready, 1)
                    else:
                        for h in range(4):
                            slope = 8.0 * 2.0 ** (-8.0 * (4 * kv + h + 1) / 16)
                            ins = STT(out=L[:, h, lo:hi], in0=nd8[:, lo:hi], scalar=slope, in1=sc[:, h, lo:hi],
                                      op0=ALU.mult, op1=ALU.add)
                            if h < 3:
                                V.up(ins)
                        ins.then_inc(lg_ready, 1)
                    dve.wait_ge(lg_ready, A.u0 + u + 1)
                    sink = col(A.sinks, 4 * kv, 4)
                    V.run(dve.tensor_reduce(row[:, 0, :], L[:, :, lo:hi], AX.X, ALU.max))
                    V.run(STT(out=row[:, 0, :], in0=sink, scalar=8.0, in1=row[:, 0, :], op0=ALU.mult, op1=ALU.max))
                    V.run(TS(row[:, 1, :], row[:, 0, :], -0.125, None, ALU.mult))
                    TT(row[:, 2, :], sink, row[:, 1, :], ALU.add).then_inc(nb_ready, 1)

                def probabilities(u):
                    row, L = mini[u % 2], A.logit[u % 2]
                    lo, hi = A.span(u)
                    dve.wait_ge(ex_done, A.u0 + u + 1)
                    V.run(TT(row[:, 5, :], row[:, 3, :], row[:, 4, :], ALU.add))
                    V.run(dve.reciprocal(row[:, 5, :], row[:, 5, :]))
                    TT(L[:, :, lo:hi], L[:, :, lo:hi], row[:, 5, :].unsqueeze(2).to_broadcast([P, 4, hi - lo]),
                       ALU.mult).then_inc(pr_ready, 1)

                def outputs(u):
                    p = A.units[u][2]
                    o = mp[HD * p:HD * p + HD, 5, :].rearrange("p (h q) -> p h q", h=4)
                    dve.wait_ge(at_done, A.u0 + u + 1)
                    if A.name:
                        dve.wait_ge(h_hi_ready, H_AT["y1"] + u + 1)
                        TT(A.out_ap(h_lo, u), o, A.out_ap(h_hi, u).bitcast(F32), ALU.subtract).then_inc(h_lo_ready, 1)
                    else:
                        dve.tensor_copy(A.out_ap(Q2, u), o).then_inc(at_read, 1)

                logits(0)
                for u in range(len(A.units)):
                    probabilities(u)
                    if u + 1 < len(A.units):
                        logits(u + 1)
                    if u:
                        outputs(u - 1)
                outputs(len(A.units) - 1)

            dve.wait_ge(s_bias, 16)
            bflat = bias8.rearrange("p a b -> p (a b)")
            V.run(TS(bflat, bflat, 8.0, None, ALU.mult))
            attention(att1)

            for j in range(COUNT["branch_a"]):
                split(SLAB["branch_a"] + AHEAD, 0, j)
                for m in (2 * j, 2 * j + 1):
                    src = take("branch_a", 0, m, half=m + 1)
                    dve.wait_ge(gate_val, G_AT["gate_a"] + m + 1)
                    TT(gate1[:, m, :], src, gate1[:, m, :], ALU.mult).then_inc(out_read, 1)

            def scaled(name, dst, per=0):
                def body(i, k):
                    split(SLAB[name] + AHEAD, i, k)
                    TT(dst(i, k), take(name, i, k), R[:, :], ALU.mult).then_inc(out_read, 1)
                loop(dve, COUNT[name], body)

            scaled("gate_s", lambda i, k: at(gate2, k + 4 * i))
            for j in range(COUNT["glu"]):
                split(SLAB["glu"] + AHEAD, 0, j)
                for m in (2 * j, 2 * j + 1):
                    dve.wait_ge(glu_sig, m + 1)
                    TT(U[:, m, :], U[:, m, :], tmp[m % 2], ALU.mult).then_inc(out_read, 1)
                    h_low(H_AT["z2"] + m, m, U[:, m, :])
            for j in range(COUNT["branch_s"]):
                split(SLAB["branch_s"] + AHEAD, 0, j)
                for m in (2 * j, 2 * j + 1):
                    src = take("branch_s", 0, m, half=m + 1)
                    dve.wait_ge(gate_val, G_AT["gate_s"] + m + 1)
                    TT(tmp[m % 2], src, gate2[:, m, :], ALU.mult).then_inc(out_read, 1)
                    dve.wait_ge(out_read, OUT["branch_s"] + m + 1)
                    TT(gate1[:, m, :], gate1[:, m, :], tmp[m % 2], ALU.add).then_inc(m_val, 1)
                    a_low("merged", m, 0, gate1[:, m, :])

            clear_sum()

            def out_body(i, k):
                split(SLAB["out"] + AHEAD, i, k)
                add_square("post1", k, i)
                TS(at(Y, k + 4 * i), take("out", i, k), pcol("g_mix_post", k + 4 * i), None,
                   ALU.mult).then_inc(out_read, 1)
            loop(dve, 8, out_body)
            invert_root("post1")
            dve.wait_ge(s_x2, 16)
            clear_sum()
            dve.wait_ge(out_read, OUT["out"] + DC)
            for c in range(DC + 1):
                if c < DC:
                    V.run(TT(tmp[c % 2], Y[:, c, :], R[:, :], ALU.mult))
                    TT(X[:, c, :], X[:, c, :], tmp[c % 2], ALU.add).then_inc(x_new, 1)
                if c:
                    a_low("n2", c - 1, 0, X[:, c - 1, :], col("g_mlp_pre", c - 1))
                    add_square("n2", c - 1)
            invert_root("n2")
            V.run(dve.memset(Fo.rearrange("p a b -> p (a b)"), 0.0))

            with dve.Fori(0, FF1_PARTS) as p:
                V.start, V.i, V.per = V.n, p, 0
                for k in range(FF1_PART):
                    split(SLAB["ff"] + AHEAD, p, k, PART1)
                    TT(tmp[k % 2], take("ff", p, k, per=PART1), R[:, :], ALU.mult).then_inc(out_read, 1)
                    dve.wait_ge(out_read, OUT["ff"] + k + 1 + PART1 * p)
                    STT(out=fbuf[k % 2], in0=tmp[k % 2], scalar=0.0, in1=tmp[k % 2], op0=ALU.max,
                        op1=ALU.mult).then_inc(h_val, 1)
                    for q in ([k - 1] if k else []) + ([k] if k == FF1_PART - 1 else []):
                        h_low(H_AT["ff"] + q + FF1_PART * p, q, fbuf[q % 2])
                for m in range(DC):
                    split(SLAB["ff"] + AHEAD, p, FF1_PART + m, PART1)
                    src = take("ff", p, FF1_PART + m, per=PART1)
                    TT(Fo[:, m, :], Fo[:, m, :], src, ALU.add).then_inc(out_read, 1)
            V.i = 0
            clear_sum()
            for c in range(DC):
                add_square("post2", c)
            invert_root("post2")
            lam = col("lam", 0, 16)
            r = [spc[:, i, :] for i in range(12)]
            V.run(TS(r[0], lam, -1.0, None, ALU.mult))
            V.run(TT(r[1], r[0], lam, ALU.min))
            TS(r[0], r[0], 0.0, None, ALU.max).then_inc(spc_val, 1)
            clear_sum()
            dve.wait_ge(out_read, OUT["ff"] + PART1 * FF1_PARTS)
            for c in range(DC + 1):
                if c < DC:
                    V.run(STT(out=tmp[c % 2], in0=Fo[:, c, :], scalar=col("g_mlp_post", c), in1=R[:, :],
                              op0=ALU.mult, op1=ALU.mult))
                    TT(X[:, c, :], X[:, c, :], tmp[c % 2], ALU.add).then_inc(x_new, 1)
                if c:
                    a_low("n3", c - 1, 0, X[:, c - 1, :], col("g_mix2", c - 1))
                    add_square("n3", c - 1)
            invert_root("n3")

            scaled("q2", lambda i, k: at(Q2, k + 4 * i))
            scaled("k2", lambda i, k: KV2[:, k, :])
            scaled("v2", lambda i, k: KV2[:, 2 + k, :])
            dve.wait_ge(spc_exp, 1)
            V.run(TS(r[3], r[2], 2.0, None, ALU.add))
            V.run(dve.reciprocal(r[3], r[3]))
            V.run(TT(r[3], r[3], r[2], ALU.mult))
            V.run(TT(r[4], r[3], r[3], ALU.mult))
            V.run(TS(r[5], r[4], 1.0 / 17, None, ALU.mult))
            for d in (15, 13, 11, 9, 7, 5, 3):
                V.run(STT(out=r[5], in0=r[5], scalar=1.0 / d, in1=r[4], op0=ALU.add, op1=ALU.mult))
            V.run(STT(out=r[5], in0=r[5], scalar=1.0, in1=r[3], op0=ALU.add, op1=ALU.mult))
            V.run(STT(out=r[5], in0=r[5], scalar=2.0, in1=r[0], op0=ALU.mult, op1=ALU.add))
            V.run(TS(r[8], r[5], -8.0, None, ALU.mult))
            TS(r[9], r[5], 4.0, None, ALU.mult).then_inc(decay_ready, 1)

            def u2_body(i, k):
                split(SLAB["u2"] + AHEAD, i, k)
                u, y = tmp[k % 2], at(UC, k + 4 * i)
                TT(u, take("u2", i, k), R[:, :], ALU.mult).then_inc(out_read, 1)
                dve.wait_ge(out_read, OUT["u2"] + k + 1 + 4 * i)
                V.run(TS(y, u, pcol("conv_w", 16 + k + 4 * i), pcol("conv_b", k + 4 * i), ALU.mult, ALU.add))
                V.run(STT(out=y[:, 2:T], in0=u[:, 0:T - 2], scalar=pcol("conv_w", k + 4 * i), in1=y[:, 2:T],
                          op0=ALU.mult, op1=ALU.add))
                V.run(STT(out=y[:, 1:T], in0=u[:, 0:T - 1], scalar=pcol("conv_w", 8 + k + 4 * i), in1=y[:, 1:T],
                          op0=ALU.mult, op1=ALU.add))
                STT(out=y[:, 0:T - 1], in0=u[:, 1:T], scalar=pcol("conv_w", 24 + k + 4 * i), in1=y[:, 0:T - 1],
                    op0=ALU.mult, op1=ALU.add).then_inc(h_val, 1)
                h_low(H_AT["uc"] + k + 4 * i, k + 4 * i, y)
            loop(dve, 8, u2_body, V, 3)
            dve.wait_ge(s_nd, 16)
            attention(att2)

            for t in range(DC):
                if t % 2 == 0:
                    split(SLAB["lru"] + AHEAD, 0, t // 2)
                dve.wait_ge(lru_act, t + 1)
                TS(lru45, lru45, 0.0, None, ALU.max).then_inc(lru_mid, 1)
                for d in range(2):
                    V.up(TT(lru[1 + 2 * d], lru[1 + 2 * d], UC[:, t, :], ALU.mult))
                dve.wait_ge(lru_root, t + 1)
                for d in range(2):
                    V.up(STT(out=lru[4 + d], in0=lru[2 * d], scalar=1.0, in1=lru[4 + d], op0=ALU.add, op1=ALU.mult))
                V.settle()
                for d in range(2):
                    V.up(TT(lru[1 + 2 * d], lru[1 + 2 * d], lru[4 + d], ALU.mult))
                V.settle()
                V.up(dve.tensor_tensor_scan(HS[:, t, :], lru[0], lru[1], 0.0, ALU.mult, ALU.add))
                V.run(dve.tensor_tensor_scan(lru[5][:, ::-1], lru[2][:, ::-1], lru[3][:, ::-1], 0.0, ALU.mult, ALU.add))
                TT(HS[:, t, :], HS[:, t, :], lru[5], ALU.add).then_inc(lru_free, 1)

            scaled("g2", lambda i, k: at(G2, k + 4 * i))
            dve.wait_ge(lru_free, DC)
            dve.wait_ge(gate_val, G_AT["g2"] + DC)

            def za_body(i, k):
                split(SLAB["za"] + AHEAD, i, k)
                y = at(HS, k + 4 * i)
                TT(tmp[k % 2], take("za", i, k), R[:, :], ALU.mult).then_inc(out_read, 1)
                V.run(TT(y, y, at(G2, k + 4 * i), ALU.mult))
                dve.wait_ge(gate_val, G_AT["za"] + k + 1 + 4 * i)
                V.up(TT(y, y, tmp[k % 2], ALU.mult))
            loop(dve, 8, za_body, V, 2)
            V.settle()
            dve.wait_ge(at_read, len(att2.units))

            def zb_body(i, k):
                split(SLAB["zb"] + AHEAD, i, k)
                y = at(Q2, k + 4 * i)
                TT(tmp[k % 2], take("zb", i, k), R[:, :], ALU.mult).then_inc(out_read, 1)
                dve.wait_ge(gate_val, G_AT["zb"] + k + 1 + 4 * i)
                V.run(TT(y, y, tmp[k % 2], ALU.mult))
                TT(y, y, at(HS, k + 4 * i), ALU.add).then_inc(h_val, 1)
                h_low(H_AT["m2"] + k + 4 * i, k + 4 * i, y)
            loop(dve, 8, zb_body, V, 1)

            clear_sum()

            def out2_body(i, k):
                split(SLAB["out2"] + AHEAD, i, k)
                xc = at(X, k + 4 * i)
                TT(xc, xc, take("out2", i, k), ALU.add).then_inc(out_read, 1)
                a_low("n4", k, i, xc, pcol("g_ffn2", k + 4 * i))
                add_square("n4", k, i)
            loop(dve, 8, out2_body)
            invert_root("n4")

            def ff2_part(p, chunks, slab0):
                s0 = slab0 - SLAB["ff2"]
                v0 = 8 * (s0 // PART2)
                for c in range(chunks):
                    for e in range(2):
                        split(slab0 + AHEAD, p, 2 * c + e, PART2)
                        TT(tmp[e], take("ff2", p, s0 + 2 * c + e, per=PART2), R[:, :], ALU.mult).then_inc(out_read, 1)
                    dve.wait_ge(out_read, OUT["ff2"] + s0 + 2 * c + 2 + PART2 * p)
                    dve.wait_ge(gate_val, G_AT["ff2"] + v0 + c + 1 + 8 * p)
                    TT(fbuf[c % 2], tmp[0], tmp[1], ALU.mult).then_inc(h_val, 1)
                    for q in ([c - 1] if c else []) + ([c] if c == chunks - 1 else []):
                        h_low(H_AT["ff2"] + v0 + q + 8 * p, q, fbuf[q % 2])
                for m in range(DC):
                    split(slab0 + AHEAD, p, 2 * chunks + m, PART2)
                    src = take("ff2", p, s0 + 2 * chunks + m, per=PART2)
                    TT(X[:, m, :], X[:, m, :], src, ALU.add).then_inc(out_read, 1)
                    if chunks != FF2_CHUNKS[0]:
                        add_square("n5", m)

            with dve.Fori(0, 2) as p:
                ff2_part(p, FF2_CHUNKS[0], SLAB["ff2"])
            clear_sum()
            ff2_part(0, FF2_CHUNKS[2], SLAB["ff2"] + 2 * PART2)
            invert_root("n5")
            for c in range(DC):
                STT(out=OUTB[:, c, :], in0=X[:, c, :], scalar=col("g_fin2", c), in1=R[:, :], op0=ALU.mult,
                    op1=ALU.mult).then_inc(x_new, 1)

        @block.tensor
        def _(pe):
            def gemm(base, i, k, tiles, outs, x_hi, x_lo, out0, ready=None, per=4):
                n = base + k
                pe.wait_ge(w_lo_ready, n + 1 + per * i)
                for e in range(outs):
                    o = out0 + outs * k + e
                    if o >= 2:
                        pe.wait_ge(out_read, o - 1 + outs * per * i)
                    bank = gp[:, o % 2, :]
                    for t in range(tiles):
                        if ready:
                            ready(t)
                        cols = slice((e * tiles + t) * P, (e * tiles + t + 1) * P)
                        hi, lo = w_hi[:, n % RING, cols], w_lo[:, n % RING, cols]
                        pe.matmul(bank, hi, x_hi(t), start=t == 0, stop=False)
                        pe.matmul(bank, hi, x_lo(t), start=False, stop=False)
                        ins = pe.matmul(bank, lo, x_hi(t), start=False, stop=t == tiles - 1)
                    ins.then_inc(half_done, 2 // outs)

            def a(t):
                return a_hi[:, t, :]

            def al(t):
                return a_lo[:, t, :]

            def h(t):
                return h_hi[:, t, :]

            def hl(t):
                return h_lo[:, t, :]

            def mean_square(kind):
                pe.wait_ge(sq_added, 8 * NORM[kind] + 8)
                pe.matmul(mp[:, 5, :], ones, ssum, start=True, stop=True).then_inc(rms_sum, 1)

            def a_stage(name, i, k, ready=None):
                gemm(SLAB[name], i, k, 8, 1, a, al, OUT[name], ready)

            def a_wait(name):
                return lambda t: pe.wait_ge(a_lo_ready, A_AT[name] + t + 1)

            def inputs(ct):
                pe.wait_ge(out_read, OUT["u"] + ct + 1)
                pe.wait_ge(win_ready, 1)
                if ct:
                    pe.wait_ge(v_read, ct)
                for part in range(2):
                    for s in range(STEP):
                        for pr in range(4):
                            rows = slice(32 * pr, 32 * pr + 32)
                            ins = pe.matmul(mp[:, pr, part * NB:(part + 1) * NB], win[rows, ct, s, part, :],
                                            U[rows, ct, s * NB:(s + 1) * NB], start=s == 0, stop=s == STEP - 1)
                ins.then_inc(v_done, 1)

            def local_products():
                pe.wait_ge(ca_ready, 1)
                for ct in range(CT):
                    for pr in range(4):
                        rows, q = slice(32 * pr, 32 * pr + 32), 4 * ct + pr
                        bank = mp[rows, 4, ct * STEP * 32:(ct + 1) * STEP * 32]
                        pe.matmul(bank, b_re[:, q, :], ca_re[:, 0:STEP, q, :], start=True, stop=False)
                        ins = pe.matmul(bank, b_im[:, q, :], ca_im[:, 0:STEP, q, :], start=False, stop=True)
                ins.then_inc(kloc_done, 1)

            def outputs(ct):
                pe.wait_ge(kloc_ready, 1)
                pe.wait_ge(st_ready, ct + 1)
                if ct:
                    pe.wait_ge(y_val, ct)
                for k in range(STEP):
                    pe.matmul(mp[:, 5, k * NB:T], kloc[:, ct, k, :], U[:, ct, 0:T - k * NB], start=k == 0, stop=False,
                              skip_group_check=True)
                for pr in range(4):
                    rows, q = slice(32 * pr, 32 * pr + 32), 4 * ct + pr
                    for s in range(STEP):
                        bank = mp[rows, 5, s * NB + 1:(s + 1) * NB]
                        pe.matmul(bank, ca_re[:, s + 1, q, :], st_re[:, pr, 0:NB - 1], start=False, stop=False,
                                  skip_group_check=True)
                        ins = pe.matmul(bank, ca_im[:, s + 1, q, :], st_im[:, pr, 0:NB - 1], start=False,
                                        stop=s == STEP - 1, skip_group_check=True)
                ins.then_inc(y_done, 1)

            def attention(A):
                for pp in range(A.pairs):
                    for b in range(T // P):
                        ins = pe.transpose(mp[:, 3 + pp, b * P:(b + 1) * P], A.kt[:, A.v0 + pp + (0 if A.name else 0), b * P:(b + 1) * P],
                                           ident)
                    ins.then_inc(vt_done, 1)

                def scores(u):
                    b, pp, p = A.units[u]
                    rows = slice(HD * p, HD * p + HD)
                    if A.u0 + u:
                        pe.wait_ge(lg_ready, A.u0 + u)
                    for h4 in range(4):
                        for g, j, kb in A.chunks[u]:
                            ins = pe.matmul(A.scores()[:, h4, j * P:(j + 1) * P], A.q[rows, 4 * pp + h4, b * P:(b + 1) * P],
                                            A.kt[rows, A.k0 + pp, kb * P:(kb + 1) * P], start=True, stop=True)
                    ins.then_inc(sc_done, 1)

                n = len(A.units)
                scores(0)
                pe.wait_ge(vt_ready, A.pairs + (A.u0 > 0))
                for u in range(n):
                    b, pp, p = A.units[u]
                    if u + 1 < n:
                        scores(u + 1)
                    pe.wait_ge(pr_ready, A.u0 + u + 1)
                    for g, j, kb in A.chunks[u]:
                        if g >= 2:
                            pe.wait_ge(pt_ready, g - 1)
                        for h4 in range(4):
                            ins = pe.transpose(mp[:, 3 + g % 2, h4 * P:(h4 + 1) * P],
                                               A.logit[u % 2][:, h4, j * P:(j + 1) * P], ident)
                        ins.then_inc(pt_done, 1)
                    if u:
                        if A.name:
                            pe.wait_ge(h_lo_ready, H_AT["y1"] + u)
                        else:
                            pe.wait_ge(at_read, u)
                    for x, (g, j, kb) in enumerate(A.chunks[u]):
                        pe.wait_ge(pt_ready, g + 1)
                        ins = pe.matmul(mp[HD * p:HD * p + HD, 5, :], A.vt[:, pp, kb, HD * p:HD * p + HD],
                                        A.pt[:, j, :], start=x == 0, stop=x == len(A.chunks[u]) - 1)
                    ins.then_inc(at_done, 1)

            for n in range(SLAB["branch_a"]):
                gemm(0, 0, n, 8, 1, a, al, 0, a_wait("n1") if n == 0 else None)
                if n == 0:
                    mean_square("n1")
                if n == 6:
                    local_products()
                for ct in range(CT):
                    if n == 3 * ct + 6:
                        inputs(ct)
                    if ct < CT - 1 and n == 3 * ct + 10:
                        outputs(ct)
            outputs(CT - 1)
            pe.wait_ge(out_read, OUT["q"] + 4)
            pe.wait_ge(y_val, CT)
            attention(att1)
            pe.wait_ge(h_lo_ready, H_AT["y1"] + len(att1.units))
            for j in range(COUNT["branch_a"]):
                gemm(SLAB["branch_a"], 0, j, 4, 2, h, hl, OUT["branch_a"])
            loop(pe, 8, lambda i, k: a_stage("gate_s", i, k))
            for j in range(COUNT["glu"]):
                gemm(SLAB["glu"], 0, j, 4, 2, lambda t: h(4 + t), lambda t: hl(4 + t), OUT["glu"])
            for j in range(COUNT["branch_s"]):
                gemm(SLAB["branch_s"], 0, j, 4, 2, h, hl, OUT["branch_s"],
                     (lambda t: pe.wait_ge(h_lo_ready, H_AT["z2"] + t + 1)) if j == 0 else None)
            pe.wait_ge(a_lo_ready, A_AT["merged"] + DC)
            loop(pe, 8, lambda i, k: a_stage("out", i, k))
            mean_square("post1")
            for t in range(DC):
                pe.wait_ge(a_lo_ready, A_AT["n2"] + t + 1)
            mean_square("n2")
            with pe.Fori(0, FF1_PARTS) as p:
                for k in range(FF1_PART):
                    gemm(SLAB["ff"], p, k, 8, 1, a, al, OUT["ff"], per=PART1)
                for m in range(DC):
                    gemm(SLAB["ff"], p, FF1_PART + m, FF1_PART, 1, h, hl, OUT["ff"],
                         (lambda t: pe.wait_ge(h_lo_ready, H_AT["ff"] + t + 1 + FF1_PART * p)) if m == 0 else None,
                         per=PART1)
            mean_square("post2")

            for t in range(DC):
                pe.wait_ge(a_lo_ready, A_AT["n3"] + t + 1)
            mean_square("n3")
            for name in ("q2", "k2", "v2", "u2"):
                loop(pe, COUNT[name], lambda i, k: a_stage(name, i, k))
            pe.wait_ge(out_read, OUT["u2"] + 8)
            attention(att2)
            for j in range(COUNT["lru"]):
                n = SLAB["lru"] + j
                pe.wait_ge(w_lo_ready, n + 1)
                for q in range(8):
                    o = 8 * j + q
                    if o >= 6:
                        pe.wait_ge(lru_sig, o - 5)
                    elif o == 0:
                        pe.wait_ge(at_read, len(att2.units))
                    t, cols = o // 4, slice(q * P, (q + 1) * P)
                    hi, lo = w_hi[:, n % RING, cols], w_lo[:, n % RING, cols]
                    pe.matmul(mp[:, o % 6, :], hi, h(t), start=True, stop=False)
                    pe.matmul(mp[:, o % 6, :], hi, hl(t), start=False, stop=False)
                    ins = pe.matmul(mp[:, o % 6, :], lo, h(t), start=False, stop=True)
                    if q < 7:
                        ins.then_inc(lg_done, 1)
                    else:
                        ins.then_inc(half_done, 2)
            for name in ("g2", "za", "zb"):
                loop(pe, 8, lambda i, k: a_stage(name, i, k))
            for t in range(DC):
                pe.wait_ge(h_lo_ready, H_AT["m2"] + t + 1)
            loop(pe, 8, lambda i, k: gemm(SLAB["out2"], i, k, 8, 1, h, hl, OUT["out2"]))
            pe.wait_ge(a_lo_ready, A_AT["n4"] + DC)
            mean_square("n4")

            def ff2_part(p, chunks, slab0):
                s0 = slab0 - SLAB["ff2"]
                v0 = 8 * (s0 // PART2)
                for k in range(2 * chunks):
                    gemm(SLAB["ff2"], p, s0 + k, 8, 1, a, al, OUT["ff2"], per=PART2)
                for m in range(DC):
                    gemm(SLAB["ff2"], p, s0 + 2 * chunks + m, chunks, 1, h, hl, OUT["ff2"],
                         (lambda t: pe.wait_ge(h_lo_ready, H_AT["ff2"] + v0 + t + 1 + 8 * p)) if m == 0 else None,
                         per=PART2)

            with pe.Fori(0, 2) as p:
                ff2_part(p, FF2_CHUNKS[0], SLAB["ff2"])
            ff2_part(0, FF2_CHUNKS[2], SLAB["ff2"] + 2 * PART2)
            mean_square("n5")


def tiles_of(w, order_in=None, order_out=None):
    if order_in is not None:
        w = w.reshape(-1, HD, w.shape[1])[np.array(order_in)].reshape(w.shape)
    if order_out is not None:
        w = w.reshape(w.shape[0], -1, HD)[:, np.array(order_out)].reshape(w.shape)
    k, n = w.shape[0] // P, w.shape[1] // P
    return w.reshape(k, P, n, P).transpose(2, 0, 1, 3)


def lay_out(v):
    f = {k: np.asarray(a)[0] if a.ndim > 1 and a.shape[0] == 1 else np.asarray(a) for k, a in v.items()}
    stream = []

    def put(tiles):
        tiles = tiles.reshape(-1, tiles.shape[-3], P, P)
        per = tiles.shape[1] if tiles.shape[1] > 4 else 8
        tiles = tiles.reshape(-1, per, P, P)
        slab = np.zeros((tiles.shape[0], P, TILES, P), tiles.dtype)
        slab[:, :, :per] = tiles.transpose(0, 2, 1, 3)
        stream.append(slab.reshape(-1, P, TILES * P))

    w = f["w_in"]
    q, k, v1, u, ga, gs = np.split(w, [512, 640, 768, 1280, 2304], axis=1)
    for part in (u, k, v1, ga):
        put(tiles_of(part))
    put(tiles_of(q, None, HEADS1))
    put(tiles_of(f["w_attn_branch"], HEADS1))
    put(tiles_of(gs))
    put(tiles_of(f["w_glu"]))
    put(tiles_of(f["w_ssm_branch"]))
    put(tiles_of(f["w_out"]))
    wi, wo = tiles_of(f["w_ff_in"]), tiles_of(f["w_ff_out"])
    for p in range(FF1_PARTS):
        c = slice(p * FF1_PART, (p + 1) * FF1_PART)
        put(wi[c])
        put(wo[:, c])
    u, g, q, k, v1, za, zb = np.split(f["w_in_2"], [1024, 2048, 3072, 3328, 3584, 4608], axis=1)
    put(tiles_of(q, None, HEADS2))
    put(tiles_of(k))
    put(tiles_of(v1))
    put(tiles_of(u, None, HEADS2))
    gates = np.zeros((DC, 2, 2, P, P), np.float32)
    order = np.array(HEADS2).reshape(DC, 2)
    for half in range(2):
        rows = slice(HD * half, HD * half + HD)
        for kind, name in enumerate(("lru_wa_2", "lru_wx_2")):
            gates[:, :, kind, rows, rows] = f[name][:, order[:, half]].transpose(1, 0, 2, 3)
    put(gates.reshape(4, 8, P, P))
    for part in (g, za, zb):
        put(tiles_of(part, None, HEADS2))
    put(tiles_of(f["w_out_2"], HEADS2))
    wi, wo = tiles_of(f["w_ffn_in_2"]), tiles_of(f["w_ffn_out_2"])
    hid, c0 = wi.shape[0] // 2, 0
    for n in FF2_CHUNKS:
        c = slice(c0, c0 + n)
        put(np.stack([wi[:hid][c], wi[hid:][c]], axis=1).reshape(2 * n, DC, P, P))
        put(wo[:, c])
        c0 += n

    def column(a, order=None):
        a = a.reshape(-1, HD)
        if order is not None:
            n = len(order)
            a = np.concatenate([a[i:i + n][np.array(order)] for i in range(0, a.shape[0], n)])
        return a.reshape(-1, P).T

    def across(a):
        return np.broadcast_to(a.reshape(1, -1), (P, a.size))

    cols = {
        "g_mix_pre": column(f["norm_mix_pre"]), "g_mix_post": column(f["norm_mix_post"]),
        "g_mlp_pre": column(f["norm_mlp_pre"]), "g_mlp_post": column(f["norm_mlp_post"]),
        "sinks": across(f["sinks"]), "d_skip": column(f["d_skip"]), "g_mix2": column(f["norm_mix_g_2"]),
        "b_gate": column(f["b_gate_2"], HEADS2), "conv_w": column(f["conv_w_2"], HEADS2),
        "conv_b": column(f["conv_b_2"], HEADS2), "lam": column(f["lru_lambda_2"], HEADS2),
        "ba": column(f["lru_ba_2"], HEADS2), "bx": column(f["lru_bx_2"], HEADS2),
        "sinks2": across(f["attn_sink_2"]), "g_ffn2": column(f["norm_ffn_g_2"]), "g_fin2": column(f["norm_final_g_2"]),
        "iota": across(np.arange(16, dtype=np.float32)), "eps": np.full((P, 1), EPS, np.float32),
        "pad": np.zeros((P, 3), np.float32), "ident": np.eye(P, dtype=np.float32), "ones": np.ones((P, P), np.float32),
    }
    params = np.concatenate([cols[name] for name, _ in _cols], axis=1)
    assert params.shape == (P, NCOL)

    G, N = f["lam_re"].shape
    C = SSM_CH // G

    def by_both(a):
        a = np.broadcast_to(a.reshape(G, -1), (G, N))
        state = a.reshape(PAIRS, P).T
        pair = a.reshape(CT, 4, 1, 2 * N)
        channel = np.broadcast_to(pair, (CT, 4, 2 * C, 2 * N)).reshape(CT, P, P).transpose(1, 0, 2).reshape(P, CT * P)
        return np.concatenate([state, channel], axis=1)

    s5p = np.stack([by_both(f["lam_re"]), by_both(f["lam_im"]), by_both(f["log_dt"])], axis=1)

    def diagonal(a):
        r, c = a.shape[1:]
        d = np.zeros((PAIRS, 2, r, 2, c), a.dtype)
        for g in range(2):
            d[:, g, :, g, :] = a[g::2]
        return d.reshape(PAIRS, 2 * r, 2 * c)

    b = [diagonal(f[n]) for n in ("b_re", "b_im")]
    c = [diagonal(f[n].transpose(0, 2, 1)) for n in ("c_re", "c_im")]
    s5b = np.stack([a.transpose(1, 0, 2) for a in b], axis=1)
    s5c = np.stack([a.transpose(1, 0, 2) for a in c], axis=1)
    s5bt = np.stack([a.transpose(0, 2, 1).reshape(CT, P, P).transpose(1, 0, 2) for a in b], axis=1)

    dist = np.arange(P)[:, None] + P - np.arange(2 * P)[None, :]
    exact = NBUCKET // 2
    df = np.maximum(dist, 1).astype(np.float32)
    large = exact + (np.log(df / np.float32(exact)) / np.float32(np.log(MAXDIST / exact))
                     * np.float32(NBUCKET - exact)).astype(np.int32)
    bucket = np.where(dist < exact, np.maximum(dist, 0), np.minimum(large, NBUCKET - 1))
    inside = (dist >= 0) & (dist < P)
    bias1 = np.full((P, 8, 2 * P), -1e30, np.float32)
    rb = np.asarray(v["rel_bias"])
    for hd in range(8):
        bias1[:, hd][inside] = rb[bucket[inside], hd]
    far = np.abs(np.arange(P)[:, None] + P - np.arange(3 * P)[None, :])
    nd = np.where(far <= P, -far, -1e30).astype(np.float32)

    x = np.asarray(v["x"])[0].T.reshape(DC, P, T).transpose(1, 0, 2)
    return {"slabs": np.concatenate(stream), "params": params, "s5p": s5p, "s5bt": s5bt, "s5b": s5b, "s5c": s5c,
            "bias1": bias1, "nd2": nd, "x_in": x}


def kernel(**inputs):
    import concourse.bacc as bacc
    from concourse.bass_utils import run_bass_kernel_spmd as run

    arrays = {k: np.ascontiguousarray(a) for k, a in lay_out(inputs).items()}
    assert arrays["slabs"].shape[0] == NSLAB, arrays["slabs"].shape
    nc = bacc.Bacc("TRN2", target_bir_lowering=False, num_devices=1)
    args = {k: nc.dram_tensor(k, a.shape, F32, kind="ExternalInput").ap() for k, a in arrays.items()}
    out = nc.dram_tensor("out_t", (P, DC, T), F32, kind="ExternalOutput").ap()
    build(nc, out=out, **args)
    r = run(nc, [arrays], core_ids=[0])
    y = r.results[0]["out_t"]
    return np.ascontiguousarray(y.transpose(2, 1, 0).reshape(1, T, D))
```

```python
from contextlib import ExitStack

import numpy as np

import concourse.bass as bass
from concourse import mybir

F32 = mybir.dt.float32
F32R = mybir.dt.float32r
ALU = mybir.AluOpType
ACT = mybir.ActivationFunctionType
AX = mybir.AxisListType

P = 128
D = 1024
T = 512
DC = D // P
HD = 64
EPS = 1e-6

NBUCKET, MAXDIST = 32, 128
SSM_CH = 512
CT = SSM_CH // P
PAIRS = 16
STEP = 4
NB = T // STEP
E0 = 16
E1 = NB // E0
FF1_PARTS = 4
FF1_PART = 8
FF2_CHUNKS = [8, 8, 6]

TILES = 8
RAW = 2
RING = 4
AHEAD = 2

HEADS1 = [par * 4 + h for h in range(4) for par in range(2)]
HEADS2 = [(2 * pp + par) * 4 + h for pp in range(2) for h in range(4) for par in range(2)]

_counts = [("u", 4), ("k", 1), ("v", 1), ("gate_a", 8), ("q", 4), ("gate_s", 8), ("branch_a", 4),
           ("glu", 2), ("branch_s", 4), ("out", 8), ("ff", 16 * FF1_PARTS),
           ("q2", 8), ("k2", 2), ("v2", 2), ("u2", 8), ("g2", 8), ("mix", 20),
           ("out2", 8), ("ff2", sum(2 * c + 8 for c in FF2_CHUNKS))]
MIX = []
for _t in range(DC):
    MIX += ([("lru", _t // 2)] if _t % 2 == 0 else []) + [("zb", _t)] + ([("za", _t - 1)] if _t else [])
MIX += [("za", DC - 1)]
SLAB, _n = {}, 0
for _name, _c in _counts:
    SLAB[_name] = _n
    _n += _c
NSLAB = _n
COUNT = dict(_counts)
assert NSLAB % RING == 0

_outs = [("u", 4), ("k", 1), ("v", 1), ("gate_a", 8), ("q", 4), ("gate_s", 8), ("branch_a", 8), ("glu", 4),
         ("branch_s", 8), ("out", 8), ("ff", 16 * FF1_PARTS), ("q2", 8), ("k2", 2), ("v2", 2), ("u2", 8),
         ("g2", 8), ("mix", 16), ("out2", 8), ("ff2", sum(2 * c + 8 for c in FF2_CHUNKS))]
OUT, _n = {}, 0
for _name, _c in _outs:
    OUT[_name] = _n
    _n += _c

MIX_SLAB = {key: SLAB["mix"] + i for i, key in enumerate(MIX)}
MIX_OUT = {key: OUT["mix"] + i for i, key in enumerate(k for k in MIX if k[0] != "lru")}
MIX_GATE = [g for t in range(1, DC + 1) for g in [("zb", t - 1)] + ([("za", t - 2)] if t > 1 else [])] + [("za", DC - 1)]

_cols = [("g_mix_pre", 8), ("g_mix_post", 8), ("g_mlp_pre", 8), ("g_mlp_post", 8), ("sinks", 8), ("d_skip", 4),
         ("g_mix2", 8), ("b_gate", 16), ("conv_w", 32), ("conv_b", 8), ("lam", 16), ("ba", 16), ("bx", 16),
         ("sinks2", 16), ("g_ffn2", 8), ("g_fin2", 8), ("iota", 16), ("eps", 1), ("pad", 3),
         ("ident", P), ("ones", P)]
COL, _n = {}, 0
for _name, _c in _cols:
    COL[_name] = _n
    _n += _c
NCOL = _n
SW = PAIRS + CT * P

MAGIC = 1.5 * 2.0 ** 23
TWO_PI = 2.0 * np.pi
C1 = 6.28125
C2 = float(np.float32(np.round((TWO_PI - C1) * 2.0 ** 20) / 2.0 ** 20))
C3 = float(np.float32(TWO_PI - C1 - C2))
TURN = 6.283185


def build(nc, slabs, params, s5p, s5bt, s5b, s5c, bias1, nd2, x_in, out):
    ctx = ExitStack()
    with ctx:
        def sb(name, shape, dt=F32):
            return ctx.enter_context(nc.sbuf_tensor(name, shape, dt))

        def sem(name):
            return ctx.enter_context(nc.semaphore(name))

        raw = sb("raw", [P, RAW, TILES * P])
        w_hi = sb("w_hi", [P, RING, TILES * P], F32R)
        w_lo = sb("w_lo", [P, RING, TILES * P], F32R)
        a_hi = sb("a_hi", [P, DC, T], F32R)
        a_lo = sb("a_lo", [P, DC, T], F32R)
        h_hi = sb("h_hi", [P, DC, T], F32R)
        h_lo = sb("h_lo", [P, DC, T], F32R)
        par = sb("par", [P, NCOL])
        R = sb("R", [P, T])
        AR = 25600
        arena = sb("arena", [P, AR])

        def region(at, *shape):
            n = int(np.prod(shape))
            assert at + n <= AR, (at, shape)
            v = arena[:, at:at + n]
            if len(shape) == 2:
                v = v.rearrange("p (a b) -> p a b", a=shape[0])
            if len(shape) == 3:
                v = v.rearrange("p (a b c) -> p a b c", a=shape[0], b=shape[1])
            if len(shape) == 4:
                v = v.rearrange("p (a b c d) -> p a b c d", a=shape[0], b=shape[1], c=shape[2])
            return v

        def col(name, i=0, n=1):
            return par[:, COL[name] + i:COL[name] + i + n]

        ident = col("ident", 0, P)
        ones = col("ones", 0, P)

        X = region(0, DC, T)
        tab_c, tab_s = region(0, 4, NB), region(512, 4, NB)
        t1, t2 = region(1024, 4, NB), region(1536, 4, NB)
        g_re, g_im = region(2048, 4, NB), region(2560, 4, NB)
        st_re, st_im = region(3072, 4, NB), region(3584, 4, NB)
        win = region(4096, CT, STEP, 2, P)
        ca_re, ca_im = region(8192, STEP + 1, PAIRS, 32), region(10752, STEP + 1, PAIRS, 32)
        b_re, b_im = region(13312, PAIRS, 32), region(13824, PAIRS, 32)
        kloc = region(14336, CT, STEP, P)
        e0c, e0s = region(16384, PAIRS, E0), region(16640, PAIRS, E0)
        e1c, e1s = region(16896, PAIRS, E1), region(17024, PAIRS, E1)
        U = region(17152, CT, T)
        KV = region(19200, 2, T)
        gate1 = region(20224, DC, T)
        rho = region(24320, PAIRS)
        rot = region(24368, 4, PAIRS)
        zp = region(25088, T)
        d_are, d_aim, d_fre, d_fim = (region(20224 + SW * i, SW) for i in range(4))
        bt_re, bt_im = region(20224 + 4 * SW, CT, P), region(20736 + 4 * SW, CT, P)
        w_t1, w_t2 = region(21248 + 4 * SW, CT, P), region(25088, CT, P)
        s_w = [region(14336 + SW * i, SW) for i in range(3)] + [region(8704 + SW * i, SW) for i in range(3)] + \
              [region(11264 + SW * i, SW) for i in range(3)]
        Q = region(4096, 4, T)
        bias8 = region(6144, 8, 2 * P)
        logit1 = [region(8192, 4, 2 * P), region(9216, 4, 2 * P)]
        PT1 = region(10240, 2, T)
        VT1 = region(11264, 1, 4, P)
        mini = [region(24448 + 32 * i, 8, 4) for i in range(2)]
        gate2 = region(12288, DC, T)
        ssum = region(17152, T)
        sq = [region(17664, T), region(18176, T)]
        tmp = [region(24512, T), region(25024, T)]
        fbuf = [region(12288, T), region(12800, T)]
        Y = region(8192, DC, T)
        Fo = region(4096, DC, T)
        UC = region(4096, DC, T)
        Q2 = region(8192, DC, T)
        KV2 = region(12288, 4, T)
        VT2 = region(14336, 2, 4, P)
        G2 = region(20352, DC, T)
        HS = region(15360, DC, T)
        logit2 = [region(15360, 4, 3 * P), region(16896, 4, 3 * P)]
        PT2 = region(18432, 3, T)
        nd8 = region(19968, 3 * P)
        lru = [region(12288 + T * i, T) for i in range(6)]
        lru45 = region(12288 + 4 * T, 2 * T)
        spc = region(15360, 12, 16)
        decay_exp, decay_tanh = col("lam", 0, 16), col("iota", 0, 16)
        OUTB = region(4096, DC, T)

        gp = ctx.enter_context(nc.psum_tensor("gp", [P, 2, T], F32))
        mp = ctx.enter_context(nc.psum_tensor("mp", [P, 6, T], F32))

        s_par = sem("params_loaded")
        s_bc = sem("b_and_c_loaded")
        s_x = [sem(f"x_half{c}_loaded") for c in range(2)]
        s_raw = [sem(f"slab_loaded{i}") for i in range(RAW)]
        s_bias = sem("bias_loaded")
        s_x2 = sem("x_loaded_again")
        s_nd = sem("distances_loaded")
        w_hi_ready = sem("w_hi_ready")
        w_lo_ready = sem("w_lo_ready")
        half_done = sem("half_slab_done")
        out_read = sem("output_read")
        vec_step = sem("vec_step")
        act_step = sem("act_step")
        pool_step = sem("pool_step")
        a_hi_ready, a_lo_ready = sem("a_hi_ready"), sem("a_lo_ready")
        h_val, h_hi_ready, h_lo_ready = sem("h_value"), sem("h_hi_ready"), sem("h_lo_ready")
        x_new = sem("x_updated")
        m_val = sem("merged_value")
        sq_done, sq_added = sem("square_done"), sem("square_added")
        sq_summed = sem("square_summed")
        rms_sum, rms_root = sem("rms_sum"), sem("rms_root")
        disc_act, disc_vec = sem("discretise_act"), sem("discretise_vec")
        win_ready = sem("win_ready")
        ca_ready = sem("c_powers_ready")
        kloc_done, kloc_ready = sem("kloc_product"), sem("kloc_ready")
        v_done, v_read = sem("state_inputs"), sem("state_inputs_read")
        st_ready, y_done = sem("states_ready"), sem("ssm_output")
        y_val, z_val = sem("ssm_value"), sem("z_value")
        gate_val = sem("gate_value")
        vt_done, vt_ready = sem("v_transposed"), sem("v_ready")
        sc_done, lg_ready = sem("scores_done"), sem("logits_ready")
        nb_ready, ex_done = sem("maximum_ready"), sem("exponentials_done")
        pr_ready, pt_done, pt_ready = sem("probs_ready"), sem("probs_transposed"), sem("probs_t_ready")
        at_done = sem("attention_done")
        glu_sig = sem("glu_sigmoid")
        at_read = sem("attention_read")
        lg_done, lru_sig, lru_act, lru_mid, lru_free = (
            sem("lru_products"), sem("lru_sigmoids"), sem("lru_exp_tanh"), sem("lru_guarded"), sem("lru_free"))
        lru_root = sem("lru_root")
        spc_val, spc_exp, decay_ready = sem("lambda_magnitude"), sem("lambda_exp"), sem("decay_ready")
        s_out = sem("stored")

        block = ctx.enter_context(nc.Block())

        NORM = {"n1": 0, "post1": 1, "n2": 2, "post2": 3, "n3": 4, "n4": 5, "n5": 6}
        BY_PE = {"n1": 0, "n2": 1, "n3": 2}
        BY_VEC = {"post1": 0, "post2": 1, "n4": 2, "n5": 3}
        A_AT = {"n1": 0, "merged": 8, "n2": 16, "n3": 24, "n4": 32}
        H_AT = {"z": 0, "y1": 4, "z2": 12, "ff": 16, "uc": 48, "m2": 56, "ff2": 64}
        V_AT = {"ff": 0, "uc": 32, "m2": 40, "ff2": 48}
        X_AT = {"post1": 0, "post2": 8, "ff2": 16}
        G_AT = {"gate_a": 0, "gate_s": 8, "g2": 16, "mix": 24, "ff2": 40}
        MIX_VAL = {key: G_AT["mix"] + i + 1 for i, key in enumerate(MIX_GATE)}
        PART1 = 2 * FF1_PART + DC - FF1_PART
        PART2 = 2 * FF2_CHUNKS[0] + DC

        class Attention:

            def __init__(self, first, chunk0, pairs, back, forth, q, kt, k0, v0, vt, logit, pt, sinks, name):
                self.units = [(b, pp, p) for b in range(T // P) for pp in range(pairs) for p in range(2)]
                self.u0, self.q, self.kt, self.k0, self.v0, self.vt = first, q, kt, k0, v0, vt
                self.logit, self.pt, self.sinks, self.name, self.pairs = logit, pt, sinks, name, pairs
                self.chunks, self.done = [], []
                g = chunk0
                for b, _, _ in self.units:
                    js = [(j, b - back + j) for j in range(back + forth + 1) if 0 <= b - back + j < T // P]
                    self.chunks.append([(g + n, j, kb) for n, (j, kb) in enumerate(js)])
                    g += len(js)
                    self.done.append(g)
                self.width = (back + forth + 1) * P

            def span(self, u):
                return self.chunks[u][0][1] * P, (self.chunks[u][-1][1] + 1) * P

            def scores(self):
                return mp[:, 0:3, :].rearrange("p a b -> p (a b)")[:, 0:4 * self.width].rearrange(
                    "p (h k) -> p h k", h=4)

            def out_ap(self, view, u):
                b, pp, p = self.units[u]
                return view[HD * p:HD * p + HD, 4 * pp:4 * pp + 4, b * P:b * P + P]

        att1 = Attention(0, 0, 1, 1, 0, Q, KV, 0, 1, VT1, logit1, PT1, "sinks", "y1")
        att2 = Attention(len(att1.units), att1.done[-1], 2, 1, 1, Q2, KV2, 0, 2, VT2, logit2, PT2, "sinks2", "")

        class Tally:

            def __init__(self, eng, s):
                self.eng, self.s, self.n, self.i, self.per = eng, s, 0, 0, 0

            def up(self, ins):
                ins.then_inc(self.s, 1)
                self.n += 1

            def settle(self):
                self.eng.wait_ge(self.s, self.n + self.i * self.per)

            def run(self, ins):
                self.up(ins)
                self.settle()

        def loop(eng, count, body, tally=None, per=0, unroll=4):
            if count % unroll or count < 2 * unroll:
                for k in range(count):
                    body(0, k)
                return
            start = tally.n if tally else 0
            with eng.Fori(0, count // unroll) as i:
                if tally:
                    tally.i, tally.per = i, per * unroll
                for k in range(unroll):
                    body(i, k)
            if tally:
                assert tally.n - start == per * unroll, (tally.n - start, per)
                tally.n, tally.i, tally.per = start + per * count, 0, 0

        def at(view, e):
            if isinstance(e, int):
                return view[:, e, :]
            return view[:, bass.ds(e, 1), :].rearrange("p a b -> p (a b)")

        def pcol(name, e):
            if isinstance(e, int):
                return col(name, e)
            return par[:, bass.ds(COL[name] + e, 1)]

        @block.sync
        def _(sp):
            sp.dma_start(par[:, :], params).then_inc(s_par, 16)
            for dst, k in ((s_w[0], 0), (s_w[1], 1), (s_w[2], 2)):
                sp.dma_start(dst, s5p[:, k, :]).then_inc(s_par, 16)

            def load(n, k):
                sp.dma_start(raw[:, k % RAW, :], n).then_inc(s_raw[k % RAW], 16)

            sp.dma_start(X[:, 0:4, :], x_in[:, 0:4, :]).then_inc(s_x[0], 16)
            load(slabs[0], 0)
            sp.dma_start(X[:, 4:8, :], x_in[:, 4:8, :]).then_inc(s_x[1], 16)
            load(slabs[1], 1)
            with sp.Fori(0, (NSLAB - RAW) // RAW) as i:
                for k in range(RAW):
                    sp.wait_ge(w_lo_ready, i * RAW + (k + 1))
                    src = slabs[bass.ds(i * RAW + (k + RAW), 1), :, :].rearrange("a p n -> (a p) n")
                    load(src, k)
            for c in range(DC):
                sp.wait_ge(x_new, X_AT["ff2"] + c + 1)
                sp.dma_start(out[:, c, :], OUTB[:, c, :]).then_inc(s_out, 16)
            sp.wait_ge(s_out, 16 * DC)

        @block.gpsimd
        def _(pool):
            G = Tally(pool, pool_step)
            for dst, src in ((b_re, s5b[:, 0]), (b_im, s5b[:, 1]), (ca_re[:, 0], s5c[:, 0]), (ca_im[:, 0], s5c[:, 1]),
                             (bt_re, s5bt[:, 0]), (bt_im, s5bt[:, 1])):
                pool.dma_start(dst, src).then_inc(s_bc, 16)
            pool.wait_ge(s_bc, 96)
            pool.wait_ge(disc_vec, 2)

            def wide(v):
                return v[:, PAIRS:SW].rearrange("p (a b) -> p a b", a=CT)

            def product(o_re, o_im, a_re, a_im, c_re, c_im, last=None):
                G.up(pool.tensor_tensor(w_t1, a_re, c_re, ALU.mult))
                G.run(pool.tensor_tensor(w_t2, a_im, c_im, ALU.mult))
                G.run(pool.tensor_tensor(o_re, w_t1, w_t2, ALU.subtract))
                G.up(pool.tensor_tensor(w_t1, a_re, c_im, ALU.mult))
                G.run(pool.tensor_tensor(w_t2, a_im, c_re, ALU.mult))
                ins = pool.tensor_tensor(o_im, w_t1, w_t2, ALU.add)
                if last:
                    ins.then_inc(last, 1)
                else:
                    G.run(ins)

            def w(s, part):
                return win[:, :, s, part, :]

            product(w(STEP - 1, 0), w(STEP - 1, 1), wide(d_fre), wide(d_fim), bt_re, bt_im)
            for s in range(STEP - 2, -1, -1):
                product(w(s, 0), w(s, 1), wide(d_are), wide(d_aim), w(s + 1, 0), w(s + 1, 1),
                        win_ready if s == 0 else None)
            pool.wait_ge(v_done, CT)
            pool.dma_start(bias8, bias1).then_inc(s_bias, 16)
            pool.wait_ge(y_done, CT)
            pool.dma_start(X, x_in).then_inc(s_x2, 16)
            pool.wait_ge(x_new, DC)
            pool.dma_start(nd8, nd2).then_inc(s_nd, 16)

        @block.scalar
        def _(act):
            S = Tally(act, act_step)

            def split(base, i, k, per=4):
                n = base + k
                if isinstance(i, int) and n >= NSLAB:
                    return
                act.wait_ge(s_raw[n % RAW], 16 * (n // RAW + 1) + 16 // RAW * per * i)
                if n >= RING:
                    act.wait_ge(half_done, 2 * (n - RING + 1) + 2 * per * i)
                nc.scalar.activation(w_hi[:, n % RING, :], raw[:, n % RAW, :], ACT.Copy).then_inc(w_hi_ready, 1)

            def square(kind, c, i, src, static):
                if kind in BY_PE:
                    if c >= 2:
                        act.wait_ge(sq_summed, 8 * BY_PE[kind] + c - 1)
                elif 8 * BY_VEC[kind] + c >= 2:
                    act.wait_ge(sq_added, 8 * BY_VEC[kind] + c - 1 + 4 * i)
                dst = sq[static % 2]
                nc.scalar.activation(dst, src, ACT.Square).then_inc(sq_done, 1)

            def root(kind):
                if kind in BY_PE:
                    act.wait_ge(sq_summed, 8 * BY_PE[kind] + 8)
                else:
                    act.wait_ge(rms_sum, BY_VEC[kind] + 1)
                nc.scalar.activation(R[:, :], mp[:, 5, :], ACT.Sqrt, bias=col("eps"), scale=1.0 / D).then_inc(rms_root, 1)

            def normalised(kind, gain, wait):
                for c in range(DC):
                    wait(c)
                    nc.scalar.activation(a_hi[:, c, :], X[:, c, :], ACT.Copy, scale=col(gain, c)).then_inc(a_hi_ready, 1)
                    square(kind, c, 0, X[:, c, :], c)

            act.wait_ge(s_par, 64)
            nc.scalar.activation(s_w[2], s_w[2], ACT.Exp).then_inc(disc_act, 1)
            split(0, 0, 0)
            act.wait_ge(disc_vec, 1)
            nc.scalar.activation(s_w[6], s_w[3], ACT.Exp).then_inc(disc_act, 1)
            nc.scalar.activation(s_w[7], s_w[4], ACT.Sin).then_inc(disc_act, 1)
            nc.scalar.activation(s_w[8], s_w[4], ACT.Sin, scale=0.5).then_inc(disc_act, 1)
            split(1, 0, 0)
            normalised("n1", "g_mix_pre", lambda c: act.wait_ge(s_x[c // 4], 16))
            root("n1")

            def z_chunk(ct):
                act.wait_ge(y_val, ct + 1)
                nc.scalar.activation(U[:, ct, :], zp, ACT.Gelu_apprx_tanh).then_inc(z_val, 1)
                act.wait_ge(z_val, ct + 1)
                nc.scalar.activation(h_hi[:, 4 + ct, :], U[:, ct, :], ACT.Copy).then_inc(h_hi_ready, 1)

            for n in range(SLAB["u"], SLAB["gate_s"]):
                split(n + AHEAD, 0, 0)
                if SLAB["gate_a"] <= n < SLAB["gate_a"] + 8:
                    m = n - SLAB["gate_a"]
                    act.wait_ge(out_read, OUT["gate_a"] + m + 1)
                    nc.scalar.activation(gate1[:, m, :], gate1[:, m, :], ACT.Sigmoid).then_inc(gate_val, 1)
                if n == 1:
                    act.wait_ge(disc_vec, 3)
                    nc.scalar.activation(e0c, e0s, ACT.Sin, scale=TURN / 2).then_inc(disc_act, 1)
                    nc.scalar.activation(e1c, e1s, ACT.Sin, scale=TURN / 2).then_inc(disc_act, 1)
                    S.up(nc.scalar.activation(e0s, e0s, ACT.Sin, scale=TURN))
                    nc.scalar.activation(e1s, e1s, ACT.Sin, scale=TURN).then_inc(disc_act, 1)
                for ct in range(CT - 1):
                    if n == 3 * ct + 11:
                        z_chunk(ct)
            z_chunk(CT - 1)

            def attention(A, slab0, gate):
                for pp in range(A.pairs):
                    act.wait_ge(vt_done, pp + 1 + (A.u0 > 0))
                    nc.scalar.activation(A.vt[:, pp, :, :].rearrange("p a b -> p (a b)"), mp[:, 3 + pp, :],
                                         ACT.Copy).then_inc(vt_ready, 1)

                def exponentials(u):
                    row = mini[u % 2]
                    lo, hi = A.span(u)
                    act.wait_ge(nb_ready, A.u0 + u + 1)
                    nc.scalar.activation(row[:, 3, :], row[:, 2, :], ACT.Exp)
                    for h in range(4):
                        L = A.logit[u % 2][:, h, lo:hi]
                        ins = nc.scalar.activation(L, L, ACT.Exp, bias=row[:, 1, h:h + 1], scale=0.125,
                                                   accum_out=row[:, 4, h:h + 1])
                    ins.then_inc(ex_done, 1)

                n = len(A.units)
                exponentials(0)
                exponentials(1)
                for u in range(n):
                    for g, j, _ in A.chunks[u]:
                        if u:
                            act.wait_ge(at_done, A.u0 + u)
                        act.wait_ge(pt_done, g + 1)
                        nc.scalar.activation(A.pt[:, j, :], mp[:, 3 + g % 2, :], ACT.Copy).then_inc(pt_ready, 1)
                    if A.name and u:
                        attention_hi(A, u - 1)
                    split(slab0 + u + AHEAD, 0, 0)
                    if u + 2 < n:
                        exponentials(u + 2)
                    gate(u)
                if A.name:
                    attention_hi(A, n - 1)

            def attention_hi(A, u):
                p = A.units[u][2]
                act.wait_ge(at_done, A.u0 + u + 1)
                nc.scalar.activation(A.out_ap(h_hi, u), mp[HD * p:HD * p + HD, 5, :].rearrange("p (h q) -> p h q", h=4),
                                     ACT.Copy).then_inc(h_hi_ready, 1)

            def gate_s(u):
                act.wait_ge(out_read, OUT["gate_s"] + u + 1)
                nc.scalar.activation(gate2[:, u, :], gate2[:, u, :], ACT.Sigmoid).then_inc(gate_val, 1)

            attention(att1, SLAB["gate_s"], gate_s)

            loop(act, COUNT["branch_a"], lambda i, k: split(SLAB["branch_a"] + AHEAD, i, k))

            for j in range(COUNT["glu"]):
                split(SLAB["glu"] + AHEAD, 0, j)
                for m in (2 * j, 2 * j + 1):
                    act.wait_ge(half_done, 2 * SLAB["glu"] + m + 1)
                    if m >= 2:
                        act.wait_ge(out_read, OUT["glu"] + m - 1)
                    nc.scalar.activation(tmp[m % 2], gp[:, (OUT["glu"] + m) % 2, :], ACT.Sigmoid).then_inc(glu_sig, 1)
                    act.wait_ge(out_read, OUT["glu"] + m + 1)
                    nc.scalar.activation(h_hi[:, m, :], U[:, m, :], ACT.Copy).then_inc(h_hi_ready, 1)
            for j in range(COUNT["branch_s"]):
                split(SLAB["branch_s"] + AHEAD, 0, j)
                for m in (2 * j, 2 * j + 1):
                    act.wait_ge(m_val, m + 1)
                    nc.scalar.activation(a_hi[:, m, :], gate1[:, m, :], ACT.Copy).then_inc(a_hi_ready, 1)

            def out_body(i, k):
                split(SLAB["out"] + AHEAD, i, k)
                act.wait_ge(half_done, 2 * (SLAB["out"] + k + 1) + 8 * i)
                square("post1", k, i, gp[:, (OUT["out"] + k) % 2, :], k)
            loop(act, 8, out_body, unroll=8)
            root("post1")
            normalised("n2", "g_mlp_pre", lambda c: act.wait_ge(x_new, X_AT["post1"] + c + 1))
            root("n2")

            def ff1_part(p, part, last=False):
                n0 = SLAB["ff"] + PART1 * part
                for k in range(FF1_PART):
                    split(n0 + AHEAD, p, k, PART1)
                    act.wait_ge(h_val, V_AT["ff"] + FF1_PART * part + k + 1 + FF1_PART * p)
                    nc.scalar.activation(h_hi[:, k, :], fbuf[k % 2], ACT.Copy).then_inc(h_hi_ready, 1)
                for m in range(DC):
                    split(n0 + AHEAD, p, FF1_PART + m, PART1)
                    if last:
                        act.wait_ge(out_read, OUT["ff"] + PART1 * part + FF1_PART + m + 1)
                        square("post2", m, 0, Fo[:, m, :], m)

            ff1_part(0, 0)
            with act.Fori(0, FF1_PARTS - 2) as p:
                ff1_part(p, 1)
            ff1_part(0, FF1_PARTS - 1, last=True)
            root("post2")
            act.wait_ge(spc_val, 1)
            nc.scalar.activation(spc[:, 2, :], spc[:, 1, :], ACT.Exp).then_inc(spc_exp, 1)
            normalised("n3", "g_mix2", lambda c: act.wait_ge(x_new, X_AT["post2"] + c + 1))
            root("n3")

            for name in ("q2", "k2", "v2"):
                loop(act, COUNT[name], lambda i, k: split(SLAB[name] + AHEAD, i, k))

            def inputs2(u):
                if u < DC:
                    act.wait_ge(h_val, V_AT["uc"] + u + 1)
                    nc.scalar.activation(h_hi[:, u, :], UC[:, u, :], ACT.Copy).then_inc(h_hi_ready, 1)
                else:
                    m = u - DC
                    act.wait_ge(out_read, OUT["g2"] + m + 1)
                    nc.scalar.activation(G2[:, m, :], G2[:, m, :], ACT.Gelu_apprx_tanh).then_inc(gate_val, 1)
            attention(att2, SLAB["u2"], inputs2)

            act.wait_ge(decay_ready, 1)

            def mix_gate(kind, t):
                row, bias = {"za": (1, 0), "zb": (0, 8)}[kind]
                act.wait_ge(out_read, MIX_OUT[kind, t] + 1)
                nc.scalar.activation(tmp[row], tmp[row], ACT.Sigmoid, bias=col("b_gate", bias + t)).then_inc(gate_val, 1)

            def merged_hi(t):
                act.wait_ge(h_val, V_AT["m2"] + t + 1)
                nc.scalar.activation(h_hi[:, t, :], Q2[:, t, :], ACT.Copy).then_inc(h_hi_ready, 1)

            for t in range(DC):
                j = t // 2
                if t % 2 == 0:
                    split(MIX_SLAB["lru", j] + AHEAD, 0, 0)
                if t >= 1:
                    mix_gate("zb", t - 1)
                if t >= 2:
                    mix_gate("za", t - 2)
                if t:
                    act.wait_ge(lru_free, t)
                for q, (row, name, d) in enumerate(((0, "ba", 0), (1, "bx", 0), (2, "ba", 1), (3, "bx", 1))):
                    o = 4 * t + q
                    if o % 8 < 7:
                        act.wait_ge(lg_done, 7 * j + o % 8 + 1)
                    else:
                        act.wait_ge(half_done, 2 * (MIX_SLAB["lru", j] + 1))
                    nc.scalar.activation(lru[row], mp[:, o % 6, :], ACT.Sigmoid,
                                         bias=col(name, 8 * d + t)).then_inc(lru_sig, 1)
                act.wait_ge(lru_sig, 4 * t + 4)
                for d in range(2):
                    S.up(nc.scalar.activation(lru[4 + d], lru[2 * d], ACT.Tanh, scale=decay_tanh[:, 8 * d + t:8 * d + t + 1]))
                for d in range(2):
                    ins = nc.scalar.activation(lru[2 * d], lru[2 * d], ACT.Exp, scale=decay_exp[:, 8 * d + t:8 * d + t + 1])
                ins.then_inc(lru_act, 1)
                split(MIX_SLAB["zb", t] + AHEAD, 0, 0)
                act.wait_ge(lru_mid, t + 1)
                nc.scalar.activation(lru45, lru45, ACT.Sqrt).then_inc(lru_root, 1)
                if t >= 2:
                    merged_hi(t - 2)
                if t:
                    split(MIX_SLAB["za", t - 1] + AHEAD, 0, 0)
            mix_gate("zb", DC - 1)
            mix_gate("za", DC - 2)
            merged_hi(DC - 2)
            split(MIX_SLAB["za", DC - 1] + AHEAD, 0, 0)
            mix_gate("za", DC - 1)
            merged_hi(DC - 1)

            def out2_body(i, k):
                split(SLAB["out2"] + AHEAD, i, k)
                act.wait_ge(out_read, OUT["out2"] + k + 1 + 4 * i)
                xc = at(X, k + 4 * i)
                nc.scalar.activation(at(a_hi, k + 4 * i), xc, ACT.Copy, scale=pcol("g_ffn2", k + 4 * i)).then_inc(a_hi_ready, 1)
                square("n4", k, i, xc, k)
            loop(act, 8, out2_body, unroll=8)
            root("n4")

            def ff2_part(p, chunks, slab0):
                for c in range(chunks):
                    split(slab0 + AHEAD, p, 2 * c, PART2)
                    act.wait_ge(out_read, OUT["ff2"] + slab0 - SLAB["ff2"] + 2 * c + 1 + PART2 * p)
                    nc.scalar.activation(tmp[0], tmp[0], ACT.Silu).then_inc(gate_val, 1)
                    split(slab0 + AHEAD, p, 2 * c + 1, PART2)
                    v0 = 8 * ((slab0 - SLAB["ff2"]) // PART2)
                    act.wait_ge(h_val, V_AT["ff2"] + v0 + c + 1 + 8 * p)
                    nc.scalar.activation(h_hi[:, c, :], fbuf[c % 2], ACT.Copy).then_inc(h_hi_ready, 1)
                for m in range(DC):
                    split(slab0 + AHEAD, p, 2 * chunks + m, PART2)
                    if chunks != FF2_CHUNKS[0]:
                        act.wait_ge(out_read, OUT["ff2"] + slab0 - SLAB["ff2"] + 2 * chunks + m + 1)
                        square("n5", m, 0, X[:, m, :], m)

            with act.Fori(0, 2) as p:
                ff2_part(p, FF2_CHUNKS[0], SLAB["ff2"])
            ff2_part(0, FF2_CHUNKS[2], SLAB["ff2"] + 2 * PART2)
            root("n5")

        @block.vector
        def _(dve):
            V = Tally(dve, vec_step)
            TT, TS, STT = dve.tensor_tensor, dve.tensor_scalar, dve.scalar_tensor_tensor

            def split(base, i, k, per=4):
                n = base + k
                if isinstance(i, int) and n >= NSLAB:
                    return
                dve.wait_ge(w_hi_ready, n + 1 + per * i)
                TT(w_lo[:, n % RING, :], raw[:, n % RAW, :], w_hi[:, n % RING, :].bitcast(F32),
                   ALU.subtract).then_inc(w_lo_ready, 1)

            def take(name, i, k, half=None, per=4):
                at_half = 2 * (SLAB[name] + k + 1) if half is None else 2 * SLAB[name] + half
                dve.wait_ge(half_done, at_half + 2 * per * i)
                return gp[:, (OUT[name] + k) % 2, :]

            def clear_sum():
                V.run(dve.memset(ssum, 0.0))

            def add_square(kind, c, i=0):
                dve.wait_ge(sq_done, 8 * NORM[kind] + c + 1 + 4 * i)
                if not isinstance(i, int) or 8 * BY_VEC[kind] + c:
                    dve.wait_ge(sq_added, max(8 * BY_VEC[kind] + c, 0) + 4 * i)
                TT(ssum, ssum, sq[c % 2], ALU.add).then_inc(sq_added, 1)

            def invert_root(kind):
                dve.wait_ge(rms_root, NORM[kind] + 1)
                V.run(dve.reciprocal(R[:, :], R[:, :]))

            def a_low(name, c, i, src, gain=None):
                dve.wait_ge(a_hi_ready, A_AT[name] + c + 1 + 4 * i)
                hi = at(a_hi, c + 4 * i).bitcast(F32)
                lo = at(a_lo, c + 4 * i)
                if gain is None:
                    TT(lo, src, hi, ALU.subtract).then_inc(a_lo_ready, 1)
                else:
                    STT(out=lo, in0=src, scalar=gain, in1=hi, op0=ALU.mult, op1=ALU.subtract).then_inc(a_lo_ready, 1)

            def h_low(count, chunk, src):
                dve.wait_ge(h_hi_ready, count + 1)
                TT(at(h_lo, chunk), src, at(h_hi, chunk).bitcast(F32), ALU.subtract).then_inc(h_lo_ready, 1)

            def normalised(kind, gain):
                for c in range(DC):
                    a_low(kind, c, 0, X[:, c, :], col(gain, c))

            def as_steps(v):
                return v.rearrange("p (b s) -> p s b", s=STEP)

            def in_steps(v):
                return v.rearrange("p (s b) -> p s b", s=STEP)

            lr, li, dt, ld, ang, tmp5, mag, sn, cs = s_w
            dve.wait_ge(s_par, 64)
            dve.wait_ge(disc_act, 1)
            V.up(TT(ld, lr, dt, ALU.mult))
            V.run(TT(ang, li, dt, ALU.mult))
            V.run(TS(tmp5, ang, 1.0 / TWO_PI, MAGIC, ALU.mult, ALU.add))
            V.run(TS(tmp5, tmp5, -MAGIC, None, ALU.add))
            V.run(STT(out=ang, in0=tmp5, scalar=-C1, in1=ang, op0=ALU.mult, op1=ALU.add))
            V.run(STT(out=ang, in0=tmp5, scalar=-C2, in1=ang, op0=ALU.mult, op1=ALU.add))
            STT(out=ang, in0=tmp5, scalar=-C3, in1=ang, op0=ALU.mult, op1=ALU.add).then_inc(disc_vec, 1)
            split(0, 0, 0)
            split(0, 0, 1)
            normalised("n1", "g_mix_pre")
            dve.wait_ge(disc_act, 4)
            V.up(TT(rho, mag[:, 0:PAIRS], mag[:, 0:PAIRS], ALU.mult))
            V.run(TT(cs, cs, cs, ALU.mult))
            V.up(TT(rho, rho, rho, ALU.mult))
            V.run(TS(cs, cs, -2.0, 1.0, ALU.mult, ALU.add))
            V.up(TT(d_are, mag, cs, ALU.mult))
            V.run(TT(d_aim, mag, sn, ALU.mult))
            V.up(TT(mag, lr, lr, ALU.mult))
            V.run(TT(cs, li, li, ALU.mult))
            V.up(TS(dt, d_are, -1.0, None, ALU.add))
            V.run(TT(mag, mag, cs, ALU.add))
            V.run(dve.reciprocal(mag, mag))
            for m in range(2):
                split(AHEAD, 0, m)
                dve.tensor_copy(in_steps(U[:, m, :]), as_steps(take("u", 0, m))).then_inc(out_read, 1)
            V.up(TT(tmp5, dt, lr, ALU.mult))
            V.run(TT(cs, d_aim, li, ALU.mult))
            V.up(TT(sn, d_aim, lr, ALU.mult))
            V.run(TT(tmp5, tmp5, cs, ALU.add))
            V.up(TT(d_fre, tmp5, mag, ALU.mult))
            V.run(TT(cs, dt, li, ALU.mult))
            V.run(TT(sn, sn, cs, ALU.subtract))
            TT(d_fim, sn, mag, ALU.mult).then_inc(disc_vec, 1)

            s4 = [region(14336 + 512 * i, PAIRS, 32) for i in range(4)]

            def wave():
                dve.wait_ge(disc_vec, 2)
                V.run(TS(rot[:, 1, :], ang[:, 0:PAIRS], STEP / TWO_PI, None, ALU.mult))
                V.run(TS(rot[:, 2, :], rot[:, 1, :], MAGIC, -MAGIC, ALU.add, ALU.add))
                V.run(TT(rot[:, 1, :], rot[:, 1, :], rot[:, 2, :], ALU.subtract))
                V.run(TS(rot[:, 3, :], rot[:, 1, :], float(E0), None, ALU.mult))
                V.run(TS(rot[:, 2, :], rot[:, 3, :], MAGIC, -MAGIC, ALU.add, ALU.add))
                V.run(TT(rot[:, 3, :], rot[:, 3, :], rot[:, 2, :], ALU.subtract))
                for row, half, turns, n in ((e0s, e0c, 1, E0), (e1s, e1c, 3, E1)):
                    V.run(TT(row, rot[:, turns, :].unsqueeze(2).to_broadcast([P, PAIRS, n]),
                             col("iota", 0, n).unsqueeze(1).to_broadcast([P, PAIRS, n]), ALU.mult))
                    V.run(TS(half, row, MAGIC, -MAGIC, ALU.add, ALU.add))
                    ins = TT(row, row, half, ALU.subtract)
                    if n == E0:
                        V.run(ins)
                    else:
                        ins.then_inc(disc_vec, 1)

            def scale_b():
                dve.wait_ge(disc_act, 7)
                for half in (e0c, e1c):
                    V.run(TT(half, half, half, ALU.mult))
                    V.run(TS(half, half, -2.0, 1.0, ALU.mult, ALU.add))
                dve.wait_ge(s_bc, 96)
                fr = d_fre[:, 0:PAIRS].unsqueeze(2).to_broadcast([P, PAIRS, 32])
                fi = d_fim[:, 0:PAIRS].unsqueeze(2).to_broadcast([P, PAIRS, 32])
                V.up(TT(s4[0], fr, b_re, ALU.mult))
                V.up(TT(s4[1], fi, b_im, ALU.mult))
                V.up(TT(s4[2], fr, b_im, ALU.mult))
                V.run(TT(s4[3], fi, b_re, ALU.mult))
                V.up(TT(b_re, s4[0], s4[1], ALU.subtract))
                V.run(TT(b_im, s4[2], s4[3], ALU.add))
                V.run(TS(ca_im[:, 0], ca_im[:, 0], -1.0, None, ALU.mult))

            def c_power(k):
                ar = d_are[:, 0:PAIRS].unsqueeze(2).to_broadcast([P, PAIRS, 32])
                ai = d_aim[:, 0:PAIRS].unsqueeze(2).to_broadcast([P, PAIRS, 32])
                V.up(TT(s4[0], ca_re[:, k - 1], ar, ALU.mult))
                V.up(TT(s4[1], ca_im[:, k - 1], ai, ALU.mult))
                V.up(TT(s4[2], ca_im[:, k - 1], ar, ALU.mult))
                V.run(TT(s4[3], ca_re[:, k - 1], ai, ALU.mult))
                V.up(TT(ca_re[:, k], s4[0], s4[1], ALU.add))
                V.run(TT(ca_im[:, k], s4[2], s4[3], ALU.subtract))
                if k == STEP:
                    dve.memset(kloc, 0.0).then_inc(ca_ready, 1)

            def local_weights():
                dve.wait_ge(kloc_done, 1)
                dve.wait_ge(ca_ready, 1)
                for pr in range(4):
                    rows = slice(32 * pr, 32 * pr + 32)
                    ins = dve.tensor_copy(kloc[rows, :, :, rows],
                                          mp[rows, 4, :].rearrange("p (a b c) -> p a b c", a=CT, b=STEP))
                    if pr < 3:
                        V.up(ins)
                ins.then_inc(kloc_ready, 1)

            def table(ct):
                prs = slice(4 * ct, 4 * ct + 4)

                def fine(v):
                    return v[:, prs, :].unsqueeze(2).to_broadcast([P, 4, E1, E0])

                def coarse(v):
                    return v[:, prs, :].unsqueeze(3).to_broadcast([P, 4, E1, E0])

                def full(v):
                    return v.rearrange("p a (x y) -> p a x y", x=E1)
                if ct:
                    dve.wait_ge(st_ready, ct)
                V.up(TT(full(t1), coarse(e1c), fine(e0c), ALU.mult))
                V.run(TT(full(t2), coarse(e1s), fine(e0s), ALU.mult))
                V.run(TT(tab_c, t1, t2, ALU.subtract))
                V.up(TT(full(t1), coarse(e1s), fine(e0c), ALU.mult))
                V.run(TT(full(t2), coarse(e1c), fine(e0s), ALU.mult))
                V.run(TT(tab_s, t1, t2, ALU.add))

            def scan_states(ct):
                dve.wait_ge(v_done, ct + 1)
                v_re, v_im = mp[:, 0:4, 0:NB], mp[:, 0:4, NB:2 * NB]
                V.up(TT(t1, tab_c, v_re, ALU.mult))
                V.run(TT(t2, tab_s, v_im, ALU.mult))
                V.run(TT(g_re, t1, t2, ALU.add))
                V.up(TT(t1, tab_c, v_im, ALU.mult))
                TT(t2, tab_s, v_re, ALU.mult).then_inc(v_read, 1)
                dve.wait_ge(v_read, ct + 1)
                V.run(TT(g_im, t1, t2, ALU.subtract))
                for pr in range(4):
                    decay = rho[:, 4 * ct + pr:4 * ct + pr + 1].to_broadcast([P, NB])
                    V.up(dve.tensor_tensor_scan(g_re[:, pr, :], decay, g_re[:, pr, :], 0.0, ALU.mult, ALU.add))
                    V.up(dve.tensor_tensor_scan(g_im[:, pr, :], decay, g_im[:, pr, :], 0.0, ALU.mult, ALU.add))
                V.settle()

            def turn_states(ct):
                V.up(TT(t1, tab_c, g_re, ALU.mult))
                V.run(TT(t2, tab_s, g_im, ALU.mult))
                if ct:
                    dve.wait_ge(y_done, ct)
                V.run(TT(st_re, t1, t2, ALU.subtract))
                V.up(TT(t1, tab_c, g_im, ALU.mult))
                V.run(TT(t2, tab_s, g_re, ALU.mult))
                TT(st_im, t1, t2, ALU.add).then_inc(st_ready, 1)

            def ssm_out(ct):
                dve.wait_ge(y_done, ct + 1)
                STT(out=zp.rearrange("p (b s) -> p s b", s=STEP), in0=U[:, ct, :].rearrange("p (s b) -> p s b", s=STEP),
                    scalar=col("d_skip", ct), in1=mp[:, 5, :].rearrange("p (s b) -> p s b", s=STEP),
                    op0=ALU.mult, op1=ALU.add).then_inc(y_val, 1)

            def z_low(ct):
                h_low(H_AT["z"] + ct, 4 + ct, U[:, ct, :])

            after = {n: [] for n in range(SLAB["gate_s"])}
            after[2].append(scale_b)
            for k in range(1, STEP + 1):
                after[1 + k].append(lambda k=k: c_power(k))
            after[8].append(local_weights)
            for ct in range(CT):
                after[3 * ct + 6].append(lambda ct=ct: table(ct))
                after[3 * ct + 7].append(lambda ct=ct: scan_states(ct))
                after[3 * ct + 8].append(lambda ct=ct: turn_states(ct))
                if ct < CT - 1:
                    after[3 * ct + 11].insert(0, lambda ct=ct: ssm_out(ct))
                    after[min(3 * ct + 12, 17)].insert(len(after[17]) if ct == 2 else 0, lambda ct=ct: z_low(ct))
            invert_root("n1")
            dve.wait_ge(out_read, 2)
            for m in range(2):
                V.up(TT(in_steps(U[:, m, :]), in_steps(U[:, m, :]), as_steps(R[:, :]), ALU.mult))
            V.settle()
            wave()
            for name in ("u", "k", "v", "gate_a", "q"):
                for m in range(2 if name == "u" else 0, COUNT[name]):
                    split(SLAB[name] + AHEAD, 0, m)
                    src, r = take(name, 0, m), R[:, :]
                    if name == "u":
                        dst, src, r = in_steps(U[:, m, :]), as_steps(src), as_steps(r)
                    else:
                        dst = {"k": KV[:, 0, :], "v": KV[:, 1, :], "gate_a": gate1[:, m, :], "q": Q[:, min(m, 3), :]}[name]
                    if name == "gate_a" and m == 0:
                        dve.wait_ge(win_ready, 1)
                    if name == "q" and m == 0:
                        dve.wait_ge(v_done, CT // 2)
                    TT(dst, src, r, ALU.mult).then_inc(out_read, 1)
                    for piece in after[SLAB[name] + m]:
                        piece()
            ssm_out(CT - 1)
            z_low(CT - 1)

            def attention(A, between):
                def logits(u):
                    row, L = mini[u % 2], A.logit[u % 2]
                    b, pp, p = A.units[u]
                    lo, hi = A.span(u)
                    kv = 2 * pp + p
                    dve.wait_ge(sc_done, A.u0 + u + 1)
                    if u >= 2:
                        dve.wait_ge(pt_done, A.done[u - 2])
                    sc = A.scores()
                    if A.name:
                        TT(L[:, :, lo:hi], sc[:, :, lo:hi], bias8[:, 4 * kv:4 * kv + 4, lo:hi], ALU.add).then_inc(lg_ready, 1)
                    else:
                        for h in range(4):
                            slope = 8.0 * 2.0 ** (-8.0 * (4 * kv + h + 1) / 16)
                            ins = STT(out=L[:, h, lo:hi], in0=nd8[:, lo:hi], scalar=slope, in1=sc[:, h, lo:hi],
                                      op0=ALU.mult, op1=ALU.add)
                            if h < 3:
                                V.up(ins)
                        ins.then_inc(lg_ready, 1)
                    dve.wait_ge(lg_ready, A.u0 + u + 1)
                    sink = col(A.sinks, 4 * kv, 4)
                    V.run(dve.tensor_reduce(row[:, 0, :], L[:, :, lo:hi], AX.X, ALU.max))
                    V.run(STT(out=row[:, 0, :], in0=sink, scalar=8.0, in1=row[:, 0, :], op0=ALU.mult, op1=ALU.max))
                    V.run(TS(row[:, 1, :], row[:, 0, :], -0.125, None, ALU.mult))
                    TT(row[:, 2, :], sink, row[:, 1, :], ALU.add).then_inc(nb_ready, 1)

                def probabilities(u):
                    row, L = mini[u % 2], A.logit[u % 2]
                    lo, hi = A.span(u)
                    dve.wait_ge(ex_done, A.u0 + u + 1)
                    V.run(TT(row[:, 5, :], row[:, 3, :], row[:, 4, :], ALU.add))
                    V.run(dve.reciprocal(row[:, 5, :], row[:, 5, :]))
                    TT(L[:, :, lo:hi], L[:, :, lo:hi], row[:, 5, :].unsqueeze(2).to_broadcast([P, 4, hi - lo]),
                       ALU.mult).then_inc(pr_ready, 1)

                def outputs(u):
                    p = A.units[u][2]
                    o = mp[HD * p:HD * p + HD, 5, :].rearrange("p (h q) -> p h q", h=4)
                    dve.wait_ge(at_done, A.u0 + u + 1)
                    if A.name:
                        dve.wait_ge(h_hi_ready, H_AT["y1"] + u + 1)
                        TT(A.out_ap(h_lo, u), o, A.out_ap(h_hi, u).bitcast(F32), ALU.subtract).then_inc(h_lo_ready, 1)
                    else:
                        dve.tensor_copy(A.out_ap(Q2, u), o).then_inc(at_read, 1)

                n = len(A.units)
                logits(0)
                logits(1)
                probabilities(0)
                for u in range(n):
                    if u + 1 < n:
                        probabilities(u + 1)
                    if u:
                        outputs(u - 1)
                    if u + 2 < n:
                        logits(u + 2)
                    between(u)
                outputs(n - 1)

            def evacuate(name, m, dst):
                split(SLAB[name] + AHEAD, 0, m)
                TT(dst, take(name, 0, m), R[:, :], ALU.mult).then_inc(out_read, 1)

            dve.wait_ge(s_bias, 16)
            bflat = bias8.rearrange("p a b -> p (a b)")
            V.run(TS(bflat, bflat, 8.0, None, ALU.mult))
            attention(att1, lambda u: evacuate("gate_s", u, gate2[:, u, :]))

            for j in range(COUNT["branch_a"]):
                split(SLAB["branch_a"] + AHEAD, 0, j)
                for m in (2 * j, 2 * j + 1):
                    src = take("branch_a", 0, m, half=m + 1)
                    dve.wait_ge(gate_val, G_AT["gate_a"] + m + 1)
                    TT(gate1[:, m, :], src, gate1[:, m, :], ALU.mult).then_inc(out_read, 1)

            for j in range(COUNT["glu"]):
                split(SLAB["glu"] + AHEAD, 0, j)
                for m in (2 * j, 2 * j + 1):
                    dve.wait_ge(glu_sig, m + 1)
                    TT(U[:, m, :], U[:, m, :], tmp[m % 2], ALU.mult).then_inc(out_read, 1)
                    h_low(H_AT["z2"] + m, m, U[:, m, :])
            for j in range(COUNT["branch_s"]):
                split(SLAB["branch_s"] + AHEAD, 0, j)
                for m in (2 * j, 2 * j + 1):
                    src = take("branch_s", 0, m, half=m + 1)
                    dve.wait_ge(gate_val, G_AT["gate_s"] + m + 1)
                    TT(tmp[m % 2], src, gate2[:, m, :], ALU.mult).then_inc(out_read, 1)
                    dve.wait_ge(out_read, OUT["branch_s"] + m + 1)
                    TT(gate1[:, m, :], gate1[:, m, :], tmp[m % 2], ALU.add).then_inc(m_val, 1)
                    a_low("merged", m, 0, gate1[:, m, :])

            clear_sum()

            def out_body(i, k):
                split(SLAB["out"] + AHEAD, i, k)
                add_square("post1", k, i)
                TS(at(Y, k + 4 * i), take("out", i, k), pcol("g_mix_post", k + 4 * i), None,
                   ALU.mult).then_inc(out_read, 1)
            loop(dve, 8, out_body, unroll=8)
            invert_root("post1")
            dve.wait_ge(s_x2, 16)
            dve.wait_ge(out_read, OUT["out"] + DC)
            for c in range(DC + 1):
                if c < DC:
                    V.run(TT(tmp[c % 2], Y[:, c, :], R[:, :], ALU.mult))
                    TT(X[:, c, :], X[:, c, :], tmp[c % 2], ALU.add).then_inc(x_new, 1)
                if c:
                    a_low("n2", c - 1, 0, X[:, c - 1, :], col("g_mlp_pre", c - 1))
            V.run(dve.memset(Fo.rearrange("p a b -> p (a b)"), 0.0))

            def ff1_part(p, part, last=False):
                s0 = PART1 * part

                def relu_squared(k):
                    STT(out=fbuf[k % 2], in0=tmp[k % 2], scalar=0.0, in1=tmp[k % 2], op0=ALU.max,
                        op1=ALU.mult).then_inc(h_val, 1)

                def low(k):
                    h_low(H_AT["ff"] + FF1_PART * part + k + FF1_PART * p, k, fbuf[k % 2])

                for k in range(FF1_PART):
                    if part == 0 and k < 2:
                        split(SLAB["ff"] + AHEAD, p, k, PART1)
                        if k == 0:
                            for e in range(2):
                                dve.tensor_copy(tmp[e], take("ff", 0, e)).then_inc(out_read, 1)
                            invert_root("n2")
                            dve.wait_ge(out_read, OUT["ff"] + 2)
                        V.run(TT(tmp[k], tmp[k], R[:, :], ALU.mult))
                    else:
                        split(SLAB["ff"] + AHEAD, p, s0 + k, PART1)
                        TT(tmp[k % 2], take("ff", p, s0 + k, per=PART1), R[:, :], ALU.mult).then_inc(out_read, 1)
                        dve.wait_ge(out_read, OUT["ff"] + s0 + k + 1 + PART1 * p)
                    relu_squared(k)
                    if k:
                        low(k - 1)
                low(FF1_PART - 1)
                if last:
                    clear_sum()
                for m in range(DC):
                    split(SLAB["ff"] + AHEAD, p, s0 + FF1_PART + m, PART1)
                    src = take("ff", p, s0 + FF1_PART + m, per=PART1)
                    TT(Fo[:, m, :], Fo[:, m, :], src, ALU.add).then_inc(out_read, 1)
                    if last and m:
                        add_square("post2", m - 1)
                if last:
                    add_square("post2", DC - 1)

            ff1_part(0, 0)
            with dve.Fori(0, FF1_PARTS - 2) as p:
                ff1_part(p, 1)
            ff1_part(0, FF1_PARTS - 1, last=True)
            lam = col("lam", 0, 16)
            r = [spc[:, i, :] for i in range(12)]
            V.run(TS(r[0], lam, -1.0, None, ALU.mult))
            V.run(TT(r[1], r[0], lam, ALU.min))
            TS(r[0], r[0], 0.0, None, ALU.max).then_inc(spc_val, 1)
            invert_root("post2")
            dve.wait_ge(out_read, OUT["ff"] + PART1 * FF1_PARTS)
            for c in range(DC + 1):
                if c < DC:
                    V.run(STT(out=tmp[c % 2], in0=Fo[:, c, :], scalar=col("g_mlp_post", c), in1=R[:, :],
                              op0=ALU.mult, op1=ALU.mult))
                    TT(X[:, c, :], X[:, c, :], tmp[c % 2], ALU.add).then_inc(x_new, 1)
                if c:
                    a_low("n3", c - 1, 0, X[:, c - 1, :], col("g_mix2", c - 1))

            for m in range(2):
                split(SLAB["q2"] + AHEAD, 0, m)
                dve.tensor_copy(Q2[:, m, :], take("q2", 0, m)).then_inc(out_read, 1)
            invert_root("n3")
            dve.wait_ge(out_read, OUT["q2"] + 2)
            for m in range(2):
                V.up(TT(Q2[:, m, :], Q2[:, m, :], R[:, :], ALU.mult))
            for m in range(2, DC):
                evacuate("q2", m, Q2[:, m, :])
            for m in range(2):
                evacuate("k2", m, KV2[:, m, :])
            for m in range(2):
                evacuate("v2", m, KV2[:, 2 + m, :])
            dve.wait_ge(spc_exp, 1)
            V.run(TS(r[3], r[2], 2.0, None, ALU.add))
            V.run(dve.reciprocal(r[3], r[3]))
            V.run(TT(r[3], r[3], r[2], ALU.mult))
            V.run(TT(r[4], r[3], r[3], ALU.mult))
            V.run(TS(r[5], r[4], 1.0 / 17, None, ALU.mult))
            for d in (15, 13, 11, 9, 7, 5, 3):
                V.run(STT(out=r[5], in0=r[5], scalar=1.0 / d, in1=r[4], op0=ALU.add, op1=ALU.mult))
            V.run(STT(out=r[5], in0=r[5], scalar=1.0, in1=r[3], op0=ALU.add, op1=ALU.mult))
            V.run(STT(out=r[5], in0=r[5], scalar=2.0, in1=r[0], op0=ALU.mult, op1=ALU.add))
            V.up(TS(decay_exp, r[5], -8.0, None, ALU.mult))
            TS(decay_tanh, r[5], 4.0, None, ALU.mult).then_inc(decay_ready, 1)

            def inputs2(u):
                if u >= DC:
                    evacuate("g2", u - DC, G2[:, u - DC, :])
                    return
                x, y = tmp[u % 2], UC[:, u, :]
                evacuate("u2", u, x)
                dve.wait_ge(out_read, OUT["u2"] + u + 1)
                V.run(TS(y, x, pcol("conv_w", 16 + u), pcol("conv_b", u), ALU.mult, ALU.add))
                V.run(STT(out=y[:, 2:T], in0=x[:, 0:T - 2], scalar=pcol("conv_w", u), in1=y[:, 2:T],
                          op0=ALU.mult, op1=ALU.add))
                V.run(STT(out=y[:, 1:T], in0=x[:, 0:T - 1], scalar=pcol("conv_w", 8 + u), in1=y[:, 1:T],
                          op0=ALU.mult, op1=ALU.add))
                STT(out=y[:, 0:T - 1], in0=x[:, 1:T], scalar=pcol("conv_w", 24 + u), in1=y[:, 0:T - 1],
                    op0=ALU.mult, op1=ALU.add).then_inc(h_val, 1)
                h_low(H_AT["uc"] + u, u, y)

            dve.wait_ge(decay_ready, 1)
            dve.wait_ge(s_nd, 16)
            attention(att2, inputs2)
            dve.wait_ge(gate_val, G_AT["g2"] + DC)
            dve.wait_ge(at_read, len(att2.units))

            def gate_product(kind, t, row):
                split(MIX_SLAB[kind, t] + AHEAD, 0, 0)
                dve.wait_ge(half_done, 2 * (MIX_SLAB[kind, t] + 1))
                TT(row, gp[:, MIX_OUT[kind, t] % 2, :], R[:, :], ALU.mult).then_inc(out_read, 1)

            def gated_attention(t):
                dve.wait_ge(gate_val, MIX_VAL["zb", t])
                V.run(TT(Q2[:, t, :], Q2[:, t, :], tmp[0], ALU.mult))

            def merged(t):
                dve.wait_ge(gate_val, MIX_VAL["za", t])
                V.run(TT(HS[:, t, :], HS[:, t, :], tmp[1], ALU.mult))
                TT(Q2[:, t, :], Q2[:, t, :], HS[:, t, :], ALU.add).then_inc(h_val, 1)

            for t in range(DC):
                if t % 2 == 0:
                    split(MIX_SLAB["lru", t // 2] + AHEAD, 0, 0)
                if t >= 1:
                    gated_attention(t - 1)
                if t >= 2:
                    merged(t - 2)
                dve.wait_ge(lru_act, t + 1)
                TS(lru45, lru45, 0.0, None, ALU.max).then_inc(lru_mid, 1)
                for d in range(2):
                    V.up(TT(lru[1 + 2 * d], lru[1 + 2 * d], UC[:, t, :], ALU.mult))
                gate_product("zb", t, tmp[0])
                dve.wait_ge(lru_root, t + 1)
                for d in range(2):
                    V.up(STT(out=lru[4 + d], in0=lru[2 * d], scalar=1.0, in1=lru[4 + d], op0=ALU.add, op1=ALU.mult))
                V.settle()
                for d in range(2):
                    V.up(TT(lru[1 + 2 * d], lru[1 + 2 * d], lru[4 + d], ALU.mult))
                V.settle()
                V.up(dve.tensor_tensor_scan(HS[:, t, :], lru[0], lru[1], 0.0, ALU.mult, ALU.add))
                V.run(dve.tensor_tensor_scan(lru[5][:, ::-1], lru[2][:, ::-1], lru[3][:, ::-1], 0.0, ALU.mult, ALU.add))
                TT(HS[:, t, :], HS[:, t, :], lru[5], ALU.add).then_inc(lru_free, 1)
                dve.wait_ge(lru_free, t + 1)
                V.run(TT(HS[:, t, :], HS[:, t, :], G2[:, t, :], ALU.mult))
                if t >= 1:
                    gate_product("za", t - 1, tmp[1])
                if t >= 2:
                    h_low(H_AT["m2"] + t - 2, t - 2, Q2[:, t - 2, :])
            gated_attention(DC - 1)
            merged(DC - 2)
            gate_product("za", DC - 1, tmp[1])
            h_low(H_AT["m2"] + DC - 2, DC - 2, Q2[:, DC - 2, :])
            merged(DC - 1)
            h_low(H_AT["m2"] + DC - 1, DC - 1, Q2[:, DC - 1, :])

            clear_sum()

            def out2_body(i, k):
                split(SLAB["out2"] + AHEAD, i, k)
                xc = at(X, k + 4 * i)
                TT(xc, xc, take("out2", i, k), ALU.add).then_inc(out_read, 1)
                a_low("n4", k, i, xc, pcol("g_ffn2", k + 4 * i))
                add_square("n4", k, i)
            loop(dve, 8, out2_body)
            invert_root("n4")

            def ff2_part(p, chunks, slab0):
                s0 = slab0 - SLAB["ff2"]
                v0 = 8 * (s0 // PART2)
                for c in range(chunks):
                    for e in range(2):
                        split(slab0 + AHEAD, p, 2 * c + e, PART2)
                        TT(tmp[e], take("ff2", p, s0 + 2 * c + e, per=PART2), R[:, :], ALU.mult).then_inc(out_read, 1)
                    dve.wait_ge(out_read, OUT["ff2"] + s0 + 2 * c + 2 + PART2 * p)
                    dve.wait_ge(gate_val, G_AT["ff2"] + v0 + c + 1 + 8 * p)
                    TT(fbuf[c % 2], tmp[0], tmp[1], ALU.mult).then_inc(h_val, 1)
                    for q in ([c - 1] if c else []) + ([c] if c == chunks - 1 else []):
                        h_low(H_AT["ff2"] + v0 + q + 8 * p, q, fbuf[q % 2])
                for m in range(DC):
                    split(slab0 + AHEAD, p, 2 * chunks + m, PART2)
                    src = take("ff2", p, s0 + 2 * chunks + m, per=PART2)
                    TT(X[:, m, :], X[:, m, :], src, ALU.add).then_inc(out_read, 1)
                    if chunks != FF2_CHUNKS[0]:
                        add_square("n5", m)

            with dve.Fori(0, 2) as p:
                ff2_part(p, FF2_CHUNKS[0], SLAB["ff2"])
            clear_sum()
            ff2_part(0, FF2_CHUNKS[2], SLAB["ff2"] + 2 * PART2)
            invert_root("n5")
            for c in range(DC):
                STT(out=OUTB[:, c, :], in0=X[:, c, :], scalar=col("g_fin2", c), in1=R[:, :], op0=ALU.mult,
                    op1=ALU.mult).then_inc(x_new, 1)

        @block.tensor
        def _(pe):
            def gemm(base, i, k, tiles, outs, x_hi, x_lo, out0, ready=None, per=4):
                n = base + k
                pe.wait_ge(w_lo_ready, n + 1 + per * i)
                for e in range(outs):
                    o = out0 + outs * k + e
                    if o >= 2:
                        pe.wait_ge(out_read, o - 1 + outs * per * i)
                    bank = gp[:, o % 2, :]
                    for t in range(tiles):
                        if ready:
                            ready(t)
                        cols = slice((e * tiles + t) * P, (e * tiles + t + 1) * P)
                        hi, lo = w_hi[:, n % RING, cols], w_lo[:, n % RING, cols]
                        pe.matmul(bank, hi, x_hi(t), start=t == 0, stop=False)
                        pe.matmul(bank, hi, x_lo(t), start=False, stop=False)
                        ins = pe.matmul(bank, lo, x_hi(t), start=False, stop=t == tiles - 1)
                    ins.then_inc(half_done, 2 // outs)

            def a(t):
                return a_hi[:, t, :]

            def al(t):
                return a_lo[:, t, :]

            def h(t):
                return h_hi[:, t, :]

            def hl(t):
                return h_lo[:, t, :]

            def mean_square(kind):
                pe.wait_ge(sq_added, 8 * BY_VEC[kind] + 8)
                pe.matmul(mp[:, 5, :], ones, ssum, start=True, stop=True).then_inc(rms_sum, 1)

            def a_stage(name, i, k, ready=None):
                gemm(SLAB[name], i, k, 8, 1, a, al, OUT[name], ready)

            def start_stage(name, kind):
                banks = []
                for e in range(2):
                    pe.wait_ge(w_lo_ready, SLAB[name] + e + 1)
                    o = OUT[name] + e
                    if o >= 2:
                        pe.wait_ge(out_read, o - 1)
                    banks.append(gp[:, o % 2, :])
                for c in range(DC):
                    pe.wait_ge(sq_done, 8 * NORM[kind] + c + 1)
                    pe.matmul(mp[:, 5, :], ones, sq[c % 2], start=c == 0, stop=c == DC - 1).then_inc(sq_summed, 1)
                    pe.wait_ge(a_lo_ready, A_AT[kind] + c + 1)
                    for e in range(2):
                        place, cols = (SLAB[name] + e) % RING, slice(c * P, (c + 1) * P)
                        hi, lo = w_hi[:, place, cols], w_lo[:, place, cols]
                        pe.matmul(banks[e], hi, a(c), start=c == 0, stop=False)
                        pe.matmul(banks[e], hi, al(c), start=False, stop=False)
                        ins = pe.matmul(banks[e], lo, a(c), start=False, stop=c == DC - 1)
                        if c == DC - 1:
                            ins.then_inc(half_done, 2)

            def a_wait(name):
                return lambda t: pe.wait_ge(a_lo_ready, A_AT[name] + t + 1)

            def inputs(ct):
                pe.wait_ge(out_read, OUT["u"] + CT)
                pe.wait_ge(win_ready, 1)
                if ct:
                    pe.wait_ge(v_read, ct)
                for part in range(2):
                    for s in range(STEP):
                        for pr in range(4):
                            rows = slice(32 * pr, 32 * pr + 32)
                            ins = pe.matmul(mp[:, pr, part * NB:(part + 1) * NB], win[rows, ct, s, part, :],
                                            U[rows, ct, s * NB:(s + 1) * NB], start=s == 0, stop=s == STEP - 1)
                ins.then_inc(v_done, 1)

            def local_products():
                pe.wait_ge(ca_ready, 1)
                for ct in range(CT):
                    for pr in range(4):
                        rows, q = slice(32 * pr, 32 * pr + 32), 4 * ct + pr
                        bank = mp[rows, 4, ct * STEP * 32:(ct + 1) * STEP * 32]
                        pe.matmul(bank, b_re[:, q, :], ca_re[:, 0:STEP, q, :], start=True, stop=False)
                        ins = pe.matmul(bank, b_im[:, q, :], ca_im[:, 0:STEP, q, :], start=False, stop=True)
                ins.then_inc(kloc_done, 1)

            def outputs(ct):
                pe.wait_ge(kloc_ready, 1)
                pe.wait_ge(st_ready, ct + 1)
                if ct:
                    pe.wait_ge(y_val, ct)
                for k in range(STEP):
                    pe.matmul(mp[:, 5, k * NB:T], kloc[:, ct, k, :], U[:, ct, 0:T - k * NB], start=k == 0, stop=False,
                              skip_group_check=True)
                for pr in range(4):
                    rows, q = slice(32 * pr, 32 * pr + 32), 4 * ct + pr
                    for s in range(STEP):
                        bank = mp[rows, 5, s * NB + 1:(s + 1) * NB]
                        pe.matmul(bank, ca_re[:, s + 1, q, :], st_re[:, pr, 0:NB - 1], start=False, stop=False,
                                  skip_group_check=True)
                        ins = pe.matmul(bank, ca_im[:, s + 1, q, :], st_im[:, pr, 0:NB - 1], start=False,
                                        stop=s == STEP - 1, skip_group_check=True)
                ins.then_inc(y_done, 1)

            def attention(A, between):
                for pp in range(A.pairs):
                    for b in range(T // P):
                        ins = pe.transpose(mp[:, 3 + pp, b * P:(b + 1) * P], A.kt[:, A.v0 + pp, b * P:(b + 1) * P],
                                           ident)
                    ins.then_inc(vt_done, 1)

                def scores(u):
                    b, pp, p = A.units[u]
                    rows = slice(HD * p, HD * p + HD)
                    if A.u0 + u:
                        pe.wait_ge(lg_ready, A.u0 + u)
                    for h4 in range(4):
                        for g, j, kb in A.chunks[u]:
                            ins = pe.matmul(A.scores()[:, h4, j * P:(j + 1) * P], A.q[rows, 4 * pp + h4, b * P:(b + 1) * P],
                                            A.kt[rows, A.k0 + pp, kb * P:(kb + 1) * P], start=True, stop=True)
                    ins.then_inc(sc_done, 1)

                n = len(A.units)
                scores(0)
                scores(1)
                pe.wait_ge(vt_ready, A.pairs + (A.u0 > 0))
                for u in range(n):
                    b, pp, p = A.units[u]
                    pe.wait_ge(pr_ready, A.u0 + u + 1)
                    for x, (g, j, kb) in enumerate(A.chunks[u]):
                        if x == 2 and u + 2 < n:
                            scores(u + 2)
                        if g >= 2:
                            pe.wait_ge(pt_ready, g - 1)
                        for h4 in range(4):
                            ins = pe.transpose(mp[:, 3 + g % 2, h4 * P:(h4 + 1) * P],
                                               A.logit[u % 2][:, h4, j * P:(j + 1) * P], ident)
                        ins.then_inc(pt_done, 1)
                    if u + 2 < n and len(A.chunks[u]) < 3:
                        scores(u + 2)
                    between(u)
                    if u:
                        if A.name:
                            pe.wait_ge(h_lo_ready, H_AT["y1"] + u)
                        else:
                            pe.wait_ge(at_read, u)
                    for x, (g, j, kb) in enumerate(A.chunks[u]):
                        pe.wait_ge(pt_ready, g + 1)
                        ins = pe.matmul(mp[HD * p:HD * p + HD, 5, :], A.vt[:, pp, kb, HD * p:HD * p + HD],
                                        A.pt[:, j, :], start=x == 0, stop=x == len(A.chunks[u]) - 1)
                    ins.then_inc(at_done, 1)

            start_stage("u", "n1")
            for n in range(2, SLAB["gate_s"]):
                gemm(0, 0, n, 8, 1, a, al, 0)
                if n == 7:
                    local_products()
                for ct in range(CT):
                    if n == 3 * ct + 6:
                        inputs(ct)
                    if ct < CT - 1 and n == 3 * ct + 10:
                        outputs(ct)
            outputs(CT - 1)
            pe.wait_ge(out_read, OUT["q"] + 4)
            pe.wait_ge(y_val, CT)
            attention(att1, lambda u: a_stage("gate_s", 0, u))
            pe.wait_ge(h_lo_ready, H_AT["y1"] + len(att1.units))
            for j in range(COUNT["branch_a"]):
                gemm(SLAB["branch_a"], 0, j, 4, 2, h, hl, OUT["branch_a"])
            for j in range(COUNT["glu"]):
                gemm(SLAB["glu"], 0, j, 4, 2, lambda t: h(4 + t), lambda t: hl(4 + t), OUT["glu"])
            for j in range(COUNT["branch_s"]):
                gemm(SLAB["branch_s"], 0, j, 4, 2, h, hl, OUT["branch_s"],
                     (lambda t: pe.wait_ge(h_lo_ready, H_AT["z2"] + t + 1)) if j == 0 else None)
            pe.wait_ge(a_lo_ready, A_AT["merged"] + DC)
            loop(pe, 8, lambda i, k: a_stage("out", i, k))
            mean_square("post1")

            def ff1_part(p, part):
                s0, h0 = PART1 * part, H_AT["ff"] + FF1_PART * part
                for k in range(2 if part == 0 else 0, FF1_PART):
                    gemm(SLAB["ff"], p, s0 + k, 8, 1, a, al, OUT["ff"], per=PART1)
                for m in range(DC):
                    gemm(SLAB["ff"], p, s0 + FF1_PART + m, FF1_PART, 1, h, hl, OUT["ff"],
                         (lambda t: pe.wait_ge(h_lo_ready, h0 + t + 1 + FF1_PART * p)) if m == 0 else None,
                         per=PART1)

            start_stage("ff", "n2")
            ff1_part(0, 0)
            with pe.Fori(0, FF1_PARTS - 2) as p:
                ff1_part(p, 1)
            ff1_part(0, FF1_PARTS - 1)
            mean_square("post2")

            start_stage("q2", "n3")
            for k in range(2, DC):
                a_stage("q2", 0, k)
            for name in ("k2", "v2"):
                for k in range(COUNT[name]):
                    a_stage(name, 0, k)
            pe.wait_ge(out_read, OUT["v2"] + 2)
            attention(att2, lambda u: a_stage("u2", 0, u) if u < DC else a_stage("g2", 0, u - DC))

            def recurrence_gates(j):
                n = MIX_SLAB["lru", j]
                pe.wait_ge(w_lo_ready, n + 1)
                for q in range(8):
                    o = 8 * j + q
                    if o >= 6:
                        pe.wait_ge(lru_sig, o - 5)
                    elif o == 0:
                        pe.wait_ge(at_read, len(att2.units))
                    t, cols = o // 4, slice(q * P, (q + 1) * P)
                    hi, lo = w_hi[:, n % RING, cols], w_lo[:, n % RING, cols]
                    pe.matmul(mp[:, o % 6, :], hi, h(t), start=True, stop=False)
                    pe.matmul(mp[:, o % 6, :], hi, hl(t), start=False, stop=False)
                    ins = pe.matmul(mp[:, o % 6, :], lo, h(t), start=False, stop=True)
                    if q < 7:
                        ins.then_inc(lg_done, 1)
                    else:
                        ins.then_inc(half_done, 2)

            for kind, t in MIX:
                if kind == "lru":
                    recurrence_gates(t)
                else:
                    gemm(MIX_SLAB[kind, t], 0, 0, 8, 1, a, al, MIX_OUT[kind, t])
            for k in range(DC):
                gemm(SLAB["out2"], 0, k, 8, 1, h, hl, OUT["out2"],
                     (lambda t: pe.wait_ge(h_lo_ready, H_AT["m2"] + t + 1)) if k == 0 else None)

            def ff2_part(chunks, slab0):
                s0 = slab0 - SLAB["ff2"]
                v0 = 8 * (s0 // PART2)
                for k in range(2 * chunks):
                    gemm(SLAB["ff2"], 0, s0 + k, 8, 1, a, al, OUT["ff2"], a_wait("n4") if s0 + k == 0 else None)
                    if s0 + k == 0:
                        mean_square("n4")
                for m in range(DC):
                    gemm(SLAB["ff2"], 0, s0 + 2 * chunks + m, chunks, 1, h, hl, OUT["ff2"],
                         (lambda t: pe.wait_ge(h_lo_ready, H_AT["ff2"] + v0 + t + 1)) if m == 0 else None)

            for part, chunks in enumerate(FF2_CHUNKS):
                ff2_part(chunks, SLAB["ff2"] + part * PART2)
            mean_square("n5")


def tiles_of(w, order_in=None, order_out=None):
    if order_in is not None:
        w = w.reshape(-1, HD, w.shape[1])[np.array(order_in)].reshape(w.shape)
    if order_out is not None:
        w = w.reshape(w.shape[0], -1, HD)[:, np.array(order_out)].reshape(w.shape)
    k, n = w.shape[0] // P, w.shape[1] // P
    return w.reshape(k, P, n, P).transpose(2, 0, 1, 3)


def lay_out(v):
    f = {k: np.asarray(a)[0] if a.ndim > 1 and a.shape[0] == 1 else np.asarray(a) for k, a in v.items()}
    stream = []

    def put(tiles):
        tiles = tiles.reshape(-1, tiles.shape[-3], P, P)
        per = tiles.shape[1] if tiles.shape[1] > 4 else 8
        tiles = tiles.reshape(-1, per, P, P)
        slab = np.zeros((tiles.shape[0], P, TILES, P), tiles.dtype)
        slab[:, :, :per] = tiles.transpose(0, 2, 1, 3)
        stream.append(slab.reshape(-1, P, TILES * P))

    w = f["w_in"]
    q, k, v1, u, ga, gs = np.split(w, [512, 640, 768, 1280, 2304], axis=1)
    for part in (u, k, v1, ga):
        put(tiles_of(part))
    put(tiles_of(q, None, HEADS1))
    put(tiles_of(gs))
    put(tiles_of(f["w_attn_branch"], HEADS1))
    put(tiles_of(f["w_glu"]))
    put(tiles_of(f["w_ssm_branch"]))
    put(tiles_of(f["w_out"]))
    wi, wo = tiles_of(f["w_ff_in"]), tiles_of(f["w_ff_out"])
    for p in range(FF1_PARTS):
        c = slice(p * FF1_PART, (p + 1) * FF1_PART)
        put(wi[c])
        put(wo[:, c])
    u, g, q, k, v1, za, zb = np.split(f["w_in_2"], [1024, 2048, 3072, 3328, 3584, 4608], axis=1)
    put(tiles_of(q, None, HEADS2))
    put(tiles_of(k))
    put(tiles_of(v1))
    put(tiles_of(u, None, HEADS2))
    put(tiles_of(g, None, HEADS2))
    gates = np.zeros((DC, 2, 2, P, P), np.float32)
    order = np.array(HEADS2).reshape(DC, 2)
    for half in range(2):
        rows = slice(HD * half, HD * half + HD)
        for kind, name in enumerate(("lru_wa_2", "lru_wx_2")):
            gates[:, :, kind, rows, rows] = f[name][:, order[:, half]].transpose(1, 0, 2, 3)
    kinds = {"lru": gates.reshape(4, 8, P, P), "za": tiles_of(za, None, HEADS2), "zb": tiles_of(zb, None, HEADS2)}
    for kind, t in MIX:
        put(kinds[kind][t:t + 1])
    put(tiles_of(f["w_out_2"], HEADS2))
    wi, wo = tiles_of(f["w_ffn_in_2"]), tiles_of(f["w_ffn_out_2"])
    hid, c0 = wi.shape[0] // 2, 0
    for n in FF2_CHUNKS:
        c = slice(c0, c0 + n)
        put(np.stack([wi[:hid][c], wi[hid:][c]], axis=1).reshape(2 * n, DC, P, P))
        put(wo[:, c])
        c0 += n

    def column(a, order=None):
        a = a.reshape(-1, HD)
        if order is not None:
            n = len(order)
            a = np.concatenate([a[i:i + n][np.array(order)] for i in range(0, a.shape[0], n)])
        return a.reshape(-1, P).T

    def across(a):
        return np.broadcast_to(a.reshape(1, -1), (P, a.size))

    cols = {
        "g_mix_pre": column(f["norm_mix_pre"]), "g_mix_post": column(f["norm_mix_post"]),
        "g_mlp_pre": column(f["norm_mlp_pre"]), "g_mlp_post": column(f["norm_mlp_post"]),
        "sinks": across(f["sinks"]), "d_skip": column(f["d_skip"]), "g_mix2": column(f["norm_mix_g_2"]),
        "b_gate": column(f["b_gate_2"], HEADS2), "conv_w": column(f["conv_w_2"], HEADS2),
        "conv_b": column(f["conv_b_2"], HEADS2), "lam": column(f["lru_lambda_2"], HEADS2),
        "ba": column(f["lru_ba_2"], HEADS2), "bx": column(f["lru_bx_2"], HEADS2),
        "sinks2": across(f["attn_sink_2"]), "g_ffn2": column(f["norm_ffn_g_2"]), "g_fin2": column(f["norm_final_g_2"]),
        "iota": across(np.arange(16, dtype=np.float32)), "eps": np.full((P, 1), EPS, np.float32),
        "pad": np.zeros((P, 3), np.float32), "ident": np.eye(P, dtype=np.float32), "ones": np.ones((P, P), np.float32),
    }
    params = np.concatenate([cols[name] for name, _ in _cols], axis=1)
    assert params.shape == (P, NCOL)

    G, N = f["lam_re"].shape
    C = SSM_CH // G

    def by_both(a):
        a = np.broadcast_to(a.reshape(G, -1), (G, N))
        state = a.reshape(PAIRS, P).T
        pair = a.reshape(CT, 4, 1, 2 * N)
        channel = np.broadcast_to(pair, (CT, 4, 2 * C, 2 * N)).reshape(CT, P, P).transpose(1, 0, 2).reshape(P, CT * P)
        return np.concatenate([state, channel], axis=1)

    s5p = np.stack([by_both(f["lam_re"]), by_both(f["lam_im"]), by_both(f["log_dt"])], axis=1)

    def diagonal(a):
        r, c = a.shape[1:]
        d = np.zeros((PAIRS, 2, r, 2, c), a.dtype)
        for g in range(2):
            d[:, g, :, g, :] = a[g::2]
        return d.reshape(PAIRS, 2 * r, 2 * c)

    b = [diagonal(f[n]) for n in ("b_re", "b_im")]
    c = [diagonal(f[n].transpose(0, 2, 1)) for n in ("c_re", "c_im")]
    s5b = np.stack([a.transpose(1, 0, 2) for a in b], axis=1)
    s5c = np.stack([a.transpose(1, 0, 2) for a in c], axis=1)
    s5bt = np.stack([a.transpose(0, 2, 1).reshape(CT, P, P).transpose(1, 0, 2) for a in b], axis=1)

    dist = np.arange(P)[:, None] + P - np.arange(2 * P)[None, :]
    exact = NBUCKET // 2
    df = np.maximum(dist, 1).astype(np.float32)
    large = exact + (np.log(df / np.float32(exact)) / np.float32(np.log(MAXDIST / exact))
                     * np.float32(NBUCKET - exact)).astype(np.int32)
    bucket = np.where(dist < exact, np.maximum(dist, 0), np.minimum(large, NBUCKET - 1))
    inside = (dist >= 0) & (dist < P)
    bias1 = np.full((P, 8, 2 * P), -1e30, np.float32)
    rb = np.asarray(v["rel_bias"])
    for hd in range(8):
        bias1[:, hd][inside] = rb[bucket[inside], hd]
    far = np.abs(np.arange(P)[:, None] + P - np.arange(3 * P)[None, :])
    nd = np.where(far <= P, -far, -1e30).astype(np.float32)

    x = np.asarray(v["x"])[0].T.reshape(DC, P, T).transpose(1, 0, 2)
    return {"slabs": np.concatenate(stream), "params": params, "s5p": s5p, "s5bt": s5bt, "s5b": s5b, "s5c": s5c,
            "bias1": bias1, "nd2": nd, "x_in": x}


def kernel(**inputs):
    import concourse.bacc as bacc
    from concourse.bass_utils import run_bass_kernel_spmd as run

    arrays = {k: np.ascontiguousarray(a) for k, a in lay_out(inputs).items()}
    assert arrays["slabs"].shape[0] == NSLAB, arrays["slabs"].shape
    nc = bacc.Bacc("TRN2", target_bir_lowering=False, num_devices=1)
    args = {k: nc.dram_tensor(k, a.shape, F32, kind="ExternalInput").ap() for k, a in arrays.items()}
    out = nc.dram_tensor("out_t", (P, DC, T), F32, kind="ExternalOutput").ap()
    build(nc, out=out, **args)
    r = run(nc, [arrays], core_ids=[0])
    y = r.results[0]["out_t"]
    return np.ascontiguousarray(y.transpose(2, 1, 0).reshape(1, T, D))
```

```python
from contextlib import ExitStack

import numpy as np

import concourse.bass as bass
from concourse import mybir

F32 = mybir.dt.float32
F32R = mybir.dt.float32r
ALU = mybir.AluOpType
ACT = mybir.ActivationFunctionType
AX = mybir.AxisListType

P = 128
D = 1024
T = 512
DC = D // P
HD = 64
EPS = 1e-6

NBUCKET, MAXDIST = 32, 128
SSM_CH = 512
CT = SSM_CH // P
PAIRS = 16
STEP = 4
NB = T // STEP
E0 = 16
E1 = NB // E0
FF1_PARTS = 4
FF1_PART = 8
FF2_CHUNKS = [8, 8, 6]

TILES = 8
RAW = 2
RING = 4
AHEAD = 2

HEADS1 = [par * 4 + h for h in range(4) for par in range(2)]
HEADS2 = [(2 * pp + par) * 4 + h for pp in range(2) for h in range(4) for par in range(2)]

_counts = [("u", 4), ("k", 1), ("v", 1), ("gate_a", 8), ("q", 4), ("gate_s", 8), ("branch_a", 4),
           ("glu", 2), ("branch_s", 4), ("out", 8), ("ff", 16 * FF1_PARTS),
           ("q2", 8), ("k2", 2), ("v2", 2), ("u2", 8), ("g2", 8), ("mix", 20),
           ("out2", 8), ("ff2", sum(2 * c + 8 for c in FF2_CHUNKS))]
MIX = []
for _t in range(DC):
    MIX += ([("lru", _t // 2)] if _t % 2 == 0 else []) + [("zb", _t)] + ([("za", _t - 1)] if _t else [])
MIX += [("za", DC - 1)]
SLAB, _n = {}, 0
for _name, _c in _counts:
    SLAB[_name] = _n
    _n += _c
NSLAB = _n
COUNT = dict(_counts)
assert NSLAB % RING == 0

_outs = [("u", 4), ("k", 1), ("v", 1), ("gate_a", 8), ("q", 4), ("gate_s", 8), ("branch_a", 8), ("glu", 4),
         ("branch_s", 8), ("out", 8), ("ff", 16 * FF1_PARTS), ("q2", 8), ("k2", 2), ("v2", 2), ("u2", 8),
         ("g2", 8), ("mix", 16), ("out2", 8), ("ff2", sum(2 * c + 8 for c in FF2_CHUNKS))]
OUT, _n = {}, 0
for _name, _c in _outs:
    OUT[_name] = _n
    _n += _c

MIX_SLAB = {key: SLAB["mix"] + i for i, key in enumerate(MIX)}
MIX_OUT = {key: OUT["mix"] + i for i, key in enumerate(k for k in MIX if k[0] != "lru")}
MIX_GATE = [g for t in range(1, DC + 1) for g in [("zb", t - 1)] + ([("za", t - 2)] if t > 1 else [])] + [("za", DC - 1)]

_cols = [("g_mix_pre", 8), ("g_mix_post", 8), ("g_mlp_pre", 8), ("g_mlp_post", 8), ("sinks", 8), ("d_skip", 4),
         ("g_mix2", 8), ("b_gate", 16), ("conv_w", 32), ("conv_b", 8), ("lam", 16), ("ba", 16), ("bx", 16),
         ("sinks2", 16), ("g_ffn2", 8), ("g_fin2", 8), ("iota", 16), ("eps", 1), ("pad", 3),
         ("ident", P), ("ones", P)]
COL, _n = {}, 0
for _name, _c in _cols:
    COL[_name] = _n
    _n += _c
NCOL = _n
SW = PAIRS + CT * P

MAGIC = 1.5 * 2.0 ** 23
TWO_PI = 2.0 * np.pi
C1 = 6.28125
C2 = float(np.float32(np.round((TWO_PI - C1) * 2.0 ** 20) / 2.0 ** 20))
C3 = float(np.float32(TWO_PI - C1 - C2))
TURN = 6.283185


def build(nc, slabs, params, s5p, s5bt, s5b, s5c, bias1, nd2, x_in, out):
    ctx = ExitStack()
    with ctx:
        def sb(name, shape, dt=F32):
            return ctx.enter_context(nc.sbuf_tensor(name, shape, dt))

        def sem(name):
            return ctx.enter_context(nc.semaphore(name))

        raw = sb("raw", [P, RAW, TILES * P])
        w_hi = sb("w_hi", [P, RING, TILES * P], F32R)
        w_lo = sb("w_lo", [P, RING, TILES * P], F32R)
        a_hi = sb("a_hi", [P, DC, T], F32R)
        a_lo = sb("a_lo", [P, DC, T], F32R)
        h_hi = sb("h_hi", [P, DC, T], F32R)
        h_lo = sb("h_lo", [P, DC, T], F32R)
        par = sb("par", [P, NCOL])
        R = sb("R", [P, T])
        AR = 25600
        arena = sb("arena", [P, AR])

        def region(at, *shape):
            n = int(np.prod(shape))
            assert at + n <= AR, (at, shape)
            v = arena[:, at:at + n]
            if len(shape) == 2:
                v = v.rearrange("p (a b) -> p a b", a=shape[0])
            if len(shape) == 3:
                v = v.rearrange("p (a b c) -> p a b c", a=shape[0], b=shape[1])
            if len(shape) == 4:
                v = v.rearrange("p (a b c d) -> p a b c d", a=shape[0], b=shape[1], c=shape[2])
            return v

        def col(name, i=0, n=1):
            return par[:, COL[name] + i:COL[name] + i + n]

        ident = col("ident", 0, P)
        ones = col("ones", 0, P)

        X = region(0, DC, T)
        tab = [(region(0, 4, NB), region(512, 4, NB)), (region(13312, 4, NB), region(13824, 4, NB))]
        tab_t = region(24512, 4, NB)
        t1, t2 = region(1024, 4, NB), region(1536, 4, NB)
        g_re, g_im = region(2048, 4, NB), region(2560, 4, NB)
        st_re, st_im = region(3072, 4, NB), region(3584, 4, NB)
        win = region(4096, CT, STEP, 2, P)
        ca_re, ca_im = region(8192, STEP + 1, PAIRS, 32), region(10752, STEP + 1, PAIRS, 32)
        b_re, b_im = region(13312, PAIRS, 32), region(13824, PAIRS, 32)
        kloc = region(14336, CT, STEP, P)
        e0c, e0s = region(16384, PAIRS, E0), region(16640, PAIRS, E0)
        e1c, e1s = region(16896, PAIRS, E1), region(17024, PAIRS, E1)
        U = region(17152, CT, T)
        KV = region(19200, 2, T)
        gate1 = region(20224, DC, T)
        rho = region(24320, PAIRS)
        a_re, a_im = region(24336, PAIRS), region(24352, PAIRS)
        rot = region(24368, 4, PAIRS)
        zp = region(25088, T)
        d_are, d_aim, d_fre, d_fim = (region(20224 + SW * i, SW) for i in range(4))
        bt_re, bt_im = region(20224 + 4 * SW, CT, P), region(20736 + 4 * SW, CT, P)
        w_t1, w_t2 = region(21248 + 4 * SW, CT, P), region(25088, CT, P)
        s_w = [region(14336 + SW * i, SW) for i in range(3)] + [region(8704 + SW * i, SW) for i in range(3)] + \
              [region(11264 + SW * i, SW) for i in range(3)]
        Q = region(4096, 4, T)
        bias8 = region(6144, 8, 2 * P)
        logit1 = [region(8192, 4, 2 * P), region(9216, 4, 2 * P)]
        PT1 = region(10240, 2, T)
        VT1 = region(11264, 1, 4, P)
        mini = [region(24448 + 32 * i, 8, 4) for i in range(2)]
        gate2 = region(12288, DC, T)
        by_token = region(24432, T // P)
        ssum = region(17152, T)
        sq = [region(17664, T), region(18176, T)]
        diag = region(17664, T // P, P)
        tmp = [region(24512, T), region(25024, T)]
        fbuf = [region(12288, T), region(12800, T)]
        Y = region(8192, DC, T)
        Fo = region(4096, DC, T)
        UC = region(4096, DC, T)
        Q2 = region(8192, DC, T)
        KV2 = region(12288, 4, T)
        VT2 = region(14336, 2, 4, P)
        G2 = region(20352, DC, T)
        HS = region(15360, DC, T)
        logit2 = [region(15360, 4, 3 * P), region(16896, 4, 3 * P)]
        PT2 = region(18432, 3, T)
        nd8 = region(19968, 3 * P)
        lru = [region(12288 + T * i, T) for i in range(6)]
        lru45 = region(12288 + 4 * T, 2 * T)
        spc = region(15360, 12, 16)
        decay_exp, decay_tanh = col("lam", 0, 16), col("iota", 0, 16)
        OUTB = region(4096, DC, T)

        gp = ctx.enter_context(nc.psum_tensor("gp", [P, 2, T], F32))
        mp = ctx.enter_context(nc.psum_tensor("mp", [P, 6, T], F32))

        s_par = sem("params_loaded")
        s_bc = sem("b_and_c_loaded")
        s_x = [sem(f"x_quarter{c}_loaded") for c in range(4)]
        s_raw = [sem(f"slab_loaded{i}") for i in range(RAW)]
        s_bias = sem("bias_loaded")
        s_x2 = sem("x_loaded_again")
        s_nd = sem("distances_loaded")
        w_hi_ready = sem("w_hi_ready")
        w_lo_ready = sem("w_lo_ready")
        half_done = sem("half_slab_done")
        out_read = sem("output_read")
        vec_step = sem("vec_step")
        act_step = sem("act_step")
        pool_step = sem("pool_step")
        a_hi_ready, a_lo_ready = sem("a_hi_ready"), sem("a_lo_ready")
        h_val, h_hi_ready, h_lo_ready = sem("h_value"), sem("h_hi_ready"), sem("h_lo_ready")
        x_new = sem("x_updated")
        m_val = sem("merged_value")
        sq_done, sq_added = sem("square_done"), sem("square_added")
        sq_summed = sem("square_summed")
        diag_ready, rms_spread = sem("inverse_rms_on_diagonals"), sem("inverse_rms_spread")
        inverse_ready, scaled, gained = sem("inverse_rms_ready"), sem("update_scaled"), sem("gain_applied")
        rms_sum, rms_root = sem("rms_sum"), sem("rms_root")
        disc_act, disc_vec = sem("discretise_act"), sem("discretise_vec")
        win_ready = sem("win_ready")
        cos_ready, tab_ready = sem("cosines_ready"), sem("rotation_table_ready")
        ca_ready = sem("c_powers_ready")
        kloc_done, kloc_ready = sem("kloc_product"), sem("kloc_ready")
        v_done, v_read = sem("state_inputs"), sem("state_inputs_read")
        st_ready, y_done = sem("states_ready"), sem("ssm_output")
        y_val, z_val = sem("ssm_value"), sem("z_value")
        gate_val = sem("gate_value")
        vt_done, vt_ready = sem("v_transposed"), sem("v_ready")
        sc_done, lg_ready = sem("scores_done"), sem("logits_ready")
        nb_ready, ex_done = sem("maximum_ready"), sem("exponentials_done")
        pr_ready, pt_done, pt_ready = sem("probs_ready"), sem("probs_transposed"), sem("probs_t_ready")
        at_done = sem("attention_done")
        glu_sig = sem("glu_sigmoid")
        at_read = sem("attention_read")
        lg_done, lru_sig, lru_act, lru_mid, lru_free = (
            sem("lru_products"), sem("lru_sigmoids"), sem("lru_exp_tanh"), sem("lru_guarded"), sem("lru_free"))
        lru_tanh, lru_root = sem("lru_tanh"), sem("lru_root")
        spc_val, spc_exp, decay_ready = sem("lambda_magnitude"), sem("lambda_exp"), sem("decay_ready")
        s_out = sem("stored")

        block = ctx.enter_context(nc.Block())

        NORM = {"n1": 0, "post1": 1, "n2": 2, "post2": 3, "n3": 4, "n4": 5, "n5": 6}
        BY_POOL = {"n1": 0, "n2": 1, "n3": 2}
        BY_VEC = {"post1": 0, "post2": 1, "n4": 2, "n5": 3}
        A_AT = {"n1": 0, "merged": 8, "n2": 16, "n3": 24, "n4": 32}
        H_AT = {"z": 0, "y1": 4, "z2": 12, "ff": 16, "uc": 48, "m2": 56, "ff2": 64}
        V_AT = {"ff": 0, "uc": 32, "m2": 40, "ff2": 48}
        X_AT = {"post1": 0, "post2": 8, "ff2": 16}
        G_AT = {"gate_a": 0, "gate_s": 8, "g2": 16, "mix": 24, "ff2": 40}
        MIX_VAL = {key: G_AT["mix"] + i + 1 for i, key in enumerate(MIX_GATE)}
        PART1 = 2 * FF1_PART + DC - FF1_PART
        PART2 = 2 * FF2_CHUNKS[0] + DC

        SCALED = [5, 6, 7]
        WITH_POOL = ["post1", "post2", "n5"]
        SSM_IN, SSM_OUT = [7, 10, 12, 14], [10, 12, 15, 16]

        class Attention:

            def __init__(self, first, chunk0, pairs, back, forth, q, kt, k0, v0, vt, logit, pt, sinks, name):
                self.units = [(b, pp, p) for b in range(T // P) for pp in range(pairs) for p in range(2)]
                self.u0, self.q, self.kt, self.k0, self.v0, self.vt = first, q, kt, k0, v0, vt
                self.logit, self.pt, self.sinks, self.name, self.pairs = logit, pt, sinks, name, pairs
                self.chunks, self.done = [], []
                g = chunk0
                for b, _, _ in self.units:
                    js = [(j, b - back + j) for j in range(back + forth + 1) if 0 <= b - back + j < T // P]
                    self.chunks.append([(g + n, j, kb) for n, (j, kb) in enumerate(js)])
                    g += len(js)
                    self.done.append(g)
                self.width = (back + forth + 1) * P

            def span(self, u):
                return self.chunks[u][0][1] * P, (self.chunks[u][-1][1] + 1) * P

            def scores(self):
                return mp[:, 0:3, :].rearrange("p a b -> p (a b)")[:, 0:4 * self.width].rearrange(
                    "p (h k) -> p h k", h=4)

            def out_ap(self, view, u):
                b, pp, p = self.units[u]
                return view[HD * p:HD * p + HD, 4 * pp:4 * pp + 4, b * P:b * P + P]

        att1 = Attention(0, 0, 1, 1, 0, Q, KV, 0, 1, VT1, logit1, PT1, "sinks", "y1")
        att2 = Attention(len(att1.units), att1.done[-1], 2, 1, 1, Q2, KV2, 0, 2, VT2, logit2, PT2, "sinks2", "")

        class Tally:

            def __init__(self, eng, s):
                self.eng, self.s, self.n, self.i, self.per = eng, s, 0, 0, 0

            def up(self, ins):
                ins.then_inc(self.s, 1)
                self.n += 1

            def settle(self):
                self.eng.wait_ge(self.s, self.n + self.i * self.per)

            def run(self, ins):
                self.up(ins)
                self.settle()

        def loop(eng, count, body, tally=None, per=0, unroll=4):
            if count % unroll or count < 2 * unroll:
                for k in range(count):
                    body(0, k)
                return
            start = tally.n if tally else 0
            with eng.Fori(0, count // unroll) as i:
                if tally:
                    tally.i, tally.per = i, per * unroll
                for k in range(unroll):
                    body(i, k)
            if tally:
                assert tally.n - start == per * unroll, (tally.n - start, per)
                tally.n, tally.i, tally.per = start + per * count, 0, 0

        def at(view, e):
            if isinstance(e, int):
                return view[:, e, :]
            return view[:, bass.ds(e, 1), :].rearrange("p a b -> p (a b)")

        def pcol(name, e):
            if isinstance(e, int):
                return col(name, e)
            return par[:, bass.ds(COL[name] + e, 1)]

        @block.sync
        def _(sp):
            sp.dma_start(par[:, :], params).then_inc(s_par, 16)

            def load(n, k):
                sp.dma_start(raw[:, k % RAW, :], n).then_inc(s_raw[k % RAW], 16)

            def load_x(q):
                sp.dma_start(X[:, 2 * q:2 * q + 2, :], x_in[:, 2 * q:2 * q + 2, :]).then_inc(s_x[q], 16)

            load_x(0)
            load(slabs[0], 0)
            load(slabs[1], 1)
            load_x(1)
            load_x(2)
            for k in (2, 0, 1):
                sp.dma_start(s_w[k], s5p[:, k, :]).then_inc(s_par, 16)
            load_x(3)
            with sp.Fori(0, (NSLAB - RAW) // RAW) as i:
                for k in range(RAW):
                    sp.wait_ge(w_lo_ready, i * RAW + (k + 1))
                    src = slabs[bass.ds(i * RAW + (k + RAW), 1), :, :].rearrange("a p n -> (a p) n")
                    load(src, k)
            for c in (0, 1, SCALED[0], 2, 3, SCALED[1], 4, SCALED[2]):
                if c in SCALED:
                    sp.wait_ge(scaled, 2 * len(SCALED) + SCALED.index(c) + 1)
                else:
                    sp.wait_ge(x_new, X_AT["ff2"] + c + 1)
                sp.dma_start(out[:, c, :], OUTB[:, c, :]).then_inc(s_out, 16)
            sp.wait_ge(s_out, 16 * DC)

        @block.gpsimd
        def _(pool):
            G = Tally(pool, pool_step)
            def sum_squares(kind):
                for c in range(DC):
                    n = 8 * BY_POOL[kind] + c
                    pool.wait_ge(sq_done, 8 * NORM[kind] + c + 1)
                    if c == 0:
                        pool.tensor_copy(ssum, sq[0]).then_inc(sq_summed, 1)
                    else:
                        pool.wait_ge(sq_summed, n)
                        pool.tensor_tensor(ssum, ssum, sq[c % 2], ALU.add).then_inc(sq_summed, 1)

            def scale_by_inverse(n, rows):
                pool.wait_ge(inverse_ready, n)
                for c in SCALED:
                    pool.tensor_tensor(rows[:, c, :], rows[:, c, :], R[:, :], ALU.mult).then_inc(scaled, 1)

            sum_squares("n1")
            for dst, src in ((b_re, s5b[:, 0]), (b_im, s5b[:, 1]), (ca_re[:, 0], s5c[:, 0]), (ca_im[:, 0], s5c[:, 1]),
                             (bt_re, s5bt[:, 0]), (bt_im, s5bt[:, 1])):
                pool.dma_start(dst, src).then_inc(s_bc, 16)
            pool.wait_ge(s_bc, 96)
            pool.wait_ge(disc_vec, 2)

            def wide(v):
                return v[:, PAIRS:SW].rearrange("p (a b) -> p a b", a=CT)

            def product(o_re, o_im, a_re, a_im, c_re, c_im, last=None):
                G.up(pool.tensor_tensor(w_t1, a_re, c_re, ALU.mult))
                G.run(pool.tensor_tensor(w_t2, a_im, c_im, ALU.mult))
                G.run(pool.tensor_tensor(o_re, w_t1, w_t2, ALU.subtract))
                G.up(pool.tensor_tensor(w_t1, a_re, c_im, ALU.mult))
                G.run(pool.tensor_tensor(w_t2, a_im, c_re, ALU.mult))
                ins = pool.tensor_tensor(o_im, w_t1, w_t2, ALU.add)
                if last:
                    ins.then_inc(last, 1)
                else:
                    G.run(ins)

            def w(s, part):
                return win[:, :, s, part, :]

            product(w(STEP - 1, 0), w(STEP - 1, 1), wide(d_fre), wide(d_fim), bt_re, bt_im)
            for s in range(STEP - 2, -1, -1):
                product(w(s, 0), w(s, 1), wide(d_are), wide(d_aim), w(s + 1, 0), w(s + 1, 1),
                        win_ready if s == 0 else None)
            def table(ct):
                def fine(v):
                    return v[:, 4 * ct:4 * ct + 4, :].unsqueeze(2).to_broadcast([P, 4, E1, E0])

                def coarse(v):
                    return v[:, 4 * ct:4 * ct + 4, :].unsqueeze(3).to_broadcast([P, 4, E1, E0])

                def full(v):
                    return v.rearrange("p a (x y) -> p a x y", x=E1)
                cos, sin = tab[ct % 2]
                if ct == 1:
                    pool.wait_ge(kloc_done, 1)
                if ct >= 2:
                    pool.wait_ge(st_ready, ct - 1)
                G.up(pool.tensor_tensor(full(cos), coarse(e1c), fine(e0c), ALU.mult))
                G.run(pool.tensor_tensor(full(tab_t), coarse(e1s), fine(e0s), ALU.mult))
                G.run(pool.tensor_tensor(cos, cos, tab_t, ALU.subtract))
                G.up(pool.tensor_tensor(full(sin), coarse(e1s), fine(e0c), ALU.mult))
                G.run(pool.tensor_tensor(full(tab_t), coarse(e1c), fine(e0s), ALU.mult))
                pool.tensor_tensor(sin, sin, tab_t, ALU.add).then_inc(tab_ready, 1)
                pool.wait_ge(tab_ready, ct + 1)

            pool.wait_ge(cos_ready, 1)
            for ct in range(CT):
                table(ct)
            pool.wait_ge(v_done, CT)
            pool.dma_start(bias8, bias1).then_inc(s_bias, 16)
            pool.wait_ge(y_done, CT)
            pool.dma_start(X, x_in).then_inc(s_x2, 16)
            scale_by_inverse(1, Y)
            sum_squares("n2")
            pool.wait_ge(x_new, DC)
            pool.dma_start(nd8, nd2).then_inc(s_nd, 16)
            scale_by_inverse(2, Fo)
            sum_squares("n3")
            pool.wait_ge(gained, len(SCALED))
            scale_by_inverse(3, OUTB)

        @block.scalar
        def _(act):
            S = Tally(act, act_step)

            def split(base, i, k, per=4):
                n = base + k
                if isinstance(i, int) and n >= NSLAB:
                    return
                act.wait_ge(s_raw[n % RAW], 16 * (n // RAW + 1) + 16 // RAW * per * i)
                if n >= RING:
                    act.wait_ge(half_done, 2 * (n - RING + 1) + 2 * per * i)
                nc.scalar.activation(w_hi[:, n % RING, :], raw[:, n % RAW, :], ACT.Copy).then_inc(w_hi_ready, 1)

            def square(kind, c, i, src, static):
                if kind in BY_POOL:
                    if c >= 2:
                        act.wait_ge(sq_summed, 8 * BY_POOL[kind] + c - 1)
                elif 8 * BY_VEC[kind] + c >= 2:
                    act.wait_ge(sq_added, 8 * BY_VEC[kind] + c - 1 + 4 * i)
                dst = sq[static % 2]
                nc.scalar.activation(dst, src, ACT.Square).then_inc(sq_done, 1)

            def root_table():
                S.run(nc.scalar.activation(col("pad"), col("eps"), ACT.Sqrt))

            def root(kind):
                act.wait_ge(rms_sum, NORM[kind] + 1)
                dst, src = (by_token, mp[:, 5, 0:T // P]) if kind in WITH_POOL else (R[:, :], mp[:, 5, :])
                nc.scalar.activation(dst, src, ACT.Sqrt, bias=col("eps"), scale=1.0 / D).then_inc(rms_root, 1)

            def normalised(kind, gain, wait, chunks=range(DC)):
                for c in chunks:
                    wait(c)
                    nc.scalar.activation(a_hi[:, c, :], X[:, c, :], ACT.Copy, scale=col(gain, c)).then_inc(a_hi_ready, 1)
                    square(kind, c, 0, X[:, c, :], c)

            x_quarter = lambda c: act.wait_ge(s_x[c // 2], 16)
            act.wait_ge(s_par, 16)
            normalised("n1", "g_mix_pre", x_quarter, range(0, 2))
            split(0, 0, 0)
            split(1, 0, 0)
            act.wait_ge(s_par, 64)
            nc.scalar.activation(s_w[2], s_w[2], ACT.Exp).then_inc(disc_act, 1)
            normalised("n1", "g_mix_pre", x_quarter, range(2, 4))
            act.wait_ge(disc_vec, 1)
            nc.scalar.activation(s_w[6], s_w[3], ACT.Exp).then_inc(disc_act, 1)
            nc.scalar.activation(s_w[7], s_w[4], ACT.Sin).then_inc(disc_act, 1)
            nc.scalar.activation(s_w[8], s_w[4], ACT.Sin, scale=0.5).then_inc(disc_act, 1)
            split(2, 0, 0)
            root_table()
            normalised("n1", "g_mix_pre", x_quarter, range(4, DC))
            root("n1")

            def z_chunk(ct):
                act.wait_ge(y_val, ct + 1)
                nc.scalar.activation(U[:, ct, :], zp, ACT.Gelu_apprx_tanh).then_inc(z_val, 1)
                act.wait_ge(z_val, ct + 1)
                nc.scalar.activation(h_hi[:, 4 + ct, :], U[:, ct, :], ACT.Copy).then_inc(h_hi_ready, 1)

            for n in range(SLAB["u"], SLAB["gate_s"]):
                if n:
                    split(n + AHEAD, 0, 0)
                if SLAB["gate_a"] <= n < SLAB["gate_a"] + 8:
                    m = n - SLAB["gate_a"]
                    act.wait_ge(out_read, OUT["gate_a"] + m + 1)
                    nc.scalar.activation(gate1[:, m, :], gate1[:, m, :], ACT.Sigmoid).then_inc(gate_val, 1)
                if n == 2:
                    act.wait_ge(disc_vec, 3)
                    nc.scalar.activation(e0c, e0s, ACT.Sin, scale=TURN / 2).then_inc(disc_act, 1)
                    nc.scalar.activation(e1c, e1s, ACT.Sin, scale=TURN / 2).then_inc(disc_act, 1)
                    S.up(nc.scalar.activation(e0s, e0s, ACT.Sin, scale=TURN))
                    nc.scalar.activation(e1s, e1s, ACT.Sin, scale=TURN).then_inc(disc_act, 1)
                if n - 1 in SSM_OUT:
                    z_chunk(SSM_OUT.index(n - 1))

            def attention(A, slab0, gate):
                for pp in range(A.pairs):
                    act.wait_ge(vt_done, pp + 1 + (A.u0 > 0))
                    nc.scalar.activation(A.vt[:, pp, :, :].rearrange("p a b -> p (a b)"), mp[:, 3 + pp, :],
                                         ACT.Copy).then_inc(vt_ready, 1)

                def exponentials(u):
                    row = mini[u % 2]
                    lo, hi = A.span(u)
                    act.wait_ge(nb_ready, A.u0 + u + 1)
                    nc.scalar.activation(row[:, 3, :], row[:, 2, :], ACT.Exp)
                    for h in range(4):
                        L = A.logit[u % 2][:, h, lo:hi]
                        ins = nc.scalar.activation(L, L, ACT.Exp, bias=row[:, 1, h:h + 1], scale=0.125,
                                                   accum_out=row[:, 4, h:h + 1])
                    ins.then_inc(ex_done, 1)

                n = len(A.units)
                split(slab0 + AHEAD, 0, 0)
                exponentials(0)
                exponentials(1)
                gate(0)
                for u in range(n):
                    for g, j, _ in A.chunks[u]:
                        if u:
                            act.wait_ge(at_done, A.u0 + u)
                        act.wait_ge(pt_done, g + 1)
                        nc.scalar.activation(A.pt[:, j, :], mp[:, 3 + g % 2, :], ACT.Copy).then_inc(pt_ready, 1)
                    if A.name and u:
                        attention_hi(A, u - 1)
                    if u + 1 < n:
                        split(slab0 + u + 1 + AHEAD, 0, 0)
                    if u + 2 < n:
                        exponentials(u + 2)
                    if u + 1 < n:
                        gate(u + 1)
                if A.name:
                    attention_hi(A, n - 1)

            def attention_hi(A, u):
                p = A.units[u][2]
                act.wait_ge(at_done, A.u0 + u + 1)
                nc.scalar.activation(A.out_ap(h_hi, u), mp[HD * p:HD * p + HD, 5, :].rearrange("p (h q) -> p h q", h=4),
                                     ACT.Copy).then_inc(h_hi_ready, 1)

            def gate_s(u):
                act.wait_ge(out_read, OUT["gate_s"] + u + 1)
                nc.scalar.activation(gate2[:, u, :], gate2[:, u, :], ACT.Sigmoid).then_inc(gate_val, 1)

            attention(att1, SLAB["gate_s"], gate_s)

            loop(act, COUNT["branch_a"], lambda i, k: split(SLAB["branch_a"] + AHEAD, i, k))

            for j in range(COUNT["glu"]):
                split(SLAB["glu"] + AHEAD, 0, j)
                for m in (2 * j, 2 * j + 1):
                    act.wait_ge(half_done, 2 * SLAB["glu"] + m + 1)
                    if m >= 2:
                        act.wait_ge(out_read, OUT["glu"] + m - 1)
                    nc.scalar.activation(tmp[m % 2], gp[:, (OUT["glu"] + m) % 2, :], ACT.Sigmoid).then_inc(glu_sig, 1)
                    act.wait_ge(out_read, OUT["glu"] + m + 1)
                    nc.scalar.activation(h_hi[:, m, :], U[:, m, :], ACT.Copy).then_inc(h_hi_ready, 1)
            for j in range(COUNT["branch_s"]):
                split(SLAB["branch_s"] + AHEAD, 0, j)
                for m in (2 * j, 2 * j + 1):
                    act.wait_ge(m_val, m + 1)
                    nc.scalar.activation(a_hi[:, m, :], gate1[:, m, :], ACT.Copy).then_inc(a_hi_ready, 1)

            root_table()

            def out_body(i, k):
                split(SLAB["out"] + AHEAD, i, k)
                if k == DC - 1:
                    split(SLAB["ff"] + AHEAD, 0, 0)
                act.wait_ge(half_done, 2 * (SLAB["out"] + k + 1) + 8 * i)
                square("post1", k, i, gp[:, (OUT["out"] + k) % 2, :], k)
            loop(act, 8, out_body, unroll=8)
            root("post1")
            normalised("n2", "g_mlp_pre", lambda c: act.wait_ge(x_new, X_AT["post1"] + c + 1))
            split(SLAB["ff"] + AHEAD + 1, 0, 0)
            root("n2")

            def ff1_part(p, part, last=False):
                n0 = SLAB["ff"] + PART1 * part
                for k in range(FF1_PART):
                    if part or k >= 2:
                        split(n0 + AHEAD, p, k, PART1)
                    act.wait_ge(h_val, V_AT["ff"] + FF1_PART * part + k + 1 + FF1_PART * p)
                    nc.scalar.activation(h_hi[:, k, :], fbuf[k % 2], ACT.Copy).then_inc(h_hi_ready, 1)
                if last:
                    root_table()
                for m in range(DC):
                    split(n0 + AHEAD, p, FF1_PART + m, PART1)
                    if last and m == DC - 1:
                        split(SLAB["q2"] + AHEAD, 0, 0)
                    if last:
                        act.wait_ge(out_read, OUT["ff"] + PART1 * part + FF1_PART + m + 1)
                        square("post2", m, 0, Fo[:, m, :], m)

            ff1_part(0, 0)
            with act.Fori(0, FF1_PARTS - 2) as p:
                ff1_part(p, 1)
            ff1_part(0, FF1_PARTS - 1, last=True)
            root("post2")
            act.wait_ge(spc_val, 1)
            nc.scalar.activation(spc[:, 2, :], spc[:, 1, :], ACT.Exp).then_inc(spc_exp, 1)
            root_table()
            normalised("n3", "g_mix2", lambda c: act.wait_ge(x_new, X_AT["post2"] + c + 1))
            split(SLAB["q2"] + AHEAD + 1, 0, 0)
            root("n3")

            for n in range(SLAB["q2"] + 2, SLAB["u2"]):
                split(n + AHEAD, 0, 0)

            def inputs2(u):
                if 1 <= u <= DC:
                    act.wait_ge(h_val, V_AT["uc"] + u)
                    nc.scalar.activation(h_hi[:, u - 1, :], UC[:, u - 1, :], ACT.Copy).then_inc(h_hi_ready, 1)
                if u >= DC:
                    m = u - DC
                    act.wait_ge(out_read, OUT["g2"] + m + 1)
                    nc.scalar.activation(G2[:, m, :], G2[:, m, :], ACT.Gelu_apprx_tanh).then_inc(gate_val, 1)
            attention(att2, SLAB["u2"], inputs2)

            act.wait_ge(decay_ready, 1)

            def mix_gate(kind, t):
                row, bias = {"za": (1, 0), "zb": (0, 8)}[kind]
                act.wait_ge(out_read, MIX_OUT[kind, t] + 1)
                nc.scalar.activation(tmp[row], tmp[row], ACT.Sigmoid, bias=col("b_gate", bias + t)).then_inc(gate_val, 1)

            def merged_hi(t):
                act.wait_ge(h_val, V_AT["m2"] + t + 1)
                nc.scalar.activation(h_hi[:, t, :], Q2[:, t, :], ACT.Copy).then_inc(h_hi_ready, 1)

            split(MIX_SLAB["lru", 0] + AHEAD, 0, 0)
            for t in range(DC):
                j = t // 2
                if t:
                    act.wait_ge(lru_free, t)
                for q, (row, name, d) in enumerate(((0, "ba", 0), (1, "bx", 0), (2, "ba", 1), (3, "bx", 1))):
                    o = 4 * t + q
                    if o % 8 < 7:
                        act.wait_ge(lg_done, 7 * j + o % 8 + 1)
                    else:
                        act.wait_ge(half_done, 2 * (MIX_SLAB["lru", j] + 1))
                    nc.scalar.activation(lru[row], mp[:, o % 6, :], ACT.Sigmoid,
                                         bias=col(name, 8 * d + t)).then_inc(lru_sig, 1)
                act.wait_ge(lru_sig, 4 * t + 4)
                for d in range(2):
                    ins = nc.scalar.activation(lru[4 + d], lru[2 * d], ACT.Tanh, scale=decay_tanh[:, 8 * d + t:8 * d + t + 1])
                ins.then_inc(lru_tanh, 1)
                for d in range(2):
                    ins = nc.scalar.activation(lru[2 * d], lru[2 * d], ACT.Exp, scale=decay_exp[:, 8 * d + t:8 * d + t + 1])
                ins.then_inc(lru_act, 1)
                act.wait_ge(lru_mid, t + 1)
                nc.scalar.activation(lru45, lru45, ACT.Sqrt).then_inc(lru_root, 1)
                split(MIX_SLAB["zb", t] + AHEAD, 0, 0)
                if t >= 1:
                    mix_gate("zb", t - 1)
                if t >= 2:
                    mix_gate("za", t - 2)
                if t >= 1:
                    split(MIX_SLAB["za", t - 1] + AHEAD, 0, 0)
                if t >= 3:
                    merged_hi(t - 3)
                if t % 2 and t < DC - 1:
                    split(MIX_SLAB["lru", j + 1] + AHEAD, 0, 0)
            mix_gate("zb", DC - 1)
            mix_gate("za", DC - 2)
            split(MIX_SLAB["za", DC - 1] + AHEAD, 0, 0)
            merged_hi(DC - 3)
            merged_hi(DC - 2)
            mix_gate("za", DC - 1)
            merged_hi(DC - 1)

            root_table()

            def out2_body(i, k):
                split(SLAB["out2"] + AHEAD, i, k)
                act.wait_ge(out_read, OUT["out2"] + k + 1 + 4 * i)
                xc = at(X, k + 4 * i)
                nc.scalar.activation(at(a_hi, k + 4 * i), xc, ACT.Copy, scale=pcol("g_ffn2", k + 4 * i)).then_inc(a_hi_ready, 1)
                square("n4", k, i, xc, k)
            loop(act, 8, out2_body, unroll=8)
            root("n4")

            def ff2_part(p, chunks, slab0):
                for c in range(chunks):
                    split(slab0 + AHEAD, p, 2 * c, PART2)
                    act.wait_ge(out_read, OUT["ff2"] + slab0 - SLAB["ff2"] + 2 * c + 1 + PART2 * p)
                    nc.scalar.activation(tmp[0], tmp[0], ACT.Silu).then_inc(gate_val, 1)
                    split(slab0 + AHEAD, p, 2 * c + 1, PART2)
                    v0 = 8 * ((slab0 - SLAB["ff2"]) // PART2)
                    act.wait_ge(h_val, V_AT["ff2"] + v0 + c + 1 + 8 * p)
                    nc.scalar.activation(h_hi[:, c, :], fbuf[c % 2], ACT.Copy).then_inc(h_hi_ready, 1)
                if chunks != FF2_CHUNKS[0]:
                    root_table()
                for m in range(DC):
                    split(slab0 + AHEAD, p, 2 * chunks + m, PART2)
                    if chunks != FF2_CHUNKS[0]:
                        act.wait_ge(out_read, OUT["ff2"] + slab0 - SLAB["ff2"] + 2 * chunks + m + 1)
                        square("n5", m, 0, X[:, m, :], m)

            with act.Fori(0, 2) as p:
                ff2_part(p, FF2_CHUNKS[0], SLAB["ff2"])
            ff2_part(0, FF2_CHUNKS[2], SLAB["ff2"] + 2 * PART2)
            root("n5")
            for c in SCALED:
                nc.scalar.activation(OUTB[:, c, :], X[:, c, :], ACT.Copy, scale=col("g_fin2", c)).then_inc(gained, 1)

        @block.vector
        def _(dve):
            V = Tally(dve, vec_step)
            TT, TS, STT = dve.tensor_tensor, dve.tensor_scalar, dve.scalar_tensor_tensor

            def split(base, i, k, per=4):
                n = base + k
                if isinstance(i, int) and n >= NSLAB:
                    return
                dve.wait_ge(w_hi_ready, n + 1 + per * i)
                TT(w_lo[:, n % RING, :], raw[:, n % RAW, :], w_hi[:, n % RING, :].bitcast(F32),
                   ALU.subtract).then_inc(w_lo_ready, 1)

            def take(name, i, k, half=None, per=4):
                at_half = 2 * (SLAB[name] + k + 1) if half is None else 2 * SLAB[name] + half
                dve.wait_ge(half_done, at_half + 2 * per * i)
                return gp[:, (OUT[name] + k) % 2, :]

            def clear_sum():
                V.run(dve.memset(ssum, 0.0))

            def add_square(kind, c, i=0):
                dve.wait_ge(sq_done, 8 * NORM[kind] + c + 1 + 4 * i)
                if not isinstance(i, int) or 8 * BY_VEC[kind] + c:
                    dve.wait_ge(sq_added, max(8 * BY_VEC[kind] + c, 0) + 4 * i)
                TT(ssum, ssum, sq[c % 2], ALU.add).then_inc(sq_added, 1)

            def invert_root(kind):
                dve.wait_ge(rms_root, NORM[kind] + 1)
                if kind in WITH_POOL:
                    V.run(dve.reciprocal(by_token, by_token))
                    TT(diag, ident.unsqueeze(1).to_broadcast([P, T // P, P]),
                       by_token.unsqueeze(2).to_broadcast([P, T // P, P]), ALU.mult).then_inc(diag_ready, 1)
                    dve.wait_ge(rms_spread, WITH_POOL.index(kind) + 1)
                    dve.tensor_copy(R[:, :], mp[:, 5, :]).then_inc(inverse_ready, 1)
                    dve.wait_ge(inverse_ready, WITH_POOL.index(kind) + 1)
                else:
                    V.run(dve.reciprocal(R[:, :], R[:, :]))

            def a_low(name, c, i, src, gain=None):
                dve.wait_ge(a_hi_ready, A_AT[name] + c + 1 + 4 * i)
                hi = at(a_hi, c + 4 * i).bitcast(F32)
                lo = at(a_lo, c + 4 * i)
                if gain is None:
                    TT(lo, src, hi, ALU.subtract).then_inc(a_lo_ready, 1)
                else:
                    STT(out=lo, in0=src, scalar=gain, in1=hi, op0=ALU.mult, op1=ALU.subtract).then_inc(a_lo_ready, 1)

            def h_low(count, chunk, src):
                dve.wait_ge(h_hi_ready, count + 1)
                TT(at(h_lo, chunk), src, at(h_hi, chunk).bitcast(F32), ALU.subtract).then_inc(h_lo_ready, 1)

            def normalised(kind, gain):
                for c in range(DC):
                    a_low(kind, c, 0, X[:, c, :], col(gain, c))

            def as_steps(v):
                return v.rearrange("p (b s) -> p s b", s=STEP)

            def in_steps(v):
                return v.rearrange("p (s b) -> p s b", s=STEP)

            lr, li, dt, ld, ang, tmp5, mag, sn, cs = s_w
            def low(c):
                a_low("n1", c, 0, X[:, c, :], col("g_mix_pre", c))

            dve.wait_ge(s_par, 16)
            low(0)
            low(1)
            split(0, 0, 0)
            split(0, 0, 1)
            dve.wait_ge(s_par, 64)
            dve.wait_ge(disc_act, 1)
            V.up(TT(ld, lr, dt, ALU.mult))
            V.run(TT(ang, li, dt, ALU.mult))
            V.run(TS(tmp5, ang, 1.0 / TWO_PI, MAGIC, ALU.mult, ALU.add))
            V.run(TS(tmp5, tmp5, -MAGIC, None, ALU.add))
            V.run(STT(out=ang, in0=tmp5, scalar=-C1, in1=ang, op0=ALU.mult, op1=ALU.add))
            V.run(STT(out=ang, in0=tmp5, scalar=-C2, in1=ang, op0=ALU.mult, op1=ALU.add))
            STT(out=ang, in0=tmp5, scalar=-C3, in1=ang, op0=ALU.mult, op1=ALU.add).then_inc(disc_vec, 1)
            low(2)
            low(3)
            dve.wait_ge(disc_act, 4)
            V.up(TT(rho, mag[:, 0:PAIRS], mag[:, 0:PAIRS], ALU.mult))
            V.run(TT(cs, cs, cs, ALU.mult))
            V.up(TT(rho, rho, rho, ALU.mult))
            V.run(TS(cs, cs, -2.0, 1.0, ALU.mult, ALU.add))
            V.up(TT(d_are, mag, cs, ALU.mult))
            V.run(TT(d_aim, mag, sn, ALU.mult))
            V.up(TT(mag, lr, lr, ALU.mult))
            V.run(TT(cs, li, li, ALU.mult))
            V.up(TS(dt, d_are, -1.0, None, ALU.add))
            V.run(TT(mag, mag, cs, ALU.add))
            low(4)
            low(5)
            V.up(TT(tmp5, dt, lr, ALU.mult))
            low(6)
            V.run(TT(cs, d_aim, li, ALU.mult))
            low(7)
            V.run(dve.reciprocal(mag, mag))
            V.up(TT(sn, d_aim, lr, ALU.mult))
            split(0, 0, 2)
            dve.wait_ge(rms_sum, 1)
            for m in range(2):
                dve.tensor_copy(in_steps(U[:, m, :]), as_steps(take("u", 0, m))).then_inc(out_read, 1)
            V.run(TT(tmp5, tmp5, cs, ALU.add))
            V.up(TT(d_fre, tmp5, mag, ALU.mult))
            V.run(TT(cs, dt, li, ALU.mult))
            V.run(TT(sn, sn, cs, ALU.subtract))
            TT(d_fim, sn, mag, ALU.mult).then_inc(disc_vec, 1)
            split(0, 0, 3)

            s4 = [region(14336 + 512 * i, PAIRS, 32) for i in range(4)]

            def wave():
                dve.wait_ge(disc_vec, 2)
                V.run(TS(rot[:, 1, :], ang[:, 0:PAIRS], STEP / TWO_PI, None, ALU.mult))
                V.run(TS(rot[:, 2, :], rot[:, 1, :], MAGIC, -MAGIC, ALU.add, ALU.add))
                V.run(TT(rot[:, 1, :], rot[:, 1, :], rot[:, 2, :], ALU.subtract))
                V.run(TS(rot[:, 3, :], rot[:, 1, :], float(E0), None, ALU.mult))
                V.run(TS(rot[:, 2, :], rot[:, 3, :], MAGIC, -MAGIC, ALU.add, ALU.add))
                V.run(TT(rot[:, 3, :], rot[:, 3, :], rot[:, 2, :], ALU.subtract))
                for row, half, turns, n in ((e0s, e0c, 1, E0), (e1s, e1c, 3, E1)):
                    V.run(TT(row, rot[:, turns, :].unsqueeze(2).to_broadcast([P, PAIRS, n]),
                             col("iota", 0, n).unsqueeze(1).to_broadcast([P, PAIRS, n]), ALU.mult))
                    V.run(TS(half, row, MAGIC, -MAGIC, ALU.add, ALU.add))
                    ins = TT(row, row, half, ALU.subtract)
                    if n == E0:
                        V.run(ins)
                    else:
                        ins.then_inc(disc_vec, 1)

            def keep_a():
                V.up(dve.tensor_copy(a_re, d_are[:, 0:PAIRS]))
                V.run(dve.tensor_copy(a_im, d_aim[:, 0:PAIRS]))

            def scale_b():
                dve.wait_ge(disc_act, 7)
                V.up(TT(e0c, e0c, e0c, ALU.mult))
                V.run(TT(e1c, e1c, e1c, ALU.mult))
                V.run(TS(e0c, e0c, -2.0, 1.0, ALU.mult, ALU.add))
                TS(e1c, e1c, -2.0, 1.0, ALU.mult, ALU.add).then_inc(cos_ready, 1)
                dve.wait_ge(s_bc, 96)
                fr = d_fre[:, 0:PAIRS].unsqueeze(2).to_broadcast([P, PAIRS, 32])
                fi = d_fim[:, 0:PAIRS].unsqueeze(2).to_broadcast([P, PAIRS, 32])
                V.up(TT(s4[0], fr, b_re, ALU.mult))
                V.up(TT(s4[1], fi, b_im, ALU.mult))
                V.up(TT(s4[2], fr, b_im, ALU.mult))
                V.run(TT(s4[3], fi, b_re, ALU.mult))
                V.up(TT(b_re, s4[0], s4[1], ALU.subtract))
                V.run(TT(b_im, s4[2], s4[3], ALU.add))
                V.run(TS(ca_im[:, 0], ca_im[:, 0], -1.0, None, ALU.mult))

            def c_power(k):
                ar = a_re.unsqueeze(2).to_broadcast([P, PAIRS, 32])
                ai = a_im.unsqueeze(2).to_broadcast([P, PAIRS, 32])
                V.up(TT(s4[0], ca_re[:, k - 1], ar, ALU.mult))
                V.up(TT(s4[1], ca_im[:, k - 1], ai, ALU.mult))
                V.up(TT(s4[2], ca_im[:, k - 1], ar, ALU.mult))
                V.run(TT(s4[3], ca_re[:, k - 1], ai, ALU.mult))
                V.up(TT(ca_re[:, k], s4[0], s4[1], ALU.add))
                if k < STEP:
                    V.run(TT(ca_im[:, k], s4[2], s4[3], ALU.subtract))
                else:
                    TT(ca_im[:, k], s4[2], s4[3], ALU.subtract).then_inc(ca_ready, 1)

            def clear_local():
                dve.wait_ge(ca_ready, 1)
                V.run(dve.memset(kloc, 0.0))

            def local_weights():
                dve.wait_ge(kloc_done, 1)
                for pr in range(4):
                    rows = slice(32 * pr, 32 * pr + 32)
                    ins = dve.tensor_copy(kloc[rows, :, :, rows],
                                          mp[rows, 4, :].rearrange("p (a b c) -> p a b c", a=CT, b=STEP))
                    if pr < 3:
                        V.up(ins)
                ins.then_inc(kloc_ready, 1)

            def scan_states(ct):
                dve.wait_ge(v_done, ct + 1)
                dve.wait_ge(tab_ready, ct + 1)
                cos, sin = tab[ct % 2]
                if ct:
                    dve.wait_ge(st_ready, ct)
                v_re, v_im = mp[:, 0:4, 0:NB], mp[:, 0:4, NB:2 * NB]
                V.up(TT(t1, cos, v_re, ALU.mult))
                V.run(TT(t2, sin, v_im, ALU.mult))
                V.run(TT(g_re, t1, t2, ALU.add))
                V.up(TT(t1, cos, v_im, ALU.mult))
                TT(t2, sin, v_re, ALU.mult).then_inc(v_read, 1)
                dve.wait_ge(v_read, ct + 1)
                V.run(TT(g_im, t1, t2, ALU.subtract))
                for pr in range(4):
                    decay = rho[:, 4 * ct + pr:4 * ct + pr + 1].to_broadcast([P, NB])
                    V.up(dve.tensor_tensor_scan(g_re[:, pr, :], decay, g_re[:, pr, :], 0.0, ALU.mult, ALU.add))
                    V.up(dve.tensor_tensor_scan(g_im[:, pr, :], decay, g_im[:, pr, :], 0.0, ALU.mult, ALU.add))
                V.settle()

            def turn_states(ct):
                cos, sin = tab[ct % 2]
                V.up(TT(t1, cos, g_re, ALU.mult))
                V.run(TT(t2, sin, g_im, ALU.mult))
                if ct:
                    dve.wait_ge(y_done, ct)
                V.run(TT(st_re, t1, t2, ALU.subtract))
                V.up(TT(t1, cos, g_im, ALU.mult))
                V.run(TT(t2, sin, g_re, ALU.mult))
                TT(st_im, t1, t2, ALU.add).then_inc(st_ready, 1)

            def ssm_out(ct):
                dve.wait_ge(y_done, ct + 1)
                STT(out=zp.rearrange("p (b s) -> p s b", s=STEP), in0=U[:, ct, :].rearrange("p (s b) -> p s b", s=STEP),
                    scalar=col("d_skip", ct), in1=mp[:, 5, :].rearrange("p (s b) -> p s b", s=STEP),
                    op0=ALU.mult, op1=ALU.add).then_inc(y_val, 1)

            def z_low(ct):
                h_low(H_AT["z"] + ct, 4 + ct, U[:, ct, :])

            after = {n: [] for n in range(SLAB["gate_s"])}
            after[2].append(wave)
            after[3].append(scale_b)
            for k in range(1, STEP + 1):
                after[3 + k].append(lambda k=k: c_power(k))
            for ct in range(CT):
                after[SSM_IN[ct]].append(lambda ct=ct: scan_states(ct))
                after[SSM_IN[ct] + 1].append(lambda ct=ct: turn_states(ct))
            after[8].append(clear_local)
            after[9].append(local_weights)
            for ct in range(CT):
                after[SSM_OUT[ct] + 1].insert(0, lambda ct=ct: ssm_out(ct))
                after[min(SSM_OUT[ct] + 2, 17)].append(lambda ct=ct: z_low(ct))
            keep_a()
            invert_root("n1")
            dve.wait_ge(out_read, 2)
            for m in range(2):
                V.up(TT(in_steps(U[:, m, :]), in_steps(U[:, m, :]), as_steps(R[:, :]), ALU.mult))
            V.settle()
            for name in ("u", "k", "v", "gate_a", "q"):
                for m in range(2 if name == "u" else 0, COUNT[name]):
                    split(SLAB[name] + AHEAD, 0, m)
                    src, r = take(name, 0, m), R[:, :]
                    if name == "u":
                        dst, src, r = in_steps(U[:, m, :]), as_steps(src), as_steps(r)
                    else:
                        dst = {"k": KV[:, 0, :], "v": KV[:, 1, :], "gate_a": gate1[:, m, :], "q": Q[:, min(m, 3), :]}[name]
                    if name == "gate_a" and m == 0:
                        dve.wait_ge(win_ready, 1)
                    if name == "q" and m == 0:
                        dve.wait_ge(v_done, CT // 2)
                    TT(dst, src, r, ALU.mult).then_inc(out_read, 1)
                    if name == "q" and m == 2:
                        dve.wait_ge(s_bias, 16)
                        bflat = bias8.rearrange("p a b -> p (a b)")
                        V.run(TS(bflat, bflat, 8.0, None, ALU.mult))
                    for piece in after[SLAB[name] + m]:
                        piece()

            def attention(A, between):
                def logits(u):
                    row, L = mini[u % 2], A.logit[u % 2]
                    b, pp, p = A.units[u]
                    lo, hi = A.span(u)
                    kv = 2 * pp + p
                    dve.wait_ge(sc_done, A.u0 + u + 1)
                    if u >= 2:
                        dve.wait_ge(pt_done, A.done[u - 2])
                    sc = A.scores()
                    if A.name:
                        TT(L[:, :, lo:hi], sc[:, :, lo:hi], bias8[:, 4 * kv:4 * kv + 4, lo:hi], ALU.add).then_inc(lg_ready, 1)
                    else:
                        for h in range(4):
                            slope = 8.0 * 2.0 ** (-8.0 * (4 * kv + h + 1) / 16)
                            ins = STT(out=L[:, h, lo:hi], in0=nd8[:, lo:hi], scalar=slope, in1=sc[:, h, lo:hi],
                                      op0=ALU.mult, op1=ALU.add)
                            if h < 3:
                                V.up(ins)
                        ins.then_inc(lg_ready, 1)
                    dve.wait_ge(lg_ready, A.u0 + u + 1)
                    sink = col(A.sinks, 4 * kv, 4)
                    V.run(dve.tensor_reduce(row[:, 0, :], L[:, :, lo:hi], AX.X, ALU.max))
                    V.run(STT(out=row[:, 0, :], in0=sink, scalar=8.0, in1=row[:, 0, :], op0=ALU.mult, op1=ALU.max))
                    V.run(TS(row[:, 1, :], row[:, 0, :], -0.125, None, ALU.mult))
                    TT(row[:, 2, :], sink, row[:, 1, :], ALU.add).then_inc(nb_ready, 1)

                def probabilities(u):
                    row, L = mini[u % 2], A.logit[u % 2]
                    lo, hi = A.span(u)
                    dve.wait_ge(ex_done, A.u0 + u + 1)
                    V.run(TT(row[:, 5, :], row[:, 3, :], row[:, 4, :], ALU.add))
                    V.run(dve.reciprocal(row[:, 5, :], row[:, 5, :]))
                    TT(L[:, :, lo:hi], L[:, :, lo:hi], row[:, 5, :].unsqueeze(2).to_broadcast([P, 4, hi - lo]),
                       ALU.mult).then_inc(pr_ready, 1)

                def outputs(u):
                    p = A.units[u][2]
                    o = mp[HD * p:HD * p + HD, 5, :].rearrange("p (h q) -> p h q", h=4)
                    dve.wait_ge(at_done, A.u0 + u + 1)
                    if A.name:
                        dve.wait_ge(h_hi_ready, H_AT["y1"] + u + 1)
                        TT(A.out_ap(h_lo, u), o, A.out_ap(h_hi, u).bitcast(F32), ALU.subtract).then_inc(h_lo_ready, 1)
                    else:
                        dve.tensor_copy(A.out_ap(Q2, u), o).then_inc(at_read, 1)

                n = len(A.units)
                logits(0)
                logits(1)
                probabilities(0)
                between(0)
                for u in range(n):
                    if u + 1 < n:
                        probabilities(u + 1)
                    if u:
                        outputs(u - 1)
                    if u + 2 < n:
                        logits(u + 2)
                    if u + 1 < n:
                        between(u + 1)
                outputs(n - 1)

            def evacuate(name, m, dst):
                split(SLAB[name] + AHEAD, 0, m)
                TT(dst, take(name, 0, m), R[:, :], ALU.mult).then_inc(out_read, 1)

            attention(att1, lambda u: evacuate("gate_s", u, gate2[:, u, :]))

            for j in range(COUNT["branch_a"]):
                split(SLAB["branch_a"] + AHEAD, 0, j)
                for m in (2 * j, 2 * j + 1):
                    src = take("branch_a", 0, m, half=m + 1)
                    dve.wait_ge(gate_val, G_AT["gate_a"] + m + 1)
                    TT(gate1[:, m, :], src, gate1[:, m, :], ALU.mult).then_inc(out_read, 1)

            for j in range(COUNT["glu"]):
                split(SLAB["glu"] + AHEAD, 0, j)
                for m in (2 * j, 2 * j + 1):
                    dve.wait_ge(glu_sig, m + 1)
                    TT(U[:, m, :], U[:, m, :], tmp[m % 2], ALU.mult).then_inc(out_read, 1)
                    h_low(H_AT["z2"] + m, m, U[:, m, :])
            for j in range(COUNT["branch_s"]):
                split(SLAB["branch_s"] + AHEAD, 0, j)
                for m in (2 * j, 2 * j + 1):
                    src = take("branch_s", 0, m, half=m + 1)
                    dve.wait_ge(gate_val, G_AT["gate_s"] + m + 1)
                    TT(tmp[m % 2], src, gate2[:, m, :], ALU.mult).then_inc(out_read, 1)
                    dve.wait_ge(out_read, OUT["branch_s"] + m + 1)
                    TT(gate1[:, m, :], gate1[:, m, :], tmp[m % 2], ALU.add).then_inc(m_val, 1)
                    a_low("merged", m, 0, gate1[:, m, :])

            clear_sum()

            def out_body(i, k):
                split(SLAB["out"] + AHEAD, i, k)
                if k == DC - 1:
                    split(SLAB["ff"] + AHEAD, 0, 0)
                add_square("post1", k, i)
                TS(at(Y, k + 4 * i), take("out", i, k), pcol("g_mix_post", k + 4 * i), None,
                   ALU.mult).then_inc(out_read, 1)
            loop(dve, 8, out_body, unroll=8)
            invert_root("post1")
            dve.wait_ge(s_x2, 16)
            dve.wait_ge(out_read, OUT["out"] + DC)
            for c in range(DC + 1):
                if c in SCALED:
                    dve.wait_ge(scaled, SCALED.index(c) + 1)
                    TT(X[:, c, :], X[:, c, :], Y[:, c, :], ALU.add).then_inc(x_new, 1)
                elif c < DC:
                    V.run(TT(tmp[c % 2], Y[:, c, :], R[:, :], ALU.mult))
                    TT(X[:, c, :], X[:, c, :], tmp[c % 2], ALU.add).then_inc(x_new, 1)
                if c:
                    a_low("n2", c - 1, 0, X[:, c - 1, :], col("g_mlp_pre", c - 1))

            def ff1_part(p, part, last=False):
                s0 = PART1 * part

                def relu_squared(k):
                    STT(out=fbuf[k % 2], in0=tmp[k % 2], scalar=0.0, in1=tmp[k % 2], op0=ALU.max,
                        op1=ALU.mult).then_inc(h_val, 1)

                def low(k):
                    h_low(H_AT["ff"] + FF1_PART * part + k + FF1_PART * p, k, fbuf[k % 2])

                for k in range(FF1_PART):
                    if part == 0 and k < 2:
                        if k == 0:
                            split(SLAB["ff"] + AHEAD + 1, 0, 0)
                            for e in range(2):
                                dve.tensor_copy(tmp[e], take("ff", 0, e)).then_inc(out_read, 1)
                            invert_root("n2")
                            dve.wait_ge(out_read, OUT["ff"] + 2)
                        V.run(TT(tmp[k], tmp[k], R[:, :], ALU.mult))
                    else:
                        split(SLAB["ff"] + AHEAD, p, s0 + k, PART1)
                        TT(tmp[k % 2], take("ff", p, s0 + k, per=PART1), R[:, :], ALU.mult).then_inc(out_read, 1)
                        dve.wait_ge(out_read, OUT["ff"] + s0 + k + 1 + PART1 * p)
                    relu_squared(k)
                    if k:
                        low(k - 1)
                low(FF1_PART - 1)
                if last:
                    clear_sum()
                for m in range(DC):
                    split(SLAB["ff"] + AHEAD, p, s0 + FF1_PART + m, PART1)
                    if last and m == DC - 1:
                        split(SLAB["q2"] + AHEAD, 0, 0)
                    src = take("ff", p, s0 + FF1_PART + m, per=PART1)
                    if part == 0:
                        dve.tensor_copy(Fo[:, m, :], src).then_inc(out_read, 1)
                    else:
                        TT(Fo[:, m, :], Fo[:, m, :], src, ALU.add).then_inc(out_read, 1)
                    if last and m:
                        add_square("post2", m - 1)
                if last:
                    add_square("post2", DC - 1)

            ff1_part(0, 0)
            with dve.Fori(0, FF1_PARTS - 2) as p:
                ff1_part(p, 1)
            ff1_part(0, FF1_PARTS - 1, last=True)
            lam = col("lam", 0, 16)
            r = [spc[:, i, :] for i in range(12)]
            V.run(TS(r[0], lam, -1.0, None, ALU.mult))
            V.run(TT(r[1], r[0], lam, ALU.min))
            TS(r[0], r[0], 0.0, None, ALU.max).then_inc(spc_val, 1)
            invert_root("post2")
            dve.wait_ge(out_read, OUT["ff"] + PART1 * FF1_PARTS)
            for c in range(DC + 1):
                if c in SCALED:
                    dve.wait_ge(scaled, len(SCALED) + SCALED.index(c) + 1)
                    STT(out=X[:, c, :], in0=Fo[:, c, :], scalar=col("g_mlp_post", c), in1=X[:, c, :],
                        op0=ALU.mult, op1=ALU.add).then_inc(x_new, 1)
                elif c < DC:
                    V.run(STT(out=tmp[c % 2], in0=Fo[:, c, :], scalar=col("g_mlp_post", c), in1=R[:, :],
                              op0=ALU.mult, op1=ALU.mult))
                    TT(X[:, c, :], X[:, c, :], tmp[c % 2], ALU.add).then_inc(x_new, 1)
                if c:
                    a_low("n3", c - 1, 0, X[:, c - 1, :], col("g_mix2", c - 1))

            split(SLAB["q2"] + AHEAD + 1, 0, 0)
            for m in range(2):
                dve.tensor_copy(Q2[:, m, :], take("q2", 0, m)).then_inc(out_read, 1)
            invert_root("n3")
            dve.wait_ge(out_read, OUT["q2"] + 2)
            for m in range(2):
                V.up(TT(Q2[:, m, :], Q2[:, m, :], R[:, :], ALU.mult))
            for m in range(2, DC):
                evacuate("q2", m, Q2[:, m, :])
            for m in range(2):
                evacuate("k2", m, KV2[:, m, :])
            for m in range(2):
                evacuate("v2", m, KV2[:, 2 + m, :])
            dve.wait_ge(spc_exp, 1)
            V.run(TS(r[3], r[2], 2.0, None, ALU.add))
            V.run(dve.reciprocal(r[3], r[3]))
            V.run(TT(r[3], r[3], r[2], ALU.mult))
            V.run(TT(r[4], r[3], r[3], ALU.mult))
            V.run(TS(r[5], r[4], 1.0 / 17, None, ALU.mult))
            for d in (15, 13, 11, 9, 7, 5, 3):
                V.run(STT(out=r[5], in0=r[5], scalar=1.0 / d, in1=r[4], op0=ALU.add, op1=ALU.mult))
            V.run(STT(out=r[5], in0=r[5], scalar=1.0, in1=r[3], op0=ALU.add, op1=ALU.mult))
            V.run(STT(out=r[5], in0=r[5], scalar=2.0, in1=r[0], op0=ALU.mult, op1=ALU.add))
            V.up(TS(decay_exp, r[5], -8.0, None, ALU.mult))
            TS(decay_tanh, r[5], 4.0, None, ALU.mult).then_inc(decay_ready, 1)

            def inputs2(u):
                if u >= DC:
                    evacuate("g2", u - DC, G2[:, u - DC, :])
                    if u == DC:
                        h_low(H_AT["uc"] + u - 1, u - 1, UC[:, u - 1, :])
                    return
                x, y = tmp[u % 2], UC[:, u, :]
                evacuate("u2", u, x)
                dve.wait_ge(out_read, OUT["u2"] + u + 1)
                V.run(TS(y, x, pcol("conv_w", 16 + u), pcol("conv_b", u), ALU.mult, ALU.add))
                V.run(STT(out=y[:, 2:T], in0=x[:, 0:T - 2], scalar=pcol("conv_w", u), in1=y[:, 2:T],
                          op0=ALU.mult, op1=ALU.add))
                V.run(STT(out=y[:, 1:T], in0=x[:, 0:T - 1], scalar=pcol("conv_w", 8 + u), in1=y[:, 1:T],
                          op0=ALU.mult, op1=ALU.add))
                STT(out=y[:, 0:T - 1], in0=x[:, 1:T], scalar=pcol("conv_w", 24 + u), in1=y[:, 0:T - 1],
                    op0=ALU.mult, op1=ALU.add).then_inc(h_val, 1)
                if u:
                    h_low(H_AT["uc"] + u - 1, u - 1, UC[:, u - 1, :])

            dve.wait_ge(decay_ready, 1)
            dve.wait_ge(s_nd, 16)
            attention(att2, inputs2)
            dve.wait_ge(gate_val, G_AT["g2"] + DC)
            dve.wait_ge(at_read, len(att2.units))

            def gate_product(kind, t, row):
                split(MIX_SLAB[kind, t] + AHEAD, 0, 0)
                dve.wait_ge(half_done, 2 * (MIX_SLAB[kind, t] + 1))
                TT(row, gp[:, MIX_OUT[kind, t] % 2, :], R[:, :], ALU.mult).then_inc(out_read, 1)

            def gated_attention(t):
                dve.wait_ge(gate_val, MIX_VAL["zb", t])
                V.run(TT(Q2[:, t, :], Q2[:, t, :], tmp[0], ALU.mult))

            def merged(t):
                dve.wait_ge(gate_val, MIX_VAL["za", t])
                V.run(TT(HS[:, t, :], HS[:, t, :], tmp[1], ALU.mult))
                TT(Q2[:, t, :], Q2[:, t, :], HS[:, t, :], ALU.add).then_inc(h_val, 1)

            def merged_low(t):
                h_low(H_AT["m2"] + t, t, Q2[:, t, :])

            split(MIX_SLAB["lru", 0] + AHEAD, 0, 0)
            for t in range(DC):
                dve.wait_ge(lru_tanh, t + 1)
                TS(lru45, lru45, 0.0, None, ALU.max).then_inc(lru_mid, 1)
                for d in range(2):
                    V.up(TT(lru[1 + 2 * d], lru[1 + 2 * d], UC[:, t, :], ALU.mult))
                dve.wait_ge(lru_root, t + 1)
                for d in range(2):
                    V.up(STT(out=lru[4 + d], in0=lru[2 * d], scalar=1.0, in1=lru[4 + d], op0=ALU.add, op1=ALU.mult))
                V.settle()
                for d in range(2):
                    V.up(TT(lru[1 + 2 * d], lru[1 + 2 * d], lru[4 + d], ALU.mult))
                V.settle()
                V.up(dve.tensor_tensor_scan(HS[:, t, :], lru[0], lru[1], 0.0, ALU.mult, ALU.add))
                V.run(dve.tensor_tensor_scan(lru[5][:, ::-1], lru[2][:, ::-1], lru[3][:, ::-1], 0.0, ALU.mult, ALU.add))
                TT(HS[:, t, :], HS[:, t, :], lru[5], ALU.add).then_inc(lru_free, 1)
                if t >= 1:
                    gated_attention(t - 1)
                gate_product("zb", t, tmp[0])
                dve.wait_ge(lru_free, t + 1)
                V.run(TT(HS[:, t, :], HS[:, t, :], G2[:, t, :], ALU.mult))
                if t >= 2:
                    merged(t - 2)
                if t >= 1:
                    gate_product("za", t - 1, tmp[1])
                if t >= 3:
                    merged_low(t - 3)
                if t % 2 and t < DC - 1:
                    split(MIX_SLAB["lru", t // 2 + 1] + AHEAD, 0, 0)
            gated_attention(DC - 1)
            merged(DC - 2)
            gate_product("za", DC - 1, tmp[1])
            merged_low(DC - 3)
            merged_low(DC - 2)
            merged(DC - 1)
            merged_low(DC - 1)

            clear_sum()

            def out2_body(i, k):
                split(SLAB["out2"] + AHEAD, i, k)
                xc = at(X, k + 4 * i)
                TT(xc, xc, take("out2", i, k), ALU.add).then_inc(out_read, 1)
                a_low("n4", k, i, xc, pcol("g_ffn2", k + 4 * i))
                add_square("n4", k, i)
            loop(dve, 8, out2_body)
            invert_root("n4")

            def ff2_part(p, chunks, slab0):
                s0 = slab0 - SLAB["ff2"]
                v0 = 8 * (s0 // PART2)
                for c in range(chunks):
                    for e in range(2):
                        split(slab0 + AHEAD, p, 2 * c + e, PART2)
                        TT(tmp[e], take("ff2", p, s0 + 2 * c + e, per=PART2), R[:, :], ALU.mult).then_inc(out_read, 1)
                    dve.wait_ge(out_read, OUT["ff2"] + s0 + 2 * c + 2 + PART2 * p)
                    dve.wait_ge(gate_val, G_AT["ff2"] + v0 + c + 1 + 8 * p)
                    TT(fbuf[c % 2], tmp[0], tmp[1], ALU.mult).then_inc(h_val, 1)
                    for q in ([c - 1] if c else []) + ([c] if c == chunks - 1 else []):
                        h_low(H_AT["ff2"] + v0 + q + 8 * p, q, fbuf[q % 2])
                for m in range(DC):
                    split(slab0 + AHEAD, p, 2 * chunks + m, PART2)
                    src = take("ff2", p, s0 + 2 * chunks + m, per=PART2)
                    TT(X[:, m, :], X[:, m, :], src, ALU.add).then_inc(out_read, 1)
                    if chunks != FF2_CHUNKS[0]:
                        add_square("n5", m)

            with dve.Fori(0, 2) as p:
                ff2_part(p, FF2_CHUNKS[0], SLAB["ff2"])
            clear_sum()
            ff2_part(0, FF2_CHUNKS[2], SLAB["ff2"] + 2 * PART2)
            invert_root("n5")
            for c in range(SCALED[0]):
                STT(out=OUTB[:, c, :], in0=X[:, c, :], scalar=col("g_fin2", c), in1=R[:, :], op0=ALU.mult,
                    op1=ALU.mult).then_inc(x_new, 1)

        @block.tensor
        def _(pe):
            def gemm(base, i, k, tiles, outs, x_hi, x_lo, out0, ready=None, per=4):
                n = base + k
                pe.wait_ge(w_lo_ready, n + 1 + per * i)
                for e in range(outs):
                    o = out0 + outs * k + e
                    if o >= 2:
                        pe.wait_ge(out_read, o - 1 + outs * per * i)
                    bank = gp[:, o % 2, :]
                    for t in range(tiles):
                        if ready:
                            ready(t)
                        cols = slice((e * tiles + t) * P, (e * tiles + t + 1) * P)
                        hi, lo = w_hi[:, n % RING, cols], w_lo[:, n % RING, cols]
                        pe.matmul(bank, hi, x_hi(t), start=t == 0, stop=False)
                        pe.matmul(bank, hi, x_lo(t), start=False, stop=False)
                        ins = pe.matmul(bank, lo, x_hi(t), start=False, stop=t == tiles - 1)
                    ins.then_inc(half_done, 2 // outs)

            def a(t):
                return a_hi[:, t, :]

            def al(t):
                return a_lo[:, t, :]

            def h(t):
                return h_hi[:, t, :]

            def hl(t):
                return h_lo[:, t, :]

            def mean_square(kind):
                if kind in BY_POOL:
                    pe.wait_ge(sq_summed, 8 * BY_POOL[kind] + 8)
                else:
                    pe.wait_ge(sq_added, 8 * BY_VEC[kind] + 8)
                if kind in WITH_POOL:
                    for b in range(T // P):
                        ins = pe.matmul(mp[:, 5, b:b + 1], ssum[:, b * P:(b + 1) * P], ones[:, 0:1], start=True,
                                        stop=True)
                    ins.then_inc(rms_sum, 1)
                    pe.wait_ge(diag_ready, WITH_POOL.index(kind) + 1)
                    pe.matmul(mp[:, 5, :], ones, diag.rearrange("p a b -> p (a b)"), start=True,
                              stop=True).then_inc(rms_spread, 1)
                    return
                pe.matmul(mp[:, 5, :], ones, ssum, start=True, stop=True).then_inc(rms_sum, 1)

            def a_stage(name, i, k, ready=None):
                gemm(SLAB[name], i, k, 8, 1, a, al, OUT[name], ready)

            def start_stage(name, kind):
                banks = []
                for e in range(2):
                    pe.wait_ge(w_lo_ready, SLAB[name] + e + 1)
                    o = OUT[name] + e
                    if o >= 2:
                        pe.wait_ge(out_read, o - 1)
                    banks.append(gp[:, o % 2, :])
                for c in range(DC):
                    pe.wait_ge(a_lo_ready, A_AT[kind] + c + 1)
                    for e in range(2):
                        place, cols = (SLAB[name] + e) % RING, slice(c * P, (c + 1) * P)
                        hi, lo = w_hi[:, place, cols], w_lo[:, place, cols]
                        pe.matmul(banks[e], hi, a(c), start=c == 0, stop=False)
                        pe.matmul(banks[e], hi, al(c), start=False, stop=False)
                        ins = pe.matmul(banks[e], lo, a(c), start=False, stop=c == DC - 1)
                        if c == DC - 1:
                            ins.then_inc(half_done, 2)
                mean_square(kind)

            def a_wait(name):
                return lambda t: pe.wait_ge(a_lo_ready, A_AT[name] + t + 1)

            def inputs(ct):
                pe.wait_ge(out_read, OUT["u"] + CT)
                pe.wait_ge(win_ready, 1)
                if ct:
                    pe.wait_ge(v_read, ct)
                for part in range(2):
                    for s in range(STEP):
                        for pr in range(4):
                            rows = slice(32 * pr, 32 * pr + 32)
                            ins = pe.matmul(mp[:, pr, part * NB:(part + 1) * NB], win[rows, ct, s, part, :],
                                            U[rows, ct, s * NB:(s + 1) * NB], start=s == 0, stop=s == STEP - 1)
                ins.then_inc(v_done, 1)

            def local_products():
                pe.wait_ge(ca_ready, 1)
                for ct in range(CT):
                    for pr in range(4):
                        rows, q = slice(32 * pr, 32 * pr + 32), 4 * ct + pr
                        bank = mp[rows, 4, ct * STEP * 32:(ct + 1) * STEP * 32]
                        pe.matmul(bank, b_re[:, q, :], ca_re[:, 0:STEP, q, :], start=True, stop=False)
                        ins = pe.matmul(bank, b_im[:, q, :], ca_im[:, 0:STEP, q, :], start=False, stop=True)
                ins.then_inc(kloc_done, 1)

            def outputs(ct):
                pe.wait_ge(kloc_ready, 1)
                pe.wait_ge(st_ready, ct + 1)
                if ct:
                    pe.wait_ge(y_val, ct)
                for k in range(STEP):
                    pe.matmul(mp[:, 5, k * NB:T], kloc[:, ct, k, :], U[:, ct, 0:T - k * NB], start=k == 0, stop=False,
                              skip_group_check=True)
                for pr in range(4):
                    rows, q = slice(32 * pr, 32 * pr + 32), 4 * ct + pr
                    for s in range(STEP):
                        bank = mp[rows, 5, s * NB + 1:(s + 1) * NB]
                        pe.matmul(bank, ca_re[:, s + 1, q, :], st_re[:, pr, 0:NB - 1], start=False, stop=False,
                                  skip_group_check=True)
                        ins = pe.matmul(bank, ca_im[:, s + 1, q, :], st_im[:, pr, 0:NB - 1], start=False,
                                        stop=s == STEP - 1, skip_group_check=True)
                ins.then_inc(y_done, 1)

            def transpose_values(A):
                for pp in range(A.pairs):
                    for b in range(T // P):
                        ins = pe.transpose(mp[:, 3 + pp, b * P:(b + 1) * P], A.kt[:, A.v0 + pp, b * P:(b + 1) * P], ident)
                    ins.then_inc(vt_done, 1)

            def attention(A, between):
                def scores(u):
                    b, pp, p = A.units[u]
                    rows = slice(HD * p, HD * p + HD)
                    if A.u0 + u:
                        pe.wait_ge(lg_ready, A.u0 + u)
                    for h4 in range(4):
                        for g, j, kb in A.chunks[u]:
                            ins = pe.matmul(A.scores()[:, h4, j * P:(j + 1) * P], A.q[rows, 4 * pp + h4, b * P:(b + 1) * P],
                                            A.kt[rows, A.k0 + pp, kb * P:(kb + 1) * P], start=True, stop=True)
                    ins.then_inc(sc_done, 1)

                n = len(A.units)
                scores(0)
                scores(1)
                between(0)
                pe.wait_ge(vt_ready, A.pairs + (A.u0 > 0))
                for u in range(n):
                    b, pp, p = A.units[u]
                    pe.wait_ge(pr_ready, A.u0 + u + 1)
                    for x, (g, j, kb) in enumerate(A.chunks[u]):
                        if x == 2 and u + 2 < n:
                            scores(u + 2)
                        if g >= 2:
                            pe.wait_ge(pt_ready, g - 1)
                        for h4 in range(4):
                            ins = pe.transpose(mp[:, 3 + g % 2, h4 * P:(h4 + 1) * P],
                                               A.logit[u % 2][:, h4, j * P:(j + 1) * P], ident)
                        ins.then_inc(pt_done, 1)
                    if u + 2 < n and len(A.chunks[u]) < 3:
                        scores(u + 2)
                    if u + 1 < n:
                        between(u + 1)
                    if u:
                        if A.name:
                            pe.wait_ge(h_lo_ready, H_AT["y1"] + u)
                        else:
                            pe.wait_ge(at_read, u)
                    for x, (g, j, kb) in enumerate(A.chunks[u]):
                        pe.wait_ge(pt_ready, g + 1)
                        ins = pe.matmul(mp[HD * p:HD * p + HD, 5, :], A.vt[:, pp, kb, HD * p:HD * p + HD],
                                        A.pt[:, j, :], start=x == 0, stop=x == len(A.chunks[u]) - 1)
                    ins.then_inc(at_done, 1)

            start_stage("u", "n1")
            for n in range(2, SLAB["gate_s"]):
                gemm(0, 0, n, 8, 1, a, al, 0)
                if n == 8:
                    local_products()
                if n in SSM_IN:
                    inputs(SSM_IN.index(n))
                if n in SSM_OUT:
                    outputs(SSM_OUT.index(n))
            transpose_values(att1)
            pe.wait_ge(out_read, OUT["q"] + 4)
            pe.wait_ge(y_val, CT)
            attention(att1, lambda u: a_stage("gate_s", 0, u))
            pe.wait_ge(h_lo_ready, H_AT["y1"] + len(att1.units))
            for j in range(COUNT["branch_a"]):
                gemm(SLAB["branch_a"], 0, j, 4, 2, h, hl, OUT["branch_a"])
            for j in range(COUNT["glu"]):
                gemm(SLAB["glu"], 0, j, 4, 2, lambda t: h(4 + t), lambda t: hl(4 + t), OUT["glu"])
            for j in range(COUNT["branch_s"]):
                gemm(SLAB["branch_s"], 0, j, 4, 2, h, hl, OUT["branch_s"],
                     (lambda t: pe.wait_ge(h_lo_ready, H_AT["z2"] + t + 1)) if j == 0 else None)
            for k in range(DC):
                a_stage("out", 0, k, a_wait("merged") if k == 0 else None)
            mean_square("post1")

            def ff1_part(p, part):
                s0, h0 = PART1 * part, H_AT["ff"] + FF1_PART * part
                for k in range(2 if part == 0 else 0, FF1_PART):
                    gemm(SLAB["ff"], p, s0 + k, 8, 1, a, al, OUT["ff"], per=PART1)
                for m in range(DC):
                    gemm(SLAB["ff"], p, s0 + FF1_PART + m, FF1_PART, 1, h, hl, OUT["ff"],
                         (lambda t: pe.wait_ge(h_lo_ready, h0 + t + 1 + FF1_PART * p)) if m == 0 else None,
                         per=PART1)

            start_stage("ff", "n2")
            ff1_part(0, 0)
            with pe.Fori(0, FF1_PARTS - 2) as p:
                ff1_part(p, 1)
            ff1_part(0, FF1_PARTS - 1)
            mean_square("post2")

            start_stage("q2", "n3")
            for k in range(2, DC):
                a_stage("q2", 0, k)
            for name in ("k2", "v2"):
                for k in range(COUNT[name]):
                    a_stage(name, 0, k)
            pe.wait_ge(out_read, OUT["v2"] + 2)
            transpose_values(att2)
            attention(att2, lambda u: a_stage("u2", 0, u) if u < DC else a_stage("g2", 0, u - DC))

            def recurrence_gates(j):
                n = MIX_SLAB["lru", j]
                pe.wait_ge(w_lo_ready, n + 1)
                for q in range(8):
                    o = 8 * j + q
                    if o >= 6:
                        pe.wait_ge(lru_sig, o - 5)
                    elif o == 0:
                        pe.wait_ge(at_read, len(att2.units))
                    t, cols = o // 4, slice(q * P, (q + 1) * P)
                    hi, lo = w_hi[:, n % RING, cols], w_lo[:, n % RING, cols]
                    pe.matmul(mp[:, o % 6, :], hi, h(t), start=True, stop=False)
                    pe.matmul(mp[:, o % 6, :], hi, hl(t), start=False, stop=False)
                    ins = pe.matmul(mp[:, o % 6, :], lo, h(t), start=False, stop=True)
                    if q < 7:
                        ins.then_inc(lg_done, 1)
                    else:
                        ins.then_inc(half_done, 2)

            for kind, t in MIX:
                if kind == "lru":
                    recurrence_gates(t)
                else:
                    gemm(MIX_SLAB[kind, t], 0, 0, 8, 1, a, al, MIX_OUT[kind, t])
            for k in range(DC):
                gemm(SLAB["out2"], 0, k, 8, 1, h, hl, OUT["out2"],
                     (lambda t: pe.wait_ge(h_lo_ready, H_AT["m2"] + t + 1)) if k == 0 else None)

            def ff2_part(chunks, slab0):
                s0 = slab0 - SLAB["ff2"]
                v0 = 8 * (s0 // PART2)
                for k in range(2 * chunks):
                    gemm(SLAB["ff2"], 0, s0 + k, 8, 1, a, al, OUT["ff2"], a_wait("n4") if s0 + k == 0 else None)
                    if s0 + k == 0:
                        mean_square("n4")
                for m in range(DC):
                    gemm(SLAB["ff2"], 0, s0 + 2 * chunks + m, chunks, 1, h, hl, OUT["ff2"],
                         (lambda t: pe.wait_ge(h_lo_ready, H_AT["ff2"] + v0 + t + 1)) if m == 0 else None)

            for part, chunks in enumerate(FF2_CHUNKS):
                ff2_part(chunks, SLAB["ff2"] + part * PART2)
            mean_square("n5")


def tiles_of(w, order_in=None, order_out=None):
    if order_in is not None:
        w = w.reshape(-1, HD, w.shape[1])[np.array(order_in)].reshape(w.shape)
    if order_out is not None:
        w = w.reshape(w.shape[0], -1, HD)[:, np.array(order_out)].reshape(w.shape)
    k, n = w.shape[0] // P, w.shape[1] // P
    return w.reshape(k, P, n, P).transpose(2, 0, 1, 3)


def lay_out(v):
    f = {k: np.asarray(a)[0] if a.ndim > 1 and a.shape[0] == 1 else np.asarray(a) for k, a in v.items()}
    stream = []

    def put(tiles):
        tiles = tiles.reshape(-1, tiles.shape[-3], P, P)
        per = tiles.shape[1] if tiles.shape[1] > 4 else 8
        tiles = tiles.reshape(-1, per, P, P)
        slab = np.zeros((tiles.shape[0], P, TILES, P), tiles.dtype)
        slab[:, :, :per] = tiles.transpose(0, 2, 1, 3)
        stream.append(slab.reshape(-1, P, TILES * P))

    w = f["w_in"]
    q, k, v1, u, ga, gs = np.split(w, [512, 640, 768, 1280, 2304], axis=1)
    for part in (u, k, v1, ga):
        put(tiles_of(part))
    put(tiles_of(q, None, HEADS1))
    put(tiles_of(gs))
    put(tiles_of(f["w_attn_branch"], HEADS1))
    put(tiles_of(f["w_glu"]))
    put(tiles_of(f["w_ssm_branch"]))
    put(tiles_of(f["w_out"]))
    wi, wo = tiles_of(f["w_ff_in"]), tiles_of(f["w_ff_out"])
    for p in range(FF1_PARTS):
        c = slice(p * FF1_PART, (p + 1) * FF1_PART)
        put(wi[c])
        put(wo[:, c])
    u, g, q, k, v1, za, zb = np.split(f["w_in_2"], [1024, 2048, 3072, 3328, 3584, 4608], axis=1)
    put(tiles_of(q, None, HEADS2))
    put(tiles_of(k))
    put(tiles_of(v1))
    put(tiles_of(u, None, HEADS2))
    put(tiles_of(g, None, HEADS2))
    gates = np.zeros((DC, 2, 2, P, P), np.float32)
    order = np.array(HEADS2).reshape(DC, 2)
    for half in range(2):
        rows = slice(HD * half, HD * half + HD)
        for kind, name in enumerate(("lru_wa_2", "lru_wx_2")):
            gates[:, :, kind, rows, rows] = f[name][:, order[:, half]].transpose(1, 0, 2, 3)
    kinds = {"lru": gates.reshape(4, 8, P, P), "za": tiles_of(za, None, HEADS2), "zb": tiles_of(zb, None, HEADS2)}
    for kind, t in MIX:
        put(kinds[kind][t:t + 1])
    put(tiles_of(f["w_out_2"], HEADS2))
    wi, wo = tiles_of(f["w_ffn_in_2"]), tiles_of(f["w_ffn_out_2"])
    hid, c0 = wi.shape[0] // 2, 0
    for n in FF2_CHUNKS:
        c = slice(c0, c0 + n)
        put(np.stack([wi[:hid][c], wi[hid:][c]], axis=1).reshape(2 * n, DC, P, P))
        put(wo[:, c])
        c0 += n

    def column(a, order=None):
        a = a.reshape(-1, HD)
        if order is not None:
            n = len(order)
            a = np.concatenate([a[i:i + n][np.array(order)] for i in range(0, a.shape[0], n)])
        return a.reshape(-1, P).T

    def across(a):
        return np.broadcast_to(a.reshape(1, -1), (P, a.size))

    cols = {
        "g_mix_pre": column(f["norm_mix_pre"]), "g_mix_post": column(f["norm_mix_post"]),
        "g_mlp_pre": column(f["norm_mlp_pre"]), "g_mlp_post": column(f["norm_mlp_post"]),
        "sinks": across(f["sinks"]), "d_skip": column(f["d_skip"]), "g_mix2": column(f["norm_mix_g_2"]),
        "b_gate": column(f["b_gate_2"], HEADS2), "conv_w": column(f["conv_w_2"], HEADS2),
        "conv_b": column(f["conv_b_2"], HEADS2), "lam": column(f["lru_lambda_2"], HEADS2),
        "ba": column(f["lru_ba_2"], HEADS2), "bx": column(f["lru_bx_2"], HEADS2),
        "sinks2": across(f["attn_sink_2"]), "g_ffn2": column(f["norm_ffn_g_2"]), "g_fin2": column(f["norm_final_g_2"]),
        "iota": across(np.arange(16, dtype=np.float32)), "eps": np.full((P, 1), EPS, np.float32),
        "pad": np.zeros((P, 3), np.float32), "ident": np.eye(P, dtype=np.float32), "ones": np.ones((P, P), np.float32),
    }
    params = np.concatenate([cols[name] for name, _ in _cols], axis=1)
    assert params.shape == (P, NCOL)

    G, N = f["lam_re"].shape
    C = SSM_CH // G

    def by_both(a):
        a = np.broadcast_to(a.reshape(G, -1), (G, N))
        state = a.reshape(PAIRS, P).T
        pair = a.reshape(CT, 4, 1, 2 * N)
        channel = np.broadcast_to(pair, (CT, 4, 2 * C, 2 * N)).reshape(CT, P, P).transpose(1, 0, 2).reshape(P, CT * P)
        return np.concatenate([state, channel], axis=1)

    s5p = np.stack([by_both(f["lam_re"]), by_both(f["lam_im"]), by_both(f["log_dt"])], axis=1)

    def diagonal(a):
        r, c = a.shape[1:]
        d = np.zeros((PAIRS, 2, r, 2, c), a.dtype)
        for g in range(2):
            d[:, g, :, g, :] = a[g::2]
        return d.reshape(PAIRS, 2 * r, 2 * c)

    b = [diagonal(f[n]) for n in ("b_re", "b_im")]
    c = [diagonal(f[n].transpose(0, 2, 1)) for n in ("c_re", "c_im")]
    s5b = np.stack([a.transpose(1, 0, 2) for a in b], axis=1)
    s5c = np.stack([a.transpose(1, 0, 2) for a in c], axis=1)
    s5bt = np.stack([a.transpose(0, 2, 1).reshape(CT, P, P).transpose(1, 0, 2) for a in b], axis=1)

    dist = np.arange(P)[:, None] + P - np.arange(2 * P)[None, :]
    exact = NBUCKET // 2
    df = np.maximum(dist, 1).astype(np.float32)
    large = exact + (np.log(df / np.float32(exact)) / np.float32(np.log(MAXDIST / exact))
                     * np.float32(NBUCKET - exact)).astype(np.int32)
    bucket = np.where(dist < exact, np.maximum(dist, 0), np.minimum(large, NBUCKET - 1))
    inside = (dist >= 0) & (dist < P)
    bias1 = np.full((P, 8, 2 * P), -1e30, np.float32)
    rb = np.asarray(v["rel_bias"])
    for hd in range(8):
        bias1[:, hd][inside] = rb[bucket[inside], hd]
    far = np.abs(np.arange(P)[:, None] + P - np.arange(3 * P)[None, :])
    nd = np.where(far <= P, -far, -1e30).astype(np.float32)

    x = np.asarray(v["x"])[0].T.reshape(DC, P, T).transpose(1, 0, 2)
    return {"slabs": np.concatenate(stream), "params": params, "s5p": s5p, "s5bt": s5bt, "s5b": s5b, "s5c": s5c,
            "bias1": bias1, "nd2": nd, "x_in": x}


def kernel(**inputs):
    import concourse.bacc as bacc
    from concourse.bass_utils import run_bass_kernel_spmd as run

    arrays = {k: np.ascontiguousarray(a) for k, a in lay_out(inputs).items()}
    assert arrays["slabs"].shape[0] == NSLAB, arrays["slabs"].shape
    nc = bacc.Bacc("TRN2", target_bir_lowering=False, num_devices=1)
    args = {k: nc.dram_tensor(k, a.shape, F32, kind="ExternalInput").ap() for k, a in arrays.items()}
    out = nc.dram_tensor("out_t", (P, DC, T), F32, kind="ExternalOutput").ap()
    build(nc, out=out, **args)
    r = run(nc, [arrays], core_ids=[0])
    y = r.results[0]["out_t"]
    return np.ascontiguousarray(y.transpose(2, 1, 0).reshape(1, T, D))
```
